# Optimizing a Trainium2 kernel written in Bass

```python
import jax, jax.numpy as jnp
from jax import lax
import numpy as np

D_MODEL = 1024
BATCH = 1
SEQ = 256
DEPTH = 2
DEC_BATCH = 8
DEC_SEQ = 1
PAST_LEN = 2048
PAGE_SIZE = 128

N_META = 16
NH_M = 4
DH_M = 128
W_M = NH_M * DH_M
MLSTM_CHUNK = 128
C_CONV = 512
CONV_W = 31
H_A = 8
KV_A = 2
DH_A = 64
ROT_DIM = DH_A // 4
ROPE_THETA = 500000.0
WINDOW = 128
ATTN_BLOCK = WINDOW
D_FF = 2816
FFN_CONV_W = 3
IN_SIZES = (W_M, W_M, W_M, NH_M, NH_M, W_M, C_CONV, C_CONV, H_A * DH_A, KV_A * DH_A, KV_A * DH_A, 3 * D_MODEL)
IN_COLS = sum(IN_SIZES)
RMS_EPS = 1e-6
LN_EPS = 1e-5

kernel_name = "hybrid_mlstm_conformer_swa_step"

def rmsnorm(x, g):
    x32 = x.astype(jnp.float32)
    y = x32 * lax.rsqrt(jnp.mean(x32 * x32, axis=-1, keepdims=True) + RMS_EPS)
    return (y * g.astype(jnp.float32)).astype(x.dtype)

def layernorm(x, g, b):
    x32 = x.astype(jnp.float32)
    xc = x32 - jnp.mean(x32, axis=-1, keepdims=True)
    var = jnp.mean(xc * xc, axis=-1, keepdims=True)
    return (xc * lax.rsqrt(var + LN_EPS) * g.astype(jnp.float32) + b.astype(jnp.float32)).astype(x.dtype)

def split_cols(z):
    out, start = [], 0
    for size in IN_SIZES:
        out.append(z[..., start:start + size])
        start += size
    return out

def causal_dwconv(u, buf, w, b):
    width, ch = w.shape
    xp = jnp.concatenate([buf.astype(u.dtype), u], axis=1)
    y = lax.conv_general_dilated(xp, w.astype(u.dtype)[:, None, :], (1,), 'VALID',
                                 dimension_numbers=('NWC', 'WIO', 'NWC'), feature_group_count=ch)
    return y + b.astype(u.dtype), xp[:, xp.shape[1] - (width - 1):]

def rope(x, pos):
    half = ROT_DIM // 2
    inv = jnp.power(ROPE_THETA, -jnp.arange(half, dtype=jnp.float32) / half)
    ang = pos.astype(jnp.float32)[:, None] * inv[None, :]
    cos = jnp.cos(ang)[:, None, :]
    sin = jnp.sin(ang)[:, None, :]
    x1 = x[..., :half].astype(jnp.float32)
    x2 = x[..., half:ROT_DIM].astype(jnp.float32)
    r = jnp.concatenate([x1 * cos - x2 * sin, x2 * cos + x1 * sin], axis=-1).astype(x.dtype)
    return jnp.concatenate([r, x[..., ROT_DIM:]], axis=-1)

def window_mask(qpos, kpos):
    return (kpos >= 0) & (kpos <= qpos) & (qpos - kpos <= WINDOW)

def sink_attention(q, k, v, mask, sinks):
    bsz, nblk, nq, nh, d = q.shape
    g = k.shape[3]
    r = nh // g
    qg = q.reshape(bsz, nblk, nq, g, r, d)
    s = jnp.einsum('bnqgrd,bnkgd->bngrqk', qg, k).astype(jnp.float32) * (d ** -0.5)
    s = jnp.where(mask[None, :, None, None], s, -jnp.inf)
    sk = sinks.astype(jnp.float32).reshape(1, 1, g, r, 1)
    mx = jnp.maximum(s.max(axis=-1), sk)
    p = jnp.exp(s - mx[..., None])
    den = p.sum(axis=-1) + jnp.exp(sk - mx)
    o = jnp.einsum('bngrqk,bnkgd->bnqgrd', (p / den[..., None]).astype(v.dtype), v)
    return o.reshape(bsz, nblk, nq, nh, d)

def swa_prompt(q, k, v, sinks):
    bsz, t, nh, d = q.shape
    g = k.shape[2]
    lead = (-t) % ATTN_BLOCK
    nb = (t + lead) // ATTN_BLOCK
    qp = jnp.pad(q, ((0, 0), (lead, 0), (0, 0), (0, 0))).reshape(bsz, nb, ATTN_BLOCK, nh, d)
    kp = jnp.pad(k, ((0, 0), (lead + ATTN_BLOCK, 0), (0, 0), (0, 0)))
    vp = jnp.pad(v, ((0, 0), (lead + ATTN_BLOCK, 0), (0, 0), (0, 0)))
    def band(a):
        return jnp.concatenate([a[:, :-ATTN_BLOCK].reshape(bsz, nb, ATTN_BLOCK, g, d),
                                a[:, ATTN_BLOCK:].reshape(bsz, nb, ATTN_BLOCK, g, d)], axis=2)
    qpos = (jnp.arange(nb * ATTN_BLOCK) - lead).reshape(nb, ATTN_BLOCK)
    kpos = (jnp.arange(nb)[:, None] * ATTN_BLOCK - ATTN_BLOCK - lead) + jnp.arange(2 * ATTN_BLOCK)[None, :]
    mask = window_mask(qpos[:, :, None], kpos[:, None, :])
    o = sink_attention(qp, band(kp), band(vp), mask, sinks).reshape(bsz, nb * ATTN_BLOCK, nh, d)[:, lead:]
    return o, k[:, t - WINDOW:], v[:, t - WINDOW:]

def swa_sample(q, k, v, k_buf, v_buf, pos, sinks):
    wb = k_buf.shape[1]
    kc = jnp.concatenate([k_buf.astype(k.dtype), k], axis=1)
    vc = jnp.concatenate([v_buf.astype(v.dtype), v], axis=1)
    kpos = PAST_LEN - wb + jnp.arange(kc.shape[1])
    mask = window_mask(pos[:, None], kpos[None, :])[None]
    o = sink_attention(q[:, None], kc[:, None], vc[:, None], mask, sinks)[:, 0]
    return o, kc[:, kc.shape[1] - wb:], vc[:, vc.shape[1] - wb:]

def mlstm_chunk(carry, xs):
    c, n, m = carry
    q, k, v, ig, lf = xs
    q = q.transpose(0, 2, 1, 3)
    k = k.transpose(0, 2, 1, 3)
    v = v.transpose(0, 2, 1, 3)
    ig = ig.transpose(0, 2, 1)
    b = jnp.cumsum(lf.transpose(0, 2, 1), axis=-1)
    ln = q.shape[2]
    causal = jnp.tril(jnp.ones((ln, ln), dtype=bool))
    log_d = jnp.where(causal, b[..., :, None] - b[..., None, :] + ig[..., None, :], -jnp.inf)
    log_prev = b + m[..., None]
    m_t = jnp.maximum(log_prev, log_d.max(axis=-1))
    dmat = jnp.exp(log_d - m_t[..., None])
    w_prev = jnp.exp(log_prev - m_t)
    s = jnp.einsum('bhtd,bhsd->bhts', q, k) * dmat
    num = jnp.einsum('bhts,bhsv->bhtv', s, v) + w_prev[..., None] * jnp.einsum('bhtk,bhkv->bhtv', q, c)
    dot = s.sum(axis=-1) + w_prev * jnp.einsum('bhtk,bhk->bht', q, n)
    h = num / jnp.maximum(jnp.abs(dot), jnp.exp(-m_t))[..., None]
    b_last = b[..., -1]
    log_w = b_last[..., None] - b + ig
    m_new = jnp.maximum(b_last + m, log_w.max(axis=-1))
    wts = jnp.exp(log_w - m_new[..., None])
    decay = jnp.exp(b_last + m - m_new)
    c_new = decay[..., None, None] * c + jnp.einsum('bhs,bhsk,bhsv->bhkv', wts, k, v)
    n_new = decay[..., None] * n + jnp.einsum('bhs,bhsk->bhk', wts, k)
    return (c_new, n_new, m_new), h.transpose(0, 2, 1, 3)

def mlstm_prompt(carry, q, k, v, ig, lf):
    bsz = q.shape[0]
    carry, h0 = mlstm_chunk(carry, (q[:, :N_META], k[:, :N_META], v[:, :N_META], ig[:, :N_META], lf[:, :N_META]))
    def to_chunks(a):
        r = a[:, N_META:]
        nc = r.shape[1] // MLSTM_CHUNK
        return jnp.moveaxis(r.reshape((bsz, nc, MLSTM_CHUNK) + r.shape[2:]), 1, 0)
    carry, hs = lax.scan(mlstm_chunk, carry, (to_chunks(q), to_chunks(k), to_chunks(v), to_chunks(ig), to_chunks(lf)))
    hs = jnp.moveaxis(hs, 0, 1).reshape(bsz, -1, NH_M, DH_M)
    return jnp.concatenate([h0, hs], axis=1), carry

def layer(x, pos, st, w, prompt):
    c0, n0, m0, conv_buf, k_buf, v_buf, ffn_buf = st
    bsz, ln, _ = x.shape
    f32 = jnp.float32
    h = rmsnorm(x, w['norm1_g'])
    (q_m, k_m, v_m, i_pre, f_pre, o_pre, glu_a, glu_b, q_a, k_a, v_a, g_pre) = split_cols(h @ w['w_in'])
    qm = q_m.reshape(bsz, ln, NH_M, DH_M).astype(f32)
    km = k_m.reshape(bsz, ln, NH_M, DH_M).astype(f32) * (DH_M ** -0.5)
    vm = v_m.reshape(bsz, ln, NH_M, DH_M).astype(f32)
    ig = (i_pre + w['b_igate']).astype(f32)
    lf = jax.nn.log_sigmoid((f_pre + w['b_fgate']).astype(f32))
    carry0 = (c0.astype(f32), n0.astype(f32), m0.astype(f32))
    if prompt:
        hm, (c1, n1, m1) = mlstm_prompt(carry0, qm, km, vm, ig, lf)
    else:
        (c1, n1, m1), hm = mlstm_chunk(carry0, (qm, km, vm, ig, lf))
    y_a = (jax.nn.sigmoid(o_pre) * hm.reshape(bsz, ln, W_M).astype(x.dtype)) @ w['w_mlstm_out']
    u = glu_a * jax.nn.sigmoid(glu_b)
    uc, conv_new = causal_dwconv(u, conv_buf, w['w_dconv'], w['b_dconv'])
    y_b = jax.nn.silu(layernorm(uc, w['ln_conv_g'], w['ln_conv_b'])) @ w['w_conv_out']
    qa = rope(q_a.reshape(bsz, ln, H_A, DH_A), pos)
    ka = rope(k_a.reshape(bsz, ln, KV_A, DH_A), pos)
    va = v_a.reshape(bsz, ln, KV_A, DH_A)
    if prompt:
        oa, k_new, v_new = swa_prompt(qa, ka, va, w['attn_sinks'])
    else:
        oa, k_new, v_new = swa_sample(qa, ka, va, k_buf, v_buf, pos, w['attn_sinks'])
    y_c = oa.reshape(bsz, ln, H_A * DH_A) @ w['w_attn_out']
    gates = jax.nn.sigmoid(g_pre + w['b_merge'])
    g_a, g_b, g_c = gates[..., :D_MODEL], gates[..., D_MODEL:2 * D_MODEL], gates[..., 2 * D_MODEL:]
    x = x + (g_a * y_a + g_b * y_b + g_c * y_c) @ w['w_out']
    h2 = rmsnorm(x, w['norm2_g'])
    gp = h2 @ w['w_ffn_gate']
    up = h2 @ w['w_ffn_up']
    gc, ffn_new = causal_dwconv(gp, ffn_buf, w['w_ffn_conv'], w['b_ffn_conv'])
    x = x + (jax.nn.silu(gc) * up) @ w['w_ffn_down']
    return x, (c1, n1, m1, conv_new, k_new, v_new, ffn_new)

def setup_inputs(seed: int = 0) -> dict:
    key = jax.random.key(seed)
    ks = list(jax.random.split(key, 40))
    def nrm(shape, scale):
        return scale * jax.random.normal(ks.pop(), shape, jnp.float32)
    wb = min(WINDOW, PAST_LEN)
    d = {}
    d['x_prompt'] = nrm((BATCH, SEQ, D_MODEL), 1.0)
    d['x_sample'] = nrm((DEC_BATCH, DEC_SEQ, D_MODEL), 1.0)
    d['state_mlstm_c'] = nrm((DEPTH, DEC_BATCH, NH_M, DH_M, DH_M), 0.05)
    d['state_mlstm_n'] = nrm((DEPTH, DEC_BATCH, NH_M, DH_M), 0.1)
    d['state_mlstm_m'] = nrm((DEPTH, DEC_BATCH, NH_M), 1.0)
    d['state_conv'] = nrm((DEPTH, DEC_BATCH, CONV_W - 1, C_CONV), 0.5)
    d['cache_swa_k'] = nrm((DEPTH, DEC_BATCH, wb, KV_A, DH_A), 1.0)
    d['cache_swa_v'] = nrm((DEPTH, DEC_BATCH, wb, KV_A, DH_A), 1.0)
    d['state_ffn_conv'] = nrm((DEPTH, DEC_BATCH, FFN_CONV_W - 1, D_FF), 1.0)
    d['meta_tokens'] = nrm((N_META, D_MODEL), 1.0)
    d['norm1_g'] = 1.0 + nrm((DEPTH, D_MODEL), 0.02)
    d['w_in'] = nrm((DEPTH, D_MODEL, IN_COLS), D_MODEL ** -0.5)
    d['b_igate'] = nrm((DEPTH, NH_M), 0.1)
    d['b_fgate'] = 3.0 + nrm((DEPTH, NH_M), 0.5)
    d['w_mlstm_out'] = nrm((DEPTH, W_M, D_MODEL), W_M ** -0.5)
    d['w_dconv'] = nrm((DEPTH, CONV_W, C_CONV), CONV_W ** -0.5)
    d['b_dconv'] = nrm((DEPTH, C_CONV), 0.02)
    d['ln_conv_g'] = 1.0 + nrm((DEPTH, C_CONV), 0.02)
    d['ln_conv_b'] = nrm((DEPTH, C_CONV), 0.02)
    d['w_conv_out'] = nrm((DEPTH, C_CONV, D_MODEL), C_CONV ** -0.5)
    d['attn_sinks'] = nrm((DEPTH, H_A), 0.5)
    d['w_attn_out'] = nrm((DEPTH, H_A * DH_A, D_MODEL), (H_A * DH_A) ** -0.5)
    d['b_merge'] = nrm((DEPTH, 3 * D_MODEL), 0.02)
    d['w_out'] = nrm((DEPTH, D_MODEL, D_MODEL), D_MODEL ** -0.5)
    d['norm2_g'] = 1.0 + nrm((DEPTH, D_MODEL), 0.02)
    d['w_ffn_gate'] = nrm((DEPTH, D_MODEL, D_FF), D_MODEL ** -0.5)
    d['w_ffn_up'] = nrm((DEPTH, D_MODEL, D_FF), D_MODEL ** -0.5)
    d['w_ffn_conv'] = nrm((DEPTH, FFN_CONV_W, D_FF), FFN_CONV_W ** -0.5)
    d['b_ffn_conv'] = nrm((DEPTH, D_FF), 0.02)
    d['w_ffn_down'] = nrm((DEPTH, D_FF, D_MODEL), D_FF ** -0.5)
    d['final_norm_g'] = 1.0 + nrm((D_MODEL,), 0.02)
    return d

def reference(x_prompt, x_sample, state_mlstm_c, state_mlstm_n, state_mlstm_m, state_conv, cache_swa_k, cache_swa_v,
              state_ffn_conv, meta_tokens, norm1_g, w_in, b_igate, b_fgate, w_mlstm_out, w_dconv, b_dconv, ln_conv_g,
              ln_conv_b, w_conv_out, attn_sinks, w_attn_out, b_merge, w_out, norm2_g, w_ffn_gate, w_ffn_up, w_ffn_conv,
              b_ffn_conv, w_ffn_down, final_norm_g):
    bsz = x_prompt.shape[0]
    f32 = jnp.float32
    meta = jnp.broadcast_to(meta_tokens.astype(x_prompt.dtype)[None], (bsz, N_META, D_MODEL))
    xp = jnp.concatenate([meta, x_prompt], axis=1)
    pos_p = jnp.arange(xp.shape[1])
    xs = x_sample
    pos_s = PAST_LEN + jnp.arange(xs.shape[1])
    p_states = [[] for _ in range(7)]
    s_states = [[] for _ in range(7)]
    for l in range(DEPTH):
        w = dict(norm1_g=norm1_g[l], w_in=w_in[l], b_igate=b_igate[l], b_fgate=b_fgate[l], w_mlstm_out=w_mlstm_out[l],
                 w_dconv=w_dconv[l], b_dconv=b_dconv[l], ln_conv_g=ln_conv_g[l], ln_conv_b=ln_conv_b[l],
                 w_conv_out=w_conv_out[l], attn_sinks=attn_sinks[l], w_attn_out=w_attn_out[l], b_merge=b_merge[l],
                 w_out=w_out[l], norm2_g=norm2_g[l], w_ffn_gate=w_ffn_gate[l], w_ffn_up=w_ffn_up[l],
                 w_ffn_conv=w_ffn_conv[l], b_ffn_conv=b_ffn_conv[l], w_ffn_down=w_ffn_down[l])
        p_init = (jnp.zeros((bsz, NH_M, DH_M, DH_M), f32), jnp.zeros((bsz, NH_M, DH_M), f32),
                  jnp.zeros((bsz, NH_M), f32), jnp.zeros((bsz, CONV_W - 1, C_CONV), xp.dtype), None, None,
                  jnp.zeros((bsz, FFN_CONV_W - 1, D_FF), xp.dtype))
        xp, pst = layer(xp, pos_p, p_init, w, True)
        s_init = (state_mlstm_c[l], state_mlstm_n[l], state_mlstm_m[l], state_conv[l], cache_swa_k[l], cache_swa_v[l],
                  state_ffn_conv[l])
        xs, sst = layer(xs, pos_s, s_init, w, False)
        for i in range(7):
            p_states[i].append(pst[i])
            s_states[i].append(sst[i])
    y_prompt = rmsnorm(xp[:, N_META:], final_norm_g)
    y_sample = rmsnorm(xs, final_norm_g)
    p_c, p_n, p_m, p_conv, p_k, p_v, p_ffn = [jnp.stack(a, axis=0) for a in p_states]
    s_c, s_n, s_m, s_conv, s_k, s_v, s_ffn = [jnp.stack(a, axis=0) for a in s_states]
    return (y_prompt, y_sample, p_c, p_n, p_m, p_conv, p_k, p_v, p_ffn, s_c, s_n, s_m, s_conv, s_k, s_v, s_ffn)


_drawn_inputs = setup_inputs


def setup_inputs(seed=0):
    import zlib

    import numpy as np

    out = dict(_drawn_inputs(seed))
    spreads = {}
    factors = {'attn_sinks': 5.553, 'b_merge': 3.838, 'final_norm_g': 2.797}
    for name, (base, spread) in spreads.items():
        noise = np.random.default_rng([zlib.crc32(name.encode()), seed]).standard_normal(out[name].shape)
        drawn = base * np.exp(spread * noise) if base else spread * noise
        out[name] = __import__('jax').numpy.asarray(drawn.astype(out[name].dtype))
    for name, factor in factors.items():
        out[name] = (out[name] * factor).astype(out[name].dtype)
    return out
```

```python
from contextlib import ExitStack

import numpy as np

import concourse.bass as bass
from concourse import mybir

F32 = mybir.dt.float32
F32R = mybir.dt.float32r
ALU = mybir.AluOpType
ACT = mybir.ActivationFunctionType
AX = mybir.AxisListType

P = 128
D_MODEL = 1024
SEQ = 256
DEPTH = 2
NS = 8
PAST_LEN = 2048
N_META = 16
NH_M = 4
DH_M = 128
W_M = NH_M * DH_M
C_CONV = 512
CONV_W = 31
HIST = CONV_W - 1
H_A = 8
KV_A = 2
R_A = H_A // KV_A
DH_A = 64
ROT_DIM = DH_A // 4
ROPE_THETA = 500000.0
WINDOW = 128
D_FF = 2816
FFN_CONV_W = 3
RMS_EPS = 1e-6
LN_EPS = 1e-5
NP = N_META + SEQ
T = NP + NS
KD = D_MODEL // P
KC = C_CONV // P
KF = D_FF // P
BLOCKS = [(0, 128), (128, 128), (256, 16)]
MASKED = 1e30

Q_M, K_M, V_M = 0, W_M, 2 * W_M
IF_G = 3 * W_M
O_G = IF_G + 2 * NH_M
GLU_A = O_G + W_M
GLU_B = GLU_A + C_CONV
Q_A = GLU_B + C_CONV
K_A = Q_A + H_A * DH_A
G_PRE = K_A + 2 * KV_A * DH_A

CONST_WIDTHS = [("ident", P), ("ones", NP), ("rot", P), ("cos", T), ("sin", T), ("amask", 2 * P),
                ("pmask", NP), ("sel", NH_M * P), ("sel32", P), ("sel_f", 64),
                ("half", P), ("eye32", R_A * NS)]
CONST_AT = {}
_at = 0
for _name, _w in CONST_WIDTHS:
    CONST_AT[_name] = (_at, _at + _w)
    _at += _w
CONST_COLS = _at

VEC_ROWS = [[("norm1", 8), ("norm2", 8), ("b_merge", 24), ("b_dconv", 4), ("ln_g", 4), ("ln_b", 4),
             ("state_n", 32), ("final", 8)],
            [("b_ffn", 22), ("w_ffn", 66)],
            [("w_dconv", 124)]]
VEC_AT = {}
_at = 0
for _block in VEC_ROWS:
    for _name, _w in _block:
        VEC_AT[_name] = (_at, _at + _w)
        _at += _w
VEC_COLS = _at
VEC_DMAS = sum(len(b) for b in VEC_ROWS)


def constants():
    c = np.zeros((P, CONST_COLS), np.float32)

    def part(name):
        a, b = CONST_AT[name]
        return c[:, a:b]

    part("ident")[:] = np.eye(P)
    part("ones")[:] = 1.0
    half = ROT_DIM // 2
    pos = np.concatenate([np.arange(NP), np.full(NS, PAST_LEN)]).astype(np.float32)
    inv = np.power(np.float32(ROPE_THETA), -np.arange(half, dtype=np.float32) / half).astype(np.float32)
    ang = (pos[None, :] * inv[:, None]).astype(np.float32).astype(np.float64)
    part("cos")[:] = 1.0
    for head in range(2):
        base = head * DH_A
        part("cos")[base:base + half] = np.cos(ang)
        part("cos")[base + half:base + ROT_DIM] = np.cos(ang)
        part("sin")[base:base + half] = -np.sin(ang)
        part("sin")[base + half:base + ROT_DIM] = np.sin(ang)
        for i in range(half):
            part("rot")[base + i, base + half + i] = 1.0
            part("rot")[base + half + i, base + i] = 1.0
    q = np.arange(P)[:, None]
    k = np.arange(P)[None, :]
    part("amask")[:, :P] = np.where(k >= q, 0.0, -MASKED)
    part("amask")[:, P:] = np.where(k <= q, 0.0, -MASKED)
    part("pmask")[:, :P] = np.where(q <= k, 0.0, MASKED)
    for h in range(NH_M):
        part("sel")[h, h * P:(h + 1) * P] = 1.0
        part("sel32")[h, 32 * h:32 * h + 32] = 1.0
        part("sel_f")[NH_M + h, h] = 1.0
    for r in range(2 * R_A * NS):
        g, jb = divmod(r, R_A * NS)
        part("half")[r, g * DH_A:(g + 1) * DH_A] = 1.0
        part("eye32")[r, jb] = 1.0
    return c


def weight_pieces():
    out = []

    def add(kind, i, nk, ncol, tiles):
        out.append((kind, i, nk, ncol, tiles))

    for kind in ("glub", "glua"):
        for i in range(2):
            add(kind, i, KD, 256, [(kind, 2 * i), (kind, 2 * i + 1)])
    add("kva", 0, KD, 256, [("ka", 0), ("va", 0)])
    for i in range(2):
        add("qa", i, KD, 256, [("qa", 2 * i), ("qa", 2 * i + 1)])
    add("if", 0, KD, 8, [("if", 0)])
    for kind in ("km", "vm", "qm", "o"):
        for i in range(2):
            add(kind, i, KD, 256, [(kind, 2 * i), (kind, 2 * i + 1)])
    for i in range(12):
        add("g", i, KD, 256, [("g", 2 * i), ("g", 2 * i + 1)])
    for kind in ("yb", "yc", "ya"):
        for i in range(2):
            add(kind, i, KC, 512, [(kind, 4 * i + j) for j in range(4)])
    for i in range(4):
        add("out", i, KD, 256, [("out", 2 * i), ("out", 2 * i + 1)])
    for i in range(11):
        add("gate", i, KD, 256, [("gate", 2 * i), ("gate", 2 * i + 1)])
        add("up", i, KD, 256, [("up", 2 * i), ("up", 2 * i + 1)])
    for i in range(4):
        for s, nk in enumerate((8, 8, 6)):
            add("down", 3 * i + s, nk, 256, [("down", 2 * i), ("down", 2 * i + 1)])
    return out


PIECES = weight_pieces()
N_PIECES = len(PIECES)
RAW_SLOTS = 2
SPLIT_SLOTS = 2
W_COLS = {"glub": GLU_B, "glua": GLU_A, "kva": K_A, "if": IF_G, "km": K_M, "vm": V_M, "qm": Q_M,
          "o": O_G, "g": G_PRE}
COLS = {"if": 8}
STEP = {(kind, i): n for n, (kind, i, _, _, _) in enumerate(PIECES)}
RUNS = [(n, kind, t) for n, p in enumerate(PIECES) for kind, t in p[4]]
N_RUNS = len(RUNS)
RUNS_THROUGH = [sum(1 for r in RUNS if r[0] <= n) for n in range(N_PIECES)]
LAST_RUN = {(kind, t): r for r, (n, kind, t) in enumerate(RUNS)}
TILES = sorted(LAST_RUN, key=lambda k: LAST_RUN[k])
TILE_NO = {k: i for i, k in enumerate(TILES)}
ON_ACT = ("glub", "ka", "va", "qa", "km", "vm", "qm", "o", "g")
ACT_NO, DVE_NO = {}, {}
for _k in TILES:
    _d = ACT_NO if _k[0] in ON_ACT else DVE_NO
    _d[_k] = len(_d)
DMAS = [2 if k[0] in ("qa", "yc") or k[:2] == ("qm", 0) else 1 for k in PIECES]
RAW_THROUGH = []
_slot = [0] * RAW_SLOTS
for _n in range(N_PIECES):
    _slot[_n % RAW_SLOTS] += 16 * DMAS[_n]
    RAW_THROUGH.append(_slot[_n % RAW_SLOTS])
RAW_TOTAL = list(_slot)
UNITS = [(blk, g) for blk in range(3) for g in range(2)]
CONV_FROM, CONV_STEPS, TAPS_A_STEP = 4, 16, 8
POOL_K = 4


def dve_share(nk, ncol):
    if ncol == 8:
        return nk
    return nk - (POOL_K * nk) // 8


SPLIT_THROUGH = []
for _n, _p in enumerate(PIECES):
    _old = SPLIT_THROUGH[_n - SPLIT_SLOTS] if _n >= SPLIT_SLOTS else 0
    SPLIT_THROUGH.append(_old + 1 + (dve_share(_p[2], _p[3]) < _p[2]))
SPLIT_TOTAL = [SPLIT_THROUGH[N_PIECES - SPLIT_SLOTS + (i - N_PIECES) % SPLIT_SLOTS] for i in range(SPLIT_SLOTS)]
assert RAW_SLOTS == SPLIT_SLOTS and N_PIECES % SPLIT_SLOTS == 0
MASKS_THROUGH = [1, 2, 4, 6, 8, 10]
PT_THROUGH = [1, 2, 4, 6, 8, 10]
STORES = 2 + 1 + 2 + 1 + NS
Y_BLOCKS = [(N_META, P), (N_META + P, P), (NP, NS)]


def program(nc, ins, outs):
    (x_prompt, x_sample, state_c, state_n, state_m, state_conv, cache_k, cache_v, state_ffn, meta, norm1_g, w_in,
     b_igate, b_fgate, w_mlstm_out, w_dconv, b_dconv, ln_g, ln_b, w_conv_out, attn_sinks, w_attn_out, b_merge,
     w_out, norm2_g, w_ffn_gate, w_ffn_up, w_ffn_conv, b_ffn_conv, w_ffn_down, final_g, consts) = ins
    (y_prompt, y_sample, p_c, p_n, p_m, p_conv, p_k, p_v, p_ffn, s_c, s_n, s_m, s_conv, s_k, s_v, s_ffn) = outs

    with ExitStack() as ctx:
        def sb(name, shape, dt=F32):
            return ctx.enter_context(nc.sbuf_tensor(name, shape, dt))

        raw = [sb(f"raw{i}", [P, 2048]) for i in range(RAW_SLOTS)]
        w_hi = [sb(f"w_hi{i}", [P, 2048], F32R) for i in range(SPLIT_SLOTS)]
        w_lo = [sb(f"w_lo{i}", [P, 2048], F32R) for i in range(SPLIT_SLOTS)]
        x = sb("x", [P, KD, T])
        h_hi = sb("h_hi", [P, KD, T], F32R)
        h_lo = sb("h_lo", [P, KD, T], F32R)
        const = sb("const", [P, CONST_COLS])
        vec_raw = sb("vec_raw", [P, 3, P])
        vec = sb("vec", [P, VEC_COLS])
        ffn_raw = sb("ffn_raw", [P, 3, P])
        ffn_hist = sb("ffn_hist", [P, NS * 2 * KF])
        small = sb("small", [P, 128])

        zone = {}
        arena_at = (nc.sbuf_base + 31) // 32 * 32
        arena_floats = 30100
        sb("arena", [P, arena_floats])

        def at(name, shape, offset_floats, dt=F32):
            size = int(np.prod(shape[1:]))
            assert offset_floats + size <= arena_floats, (name, offset_floats, size)
            zone[name] = (offset_floats, offset_floats + size)
            return nc.alloc_sbuf_tensor_at(name, shape, dt, offset=arena_at + 4 * offset_floats)

        TK = KC * T
        gates = at("gates", [P, 24, T], 0)
        squares = at("squares", [P, KD, T], 0)
        h_full = at("h_full", [P, KD, T], KD * T)
        rms = at("rms", [P, T], 16 * T)
        rms_inv = at("rms_inv", [P, T], 17 * T)
        x_rows = at("x_rows", [P, 3, D_MODEL], 0)
        o = 24 * T
        conv_hi = at("conv_hi", [P, KC, T], o, F32R)
        conv_lo = at("conv_lo", [P, KC, T], o + TK, F32R)
        sig_b = at("sig_b", [P, KC, T], o)
        conv_sq = at("conv_sq", [P, KC, T], o + TK)
        o += 2 * TK
        merged = at("merged", [P, KD, T], o)
        u_pad = at("u_pad", [P, KC, HIST + NP], o)
        u_new = at("u_new", [P, KC, NS], o + KC * (HIST + NP))
        u_hist = at("u_hist", [P, NS, HIST, KC], o + KC * (HIST + NP + NS))
        assert KC * (HIST + NP + NS) + 960 <= KD * T
        o += KD * T
        uc = at("uc", [P, KC, T], o)
        o += TK
        ffn_end = o
        act_hi = at("act_hi", [P, KF, T], 0, F32R)
        act_lo = at("act_lo", [P, KF, T], KF * T, F32R)
        assert 2 * KF * T <= ffn_end, (2 * KF * T, ffn_end)
        zb = ffn_end
        o = zb
        qa_t = at("qa_t", [P, R_A, T], o); o += TK
        ka_t = at("ka_t", [P, T], o); o += T
        va_t = at("va_t", [P, T], o); o += T
        cache_k_rows = at("cache_k_rows", [P, NS, P], o)
        att_hi = at("att_hi", [P, R_A, T], o, F32R); o += TK
        cache_v_rows = at("cache_v_rows", [P, NS, P], o); o += NS * P
        key_t = at("key_t", [P, NS, P], o)
        att_lo = at("att_lo", [P, R_A, T], o, F32R); o += TK
        va_rows = at("va_rows", [P, 3, P], o); o += 3 * P
        scores = at("scores", [P, 2, 1024], o); o += 2048
        probs_t = at("probs_t", [P, 2, 1024], o); o += 2048
        zb_end = o
        o = zb
        dk_rows = at("dk_rows", [NS, W_M], o); o += W_M
        v_rows_s = at("v_rows_s", [NS, W_M], o); o += W_M
        assert o <= zone["cache_k_rows"][0]
        prod = at("prod", [P, 2, T], zb)
        vd = at("vd", [NS, NS, P], zone["cache_v_rows"][0])
        conv_rows = at("conv_rows", [HIST, C_CONV], zone["scores"][0])
        conv_rows_s = at("conv_rows_s", [NS, C_CONV], zone["scores"][0] + C_CONV)
        kv_rows = at("kv_rows", [P, 4 * P], zone["probs_t"][0])
        o = zone["va_rows"][0]
        c_head = [at(f"c_head{i}", [P, NS, P], o + i * NS * P) for i in range(2)]
        o += 2 * NS * P
        decay_d = at("decay_d", [P, 432], o); o += 432
        km_rows = at("km_rows", [P, 3, W_M], o); o += 3 * W_M
        assert o <= zb_end
        zc = zb_end
        o = zc
        km_t = at("km_t", [P, NH_M, T], o)
        conv_raw = at("conv_raw", [120, NS, P], o); o += TK
        qm_t = at("qm_t", [P, NH_M, T], o); o += TK
        vm_t = at("vm_t", [P, NH_M, T], o)
        num_all = at("num_all", [P, NH_M, T], o); o += TK
        o_sig = at("o_sig", [P, NH_M, T], o); o += TK
        ml_hi = at("ml_hi", [P, NH_M, T], o, F32R)
        if_rows = at("if_rows", [8, T], o)
        m_row = at("m_row", [4, T], o + T)
        cdw_row = at("cdw_row", [4, NP + 2 * NS], o + 2 * T); o += TK
        ml_lo = at("ml_lo", [P, NH_M, T], o, F32R)
        lf_row = at("lf_row", [4, T], o)
        b_row = at("b_row", [4, NP], o + T)
        a_row = at("a_row", [4, NP], o + T + NP)
        wt_row = at("wt_row", [4, NP], o + T + 2 * NP); o += TK
        vm_rows = at("vm_rows", [P, 3, W_M], o); o += 3 * W_M
        y_rows = at("y_rows", [P, 3, D_MODEL], 18 * T)
        o = zb + 2 * W_M
        dk_t = at("dk_t", [P, NH_M, NS], o); o += NH_M * NS
        qn_t = at("qn_t", [P, NH_M, NS], o); o += NH_M * NS
        dw_b = at("dw_b", [P, NH_M, 2 * NS], o); o += 2 * NH_M * NS
        c_prompt = at("c_prompt", [P, NH_M, P], o); o += W_M
        assert o <= zone["cache_k_rows"][0]
        n_rows = at("n_rows", [36, P], zone["km_rows"][0])
        o = zone["o_sig"][0]
        s_keys = at("s_keys", [P, 2 * R_A * NS], o); o += 64
        s_rows = at("s_rows", [64, WINDOW + 8], o); o += WINDOW + 8
        p_keys = at("p_keys", [P, 64], o); o += 64
        p_self = at("p_self", [64, 32], o); o += 32
        qk_self = at("qk_self", [P, R_A, NS], o); o += 32
        att_s = at("att_s", [P, R_A, NS], o); o += 32
        gate_buf = at("gate_buf", [P, 4, T], zone["o_sig"][0])
        last_gates = at("last_gates", [P, 10, KF], zone["ml_hi"][0])
        gate_rows = at("gate_rows", [110, 2, P], zone["ml_hi"][0] + 224)
        nothing = small[:, 120:121]
        sink_b, sink_s, bias_if = small[:, 0:8], small[0:64, 8:9], small[0:8, 9:10]
        m_old, cm_last = small[0:4, 10:18], small[0:4, 18:19]
        n_all = small[:, 20:56]
        a_wt = small[:, 56:80].rearrange("p (b c) -> p b c", b=3)
        unit_small = [small[:, 80 + 16 * i:96 + 16 * i] for i in range(2)]
        samp_small = small[0:64, 112:120]

        ps_tile = [ctx.enter_context(nc.psum_tensor(f"ps_tile{i}", [P, 512], F32)) for i in range(3)]
        work = [ctx.enter_context(nc.psum_tensor(f"work{i}", [P, 512], F32)) for i in range(5)]

        def con(name, rows=P):
            a, b = CONST_AT[name]
            return const[0:rows, a:b]

        def vcol(name, i=0, n=1):
            a = VEC_AT[name][0] + i
            return vec[:, a:a + n]

        counts = {}

        def sem(name, per_layer, before=0):
            s = ctx.enter_context(nc.semaphore(name))
            counts[name] = (per_layer, before)
            return s

        def value(name, l, k):
            per_layer, before = counts[name]
            return l * per_layer + before + k

        const_in = sem("const_in", 0, 16)
        x_in = sem("x_in", 0, 16 * 5)
        raw_in = [sem(f"raw_in{i}", RAW_TOTAL[i]) for i in range(RAW_SLOTS)]
        vec_in = sem("vec_in", 16 * VEC_DMAS)
        ffn_in = sem("ffn_in", 32)
        conv_in = sem("conv_in", 16)
        keys_in = sem("keys_in", 16)
        values_in = sem("values_in", 16)
        tiny_in = sem("tiny_in", 16 * 5)
        c_in = [sem(f"c_in{i}", 32) for i in range(2)]
        shifted = sem("shifted", 0, 64)
        conv_stored = sem("conv_stored", 32)
        kv_stored = sem("kv_stored", 64)
        stored = sem("stored", 16 * STORES)
        y_stored = sem("y_stored", 0, 32)
        c_stored = [sem(f"c_stored{i}", 32) for i in range(2)]
        runs_done = sem("runs_done", N_RUNS, 1)
        vec_turned = sem("vec_turned", 2, 2)
        x_turned = sem("x_turned", 0, KD)
        squares_summed = sem("squares_summed", 2)
        conv_turned = sem("conv_turned", 3)
        keys_turned = sem("keys_turned", 2)
        rotated = sem("rotated", 5)
        f_moved = sem("f_moved", 1)
        kv_turned = sem("kv_turned", 2)
        s_scored = sem("s_scored", 1)
        s_turned = sem("s_turned", 2)
        s_pv_done = sem("s_pv_done", 1)
        scored = sem("scored", 6)
        probs_turned = sem("probs_turned", 6)
        pv_done = sem("pv_done", 6)
        ln_summed = sem("ln_summed", 2)
        ml_turned = sem("ml_turned", 3)
        dw_spread = sem("dw_spread", 1)
        sk_turned = sem("sk_turned", 1)
        outer_done = sem("outer_done", 8)
        nums_done = sem("nums_done", 4)
        ml_scored = sem("ml_scored", 4)
        num_done = sem("num_done", 4)
        dots_done = sem("dots_done", 4)
        m_spread = sem("m_spread", 1)
        n_turned = sem("n_turned", 1)
        inv_spread = sem("inv_spread", 4)
        gates_turned = sem("gates_turned", 1)
        y_turned = sem("y_turned", 0, 6)
        took_act = sem("took_act", len(ACT_NO))
        w_hi_ready = sem("w_hi_ready", N_PIECES)
        sq_act = sem("sq_act", 2)
        rms_ready = sem("rms_ready", 2)
        h_hi_ready = sem("h_hi_ready", 2 * KD)
        vec_ready = sem("vec_ready", 2)
        hist_ready = sem("hist_ready", 3)
        keys_ready = sem("keys_ready", 2)
        kv_ready = sem("kv_ready", 2)
        log_step = sem("log_step", 3)
        dw_ready = sem("dw_ready", 2)
        s_keys_ready = sem("s_keys_ready", 1)
        s_exp = sem("s_exp", 2)
        s_p_ready = sem("s_p_ready", 1)
        unit_exp = sem("unit_exp", 30)
        pt_ready = sem("pt_ready", PT_THROUGH[-1])
        att_hi_ready = sem("att_hi_ready", 4)
        ln_sq = sem("ln_sq", 1)
        ln_std = sem("ln_std", 1)
        conv_silu = sem("conv_silu", 4)
        conv_hi_ready = sem("conv_hi_ready", 4)
        ml_rows_ready = sem("ml_rows_ready", 3)
        sk_rows_ready = sem("sk_rows_ready", 2)
        decay_ready = sem("decay_ready", 8)
        num_ready = sem("num_ready", 5)
        c_prompt_ready = sem("c_prompt_ready", 4)
        inv_m = sem("inv_m", 2)
        n_kept = sem("n_kept", 4)
        n_ready = sem("n_ready", 1)
        ml_hi_ready = sem("ml_hi_ready", 4)
        merged_hi_ready = sem("merged_hi_ready", 8)
        gate_first = sem("gate_first", KF)
        last_gate_kept = sem("last_gate_kept", KF)
        gate_silu = sem("gate_silu", KF)
        act_hi_ready = sem("act_hi_ready", KF)
        gate_rows_ready = sem("gate_rows_ready", 1)
        y_rows_half = sem("y_rows_half", 0, 6)
        took_dve = sem("took_dve", len(DVE_NO), KD)
        sq_dve = sem("sq_dve", 2)
        rms_inv_ready = sem("rms_inv_ready", 2)
        h_ready = sem("h_ready", 2 * KD)
        h_lo_ready = sem("h_lo_ready", 2 * KD)
        pad_zero = sem("pad_zero", 1)
        tap_done = sem("tap_done", KC * CONV_W)
        hist_sum = sem("hist_sum", 5)
        rope_sin = sem("rope_sin", 5)
        rope_cos = sem("rope_cos", 5)
        roped = sem("roped", 5)
        row_step = sem("row_step", 10)
        qk_ready = sem("qk_ready", 1)
        s_max = sem("s_max", 9)
        s_self = sem("s_self", 1)
        s_out = sem("s_out", 2)
        s_lo = sem("s_lo", 1)
        masked = sem("masked", MASKS_THROUGH[-1])
        unit_max = sem("unit_max", 24)
        unit_p = sem("unit_p", 18)
        att_lo_ready = sem("att_lo_ready", 3)
        centred = sem("centred", 4)
        ln_inv = sem("ln_inv", 5)
        conv_lo_ready = sem("conv_lo_ready", 4)
        a_wt_ready = sem("a_wt_ready", 2)
        km_rows_ready = sem("km_rows_ready", 3)
        dk_ready = sem("dk_ready", 5)
        c_new = sem("c_new", 8)
        decay_arg = sem("decay_arg", 12)
        ml_p_ready = sem("ml_p_ready", 8)
        dots_inv = sem("dots_inv", 2)
        hm_ready = sem("hm_ready", 4)
        ml_lo_ready = sem("ml_lo_ready", 4)
        merged_ready = sem("merged_ready", 16)
        merged_lo_ready = sem("merged_lo_ready", 8)
        gate_conv = sem("gate_conv", 3 * KF)
        act_lo_ready = sem("act_lo_ready", KF)
        w_split = [sem(f"w_split{i}", SPLIT_TOTAL[i], 1) for i in range(SPLIT_SLOTS)]
        c_scaled = sem("c_scaled", 4)
        vd_ready = sem("vd_ready", 4)
        num_gated = sem("num_gated", 4)

        block = ctx.enter_context(nc.Block())
        ident, ones = con("ident"), con("ones")
        LAST = {"store": 0}

        def units_of(u):
            blk, g = UNITS[u]
            q0, nq = BLOCKS[blk]
            k0 = max(0, q0 - WINDOW)
            nk = q0 + nq - k0
            return blk, g, q0, nq, k0, nk, (4 if nk == P else 2)

        def key_chunks(nk):
            return [(0, P)] + ([(P, nk - P)] if nk > P else [])

        SOURCES = [(0, 128, 0, 272, 0), (1, 128, 128, 144, 272), (2, 16, 256, 16, 416)]

        def weight_source(l, n):
            kind, i, nk, ncol, _ = PIECES[n]
            slot = raw[n % RAW_SLOTS]
            whole = slot[:, 0:nk * ncol].rearrange("p (k n) -> p k n", k=nk)
            if kind in W_COLS and kind != "qa":
                c0 = W_COLS[kind] + i * ncol
                if DMAS[n] == 2:
                    return [(whole[:, k:k + nk // 2], w_in[l, k * P:(k + nk // 2) * P, c0:c0 + ncol].rearrange("(k p) n -> p k n", p=P))
                            for k in (nk // 2, 0)]
                return [(whole, w_in[l, :, c0:c0 + ncol].rearrange("(k p) n -> p k n", p=P))]
            if kind == "qa":
                out = []
                for g in range(KV_A):
                    c0 = Q_A + (g * R_A + 2 * i) * DH_A
                    out.append((whole[:, :, g * P:(g + 1) * P],
                                w_in[l, :, c0:c0 + P].rearrange("(k p) n -> p k n", p=P)))
                return out
            if kind in ("yb", "ya"):
                w = w_conv_out if kind == "yb" else w_mlstm_out
                return [(whole, w[l, :, i * ncol:(i + 1) * ncol].rearrange("(k p) n -> p k n", p=P))]
            if kind == "yc":
                w = w_attn_out[l, :, i * ncol:(i + 1) * ncol].rearrange("(g j d) n -> g d j n", g=KV_A, j=R_A)
                return [(whole[g * DH_A:(g + 1) * DH_A], w[g]) for g in range(KV_A)]
            if kind == "down":
                pair, s = divmod(i, 3)
                rows = w_ffn_down[l, s * KD * P:s * KD * P + nk * P, pair * ncol:(pair + 1) * ncol]
                return [(whole, rows.rearrange("(k p) n -> p k n", p=P))]
            w = {"out": w_out, "gate": w_ffn_gate, "up": w_ffn_up}[kind]
            return [(whole, w[l, :, i * ncol:(i + 1) * ncol].rearrange("(k p) n -> p k n", p=P))]

        @block.sync
        def _(sp):
            sp.dma_start(const[:, :], consts).then_inc(const_in, 16)
            sp.dma_start(x_rows[0:N_META, 0, :], meta).then_inc(x_in, 16)
            sp.dma_start(x_rows[N_META:P, 0, :], x_prompt[0, 0:P - N_META, :]).then_inc(x_in, 16)
            sp.dma_start(x_rows[:, 1, :], x_prompt[0, P - N_META:2 * P - N_META, :]).then_inc(x_in, 16)
            sp.dma_start(x_rows[0:N_META, 2, :], x_prompt[0, SEQ - N_META:SEQ, :]).then_inc(x_in, 16)
            sp.dma_start(x_rows[N_META:N_META + NS, 2, :], x_sample[:, 0, :]).then_inc(x_in, 16)
            sp.dma_start(s_conv[:, :, 0:HIST - 1, :].rearrange("l b t c -> (l b) (t c)"),
                         state_conv[:, :, 1:HIST, :].rearrange("l b t c -> (l b) (t c)")).then_inc(shifted, 16)
            sp.dma_start(s_k[:, :, 0:WINDOW - 1].rearrange("l b t g d -> (l b) (t g d)"),
                         cache_k[:, :, 1:WINDOW].rearrange("l b t g d -> (l b) (t g d)")).then_inc(shifted, 16)
            sp.dma_start(s_v[:, :, 0:WINDOW - 1].rearrange("l b t g d -> (l b) (t g d)"),
                         cache_v[:, :, 1:WINDOW].rearrange("l b t g d -> (l b) (t g d)")).then_inc(shifted, 16)
            sp.dma_start(s_ffn[:, :, 0, :].rearrange("l b c -> (l b) c"),
                         state_ffn[:, :, 1, :].rearrange("l b c -> (l b) c")).then_inc(shifted, 16)

            with nc.sync.Fori(0, DEPTH) as l:
                def load_vectors():
                    sp.wait_ge(vec_turned, value("vec_turned", l, 0))
                    sources = {
                        "norm1": norm1_g[l].rearrange("(r p) -> r p", p=P), "norm2": norm2_g[l].rearrange("(r p) -> r p", p=P),
                        "b_merge": b_merge[l].rearrange("(r p) -> r p", p=P), "b_dconv": b_dconv[l].rearrange("(r p) -> r p", p=P),
                        "ln_g": ln_g[l].rearrange("(r p) -> r p", p=P), "ln_b": ln_b[l].rearrange("(r p) -> r p", p=P),
                        "state_n": state_n[l].rearrange("b h p -> (b h) p"), "final": final_g.rearrange("(r p) -> r p", p=P),
                        "b_ffn": b_ffn_conv[l].rearrange("(r p) -> r p", p=P),
                        "w_ffn": w_ffn_conv[l].rearrange("t (r p) -> (t r) p", p=P),
                        "w_dconv": w_dconv[l].rearrange("t (r p) -> (t r) p", p=P)}
                    for i, rows in enumerate(VEC_ROWS):
                        r0 = 0
                        for name, n in rows:
                            sp.dma_start(vec_raw[r0:r0 + n, i, :], sources[name]).then_inc(vec_in, 16)
                            r0 += n
                    hist = state_ffn[l].rearrange("b w (c p) -> (b w c) p", p=P)
                    sp.dma_start(ffn_raw[:, 0:2, :], hist[0:2 * P].rearrange("(i p) c -> p i c", p=P)).then_inc(ffn_in, 16)
                    sp.dma_start(ffn_raw[0:NS * 2 * KF - 2 * P, 2, :], hist[2 * P:NS * 2 * KF]).then_inc(ffn_in, 16)

                def load_states():
                    sp.wait_ge(runs_done, value("runs_done", l, 0))
                    sp.dma_start(conv_raw[:, :, :], state_conv[l].rearrange("b t (c p) -> (t c) b p", p=P)).then_inc(conv_in, 16)
                    sp.dma_start(cache_k_rows[:, :, :], cache_k[l].rearrange("b t g d -> t b (g d)")).then_inc(keys_in, 16)
                    sp.dma_start(cache_v_rows[:, :, :], cache_v[l].rearrange("b t g d -> t b (g d)")).then_inc(values_in, 16)
                    with nc.allow_non_contiguous_dma(reason="a few words"):
                        sp.dma_start(bias_if[0:NH_M], b_igate[l].rearrange("(h a) -> h a", a=1)).then_inc(tiny_in, 16)
                        sp.dma_start(bias_if[NH_M:2 * NH_M], b_fgate[l].rearrange("(h a) -> h a", a=1)).then_inc(tiny_in, 16)
                        sp.dma_start(m_old, state_m[l].rearrange("b h -> h b")).then_inc(tiny_in, 16)
                        sp.dma_start(sink_b, attn_sinks[l].rearrange("(a h) -> a h", a=1).to_broadcast([P, H_A])).then_inc(tiny_in, 16)
                        sp.dma_start(sink_s, attn_sinks[l].rearrange("(h a c) -> h a c", a=1, c=1)
                                     .to_broadcast([H_A, NS, 1])).then_inc(tiny_in, 16)

                def load_c(h):
                    if h == 0:
                        sp.wait_ge(att_lo_ready, value("att_lo_ready", l, 3))
                    if h >= 2:
                        sp.compute_val(value("nums_done", l, h - 1))
                        sp.wait_ge(c_stored[h % 2], value(f"c_stored{h % 2}", l, 16 * (h // 2)))
                        sp.wait_ge(nums_done, value("nums_done", l, h - 1))
                    sp.dma_start(c_head[h % 2][:, :, :], state_c[l, :, h].rearrange("b k v -> k b v")).then_inc(c_in[h % 2], 16)

                def store_c(h):
                    sp.wait_ge(c_new, value("c_new", l, 2 * h + 2))
                    sp.dma_start(s_c[l, :, h].rearrange("b k v -> k b v"), c_head[h % 2][:, :, :]).then_inc(c_stored[h % 2], 16)

                def store_conv():
                    sp.wait_ge(hist_ready, value("hist_ready", l, 3))
                    sp.dma_start(p_conv[l, 0], conv_rows[:, :]).then_inc(conv_stored, 16)
                    sp.dma_start(s_conv[l, :, HIST - 1, :], conv_rows_s[:, :]).then_inc(conv_stored, 16)

                def store_kv():
                    sp.wait_ge(kv_ready, value("kv_ready", l, 1))
                    sp.dma_start(p_k[l, 0].rearrange("t g d -> t (g d)"), kv_rows[:, 0:P]).then_inc(kv_stored, 16)
                    sp.dma_start(p_v[l, 0].rearrange("t g d -> t (g d)"), kv_rows[:, P:2 * P]).then_inc(kv_stored, 16)
                    sp.dma_start(s_k[l, :, WINDOW - 1].rearrange("b g d -> b (g d)"), kv_rows[0:NS, 2 * P:3 * P]).then_inc(kv_stored, 16)
                    sp.dma_start(s_v[l, :, WINDOW - 1].rearrange("b g d -> b (g d)"), kv_rows[0:NS, 3 * P:4 * P]).then_inc(kv_stored, 16)

                def store_m():
                    sp.wait_ge(row_step, value("row_step", l, 8))
                    with nc.allow_non_contiguous_dma(reason="a few words"):
                        sp.dma_start(p_m[l].rearrange("a h -> h a"), m_row[:, NP - 1:NP]).then_inc(stored, 16)
                        sp.dma_start(s_m[l].rearrange("b h -> h b"), m_row[:, NP:T]).then_inc(stored, 16)

                def store_c_prompt():
                    sp.wait_ge(c_prompt_ready, value("c_prompt_ready", l, 4))
                    sp.dma_start(p_c[l, 0].rearrange("h k v -> k h v"), c_prompt[:, :, :]).then_inc(stored, 16)

                def store_n():
                    sp.wait_ge(n_ready, value("n_ready", l, 1))
                    sp.dma_start(s_n[l].rearrange("b h p -> (b h) p"), n_rows[0:NS * NH_M, :]).then_inc(stored, 16)
                    sp.dma_start(p_n[l, 0], n_rows[NS * NH_M:36, :]).then_inc(stored, 16)

                def store_ffn():
                    sp.wait_ge(gate_rows_ready, value("gate_rows_ready", l, 1))
                    sp.dma_start(p_ffn[l, 0].rearrange("w (c p) -> (w c) p", p=P), gate_rows[0:2 * KF, 0, :]).then_inc(stored, 16)
                    for b in range(NS):
                        half, r = divmod((b + 2) * KF, 5 * KF)
                        sp.dma_start(s_ffn[l, b, 1, :].rearrange("(c p) -> c p", p=P),
                                     gate_rows[r:r + KF, half, :]).then_inc(stored, 16)

                def stores_done():
                    sp.compute_val(value("kv_stored", l, 64))
                    sp.compute_val(value("stored", l, 16 * STORES))
                    sp.compute_val(value("w_split0", l, SPLIT_THROUGH[N_PIECES - 2 - RAW_SLOTS]))
                    sp.wait_ge(conv_stored, value("conv_stored", l, 32))
                    sp.wait_ge(c_stored[0], value("c_stored0", l, 32))
                    sp.wait_ge(c_stored[1], value("c_stored1", l, 32))
                    sp.wait_ge(kv_stored, value("kv_stored", l, 64))
                    sp.wait_ge(stored, value("stored", l, 16 * STORES))

                other = {0: [load_vectors], 2: [load_states], 7: [store_conv], 12: [store_kv], 14: [store_m],
                         21: [lambda: load_c(0), lambda: load_c(1)],
                         24: [lambda: store_c(0)], 25: [lambda: load_c(2)], 26: [lambda: store_c(1)], 27: [lambda: load_c(3)],
                         28: [lambda: store_c(2)], 30: [store_c_prompt], 32: [lambda: store_c(3)], 34: [store_n], 64: [store_ffn],
                         N_PIECES - 2: [stores_done]}
                for n in range(N_PIECES):
                    for move in other.get(n, ()):
                        move()
                    used = SPLIT_THROUGH[n - RAW_SLOTS] if n >= RAW_SLOTS else 0
                    sp.wait_ge(w_split[n % RAW_SLOTS], value(f"w_split{n % RAW_SLOTS}", l, used))
                    for dst, src in weight_source(l, n):
                        sp.dma_start(dst, src).then_inc(raw_in[n % RAW_SLOTS], 16)

            sp.wait_ge(shifted, 16 * 4)
            sp.wait_ge(y_rows_half, 6)
            sp.dma_start(y_prompt[0].rearrange("(i p) d -> p i d", p=P), y_rows[:, 0:2, :]).then_inc(y_stored, 16)
            sp.dma_start(y_sample[:, 0, :], y_rows[0:NS, 2, :]).then_inc(y_stored, 16)
            sp.wait_ge(y_stored, 32)

        @block.tensor
        def _(pe):
            mm, turn = nc.tensor.matmul, nc.tensor.transpose
            pe.wait_ge(const_in, 16)
            pe.wait_ge(x_in, 16 * 5)
            for c in range(KD):
                if c >= 4:
                    pe.wait_ge(took_dve, c - 3)
                a = turn(work[c % 4][:, 0:P], x_rows[:, 0, c * P:(c + 1) * P], ident)
                b = turn(work[c % 4][:, P:2 * P], x_rows[:, 1, c * P:(c + 1) * P], ident)
                turn(work[c % 4][:, 2 * P:T], x_rows[0:T - 2 * P, 2, c * P:(c + 1) * P], ident[0:T - 2 * P, 0:T - 2 * P])\
                    .then_inc(x_turned, 1)
                if c == 0:
                    a.then_inc(runs_done, 1)
                    b.then_inc(vec_turned, 1)
                if c == 1:
                    a.then_inc(vec_turned, 1)

            def sum_squares(w_act, w_dve):
                for c in range(KD):
                    if c == 0:
                        pe.wait_ge(sq_act, w_act)
                    if c == KD // 2:
                        pe.wait_ge(sq_dve, w_dve)
                    m = mm(work[0][:, 0:T], ones[:, 0:P], squares[:, c, :], start=(c == 0), stop=(c == KD - 1))
                m.then_inc(squares_summed, 1)

            with nc.tensor.Fori(0, DEPTH) as l:
                pe.wait_ge(vec_in, value("vec_in", l, 16 * VEC_DMAS))
                pe.wait_ge(ffn_in, value("ffn_in", l, 32))
                pe.wait_ge(took_dve, value("took_dve", l, 0))
                c0 = 0
                for i, rows in enumerate(VEC_ROWS):
                    n = sum(w for _, w in rows)
                    m = turn(work[1][:, c0:c0 + n], vec_raw[0:n, i, :], ident[0:n, 0:n])
                    c0 += n
                m.then_inc(vec_turned, 1)
                for i, n in enumerate((P, P, NS * 2 * KF - 2 * P)):
                    m = turn(work[2][:, i * P:i * P + n], ffn_raw[0:n, i, :], ident[0:n, 0:n])
                m.then_inc(vec_turned, 1)

                def project(n):
                    kind, i, nk, ncol, tiles = PIECES[n]
                    pe.wait_ge(w_split[n % SPLIT_SLOTS], value(f"w_split{n % SPLIT_SLOTS}", l, SPLIT_THROUGH[n]))
                    hi = w_hi[n % SPLIT_SLOTS][:, 0:nk * ncol].rearrange("p (k n) -> p k n", k=nk)
                    lo = w_lo[n % SPLIT_SLOTS][:, 0:nk * ncol].rearrange("p (k n) -> p k n", k=nk)
                    a_hi, a_lo = {"yb": (conv_hi, conv_lo), "yc": (att_hi, att_lo), "ya": (ml_hi, ml_lo),
                                  "down": (act_hi, act_lo)}.get(kind, (h_hi, h_lo))
                    k0 = KD * (i % 3) if kind == "down" else 0
                    opens = kind != "down" or i % 3 == 0
                    closes = kind != "down" or i % 3 == 2
                    for j, tile in enumerate(tiles):
                        t = TILE_NO[tile]
                        bank = ps_tile[t % 3]
                        if opens and t >= 3:
                            old = TILES[t - 3]
                            if old in ACT_NO:
                                pe.wait_ge(took_act, value("took_act", l, ACT_NO[old] + 1))
                            else:
                                pe.wait_ge(took_dve, value("took_dve", l, DVE_NO[old] + 1))
                        cols = slice(0, 8) if kind == "if" else slice(j * P, (j + 1) * P)
                        out = bank[0:8, 0:T] if kind == "if" else bank[:, 0:T]
                        for k in range(nk):
                            if j == 0:
                                if n == 0:
                                    pe.wait_ge(h_lo_ready, value("h_lo_ready", l, k + 1))
                                if n == STEP["gate", 0]:
                                    pe.wait_ge(h_lo_ready, value("h_lo_ready", l, KD + k + 1))
                                if n == STEP["yb", 0]:
                                    pe.wait_ge(conv_lo_ready, value("conv_lo_ready", l, k + 1))
                                if n == STEP["yc", 0] and k == 0:
                                    pe.wait_ge(att_lo_ready, value("att_lo_ready", l, 3))
                                    pe.wait_ge(s_lo, value("s_lo", l, 1))
                                if n == STEP["ya", 0]:
                                    pe.wait_ge(ml_lo_ready, value("ml_lo_ready", l, k + 1))
                                if n == STEP["out", 0]:
                                    pe.wait_ge(merged_lo_ready, value("merged_lo_ready", l, k + 1))
                                if kind == "down" and i < 3:
                                    pe.wait_ge(act_lo_ready, value("act_lo_ready", l, k0 + k + 1))
                            first, last = opens and k == 0, closes and k == nk - 1
                            mm(out, hi[:, k, cols], a_hi[:, k0 + k, :], start=first, stop=False, skip_group_check=True)
                            mm(out, hi[:, k, cols], a_lo[:, k0 + k, :], start=False, stop=False, skip_group_check=True)
                            m = mm(out, lo[:, k, cols], a_hi[:, k0 + k, :], start=False, stop=last, skip_group_check=True)
                        m.then_inc(runs_done, 1)

                def turn_conv_history():
                    pe.wait_ge(conv_in, value("conv_in", l, 16))
                    for half in range(2):
                        for b in range(4):
                            m = turn(work[3 + half][:, b * 120:(b + 1) * 120], conv_raw[:, 4 * half + b, :], ident[0:120, 0:120])
                        m.then_inc(conv_turned, 1)

                def turn_new_conv():
                    pe.wait_ge(took_dve, value("took_dve", l, DVE_NO["glua", KC - 1] + 1))
                    pe.wait_ge(hist_ready, value("hist_ready", l, 1))
                    for c in range(KC):
                        turn(work[0][0:HIST, c * P:(c + 1) * P], u_pad[:, c, NP:NP + HIST], ident)
                        m = turn(work[3][0:NS, c * P:(c + 1) * P], u_new[:, c, :], ident)
                    m.then_inc(conv_turned, 1)

                def turn_keys():
                    pe.wait_ge(keys_in, value("keys_in", l, 16))
                    pe.wait_ge(vec_ready, value("vec_ready", l, 2))
                    for half in range(2):
                        for b in range(4):
                            m = turn(work[1 + half][:, b * P:(b + 1) * P], cache_k_rows[:, 4 * half + b, :], ident)
                        m.then_inc(keys_turned, 1)

                def rotate():
                    pe.wait_ge(hist_ready, value("hist_ready", l, 3))
                    pe.wait_ge(took_act, value("took_act", l, ACT_NO["qa", 3] + 1))
                    for i, bank in enumerate((0, 3, 4, 1, 2)):
                        if bank == 1:
                            pe.wait_ge(keys_ready, value("keys_ready", l, 2))
                        src = qa_t[:, i, :] if i < R_A else ka_t[:, :]
                        mm(work[bank][:, 0:T], con("rot"), src, start=True, stop=True).then_inc(rotated, 1)

                def move_f():
                    pe.wait_ge(took_dve, value("took_dve", l, DVE_NO["if", 0] + 1))
                    pe.wait_ge(rope_sin, value("rope_sin", l, 1))
                    mm(work[0][0:64, 0:T], con("sel_f", 8), if_rows[:, :], start=True, stop=True).then_inc(f_moved, 1)

                def turn_kv():
                    pe.wait_ge(roped, value("roped", l, 5))
                    w0 = NP - WINDOW
                    turn(work[3][:, 0:P], ka_t[:, w0:NP], ident)
                    turn(work[3][:, P:2 * P], va_t[:, w0:NP], ident)
                    turn(work[3][0:NS, 2 * P:3 * P], ka_t[:, NP:T], ident)
                    turn(work[3][0:NS, 3 * P:4 * P], va_t[:, NP:T], ident).then_inc(kv_turned, 1)
                    for i, (t0, n) in enumerate(BLOCKS):
                        m = turn(work[4][0:n, i * P:(i + 1) * P], va_t[:, t0:t0 + n], ident)
                    m.then_inc(kv_turned, 1)

                def score_sample():
                    pe.wait_ge(qk_ready, value("qk_ready", l, 1))
                    for g in range(KV_A):
                        d = slice(g * DH_A, (g + 1) * DH_A)
                        for b in range(NS):
                            mm(work[1 + g][:, P + b:P + 32:NS], key_t[d, b, :], qa_t[d, :, NP + b], start=True, stop=True)
                    for g in range(KV_A):
                        d = slice(g * DH_A, (g + 1) * DH_A)
                        m = mm(work[1 + g][g * 32:(g + 1) * 32, P + 32:P + 33], qk_self[d, :, :].rearrange("p j b -> p (j b)"),
                               ones[d, 0:1], start=True, stop=True)
                    m.then_inc(s_scored, 1)

                def turn_sample_scores():
                    pe.wait_ge(s_keys_ready, value("s_keys_ready", l, 1))
                    mm(work[2][0:64, 0:P], s_keys[:, :], ident, start=True, stop=True).then_inc(s_turned, 1)

                def turn_sample_probs():
                    pe.wait_ge(s_self, value("s_self", l, 1))
                    mm(work[1][:, P:P + 64], s_rows[:, 0:P], ident[0:64, 0:64], start=True, stop=True)
                    mm(work[1][:, P + 64:P + 96], con("half", 64), p_self[:, :], start=True, stop=True).then_inc(s_turned, 1)

                def values_sample():
                    pe.wait_ge(s_p_ready, value("s_p_ready", l, 1))
                    pe.wait_ge(values_in, value("values_in", l, 16))
                    for g in range(KV_A):
                        d = slice(g * DH_A, (g + 1) * DH_A)
                        for b in range(NS):
                            m = mm(work[2][d, 2 * P + b:2 * P + 32:NS], cache_v_rows[:, b, d], p_keys[:, g * 32 + b:g * 32 + 32:NS],
                                   start=True, stop=True)
                    m.then_inc(s_pv_done, 1)

                def score_unit(u):
                    blk, g, q0, nq, k0, nk, per_bank = units_of(u)
                    d = slice(g * DH_A, (g + 1) * DH_A)
                    if u == 0:
                        pe.wait_ge(s_out, value("s_out", l, 2))
                        pe.wait_ge(row_step, value("row_step", l, 1))
                    for j in range(R_A):
                        bank, c = divmod(j, per_bank)
                        m = mm(work[bank][0:nq, c * nk:(c + 1) * nk], qa_t[d, j, q0:q0 + nq], ka_t[d, k0:k0 + nk],
                               start=True, stop=True)
                    m.then_inc(scored, 1)

                def turn_probs(u):
                    blk, g, q0, nq, k0, nk, per_bank = units_of(u)
                    pe.wait_ge(unit_p, value("unit_p", l, 3 * u + 3))
                    if u == 0:
                        pe.wait_ge(kv_ready, value("kv_ready", l, 2))
                    else:
                        pe.wait_ge(pt_ready, value("pt_ready", l, PT_THROUGH[u - 1]))
                    for i, (c, n) in enumerate(key_chunks(nk)):
                        for j in range(R_A):
                            out, p = work[2 + i][0:n, j * nq:(j + 1) * nq], scores[0:nq, u % 2, j * nk + c:j * nk + c + n]
                            if nq == P:
                                m = turn(out, p, ident)
                            else:
                                m = mm(out, p, ident[0:nq, 0:nq], start=True, stop=True)
                    m.then_inc(probs_turned, 1)

                def values_unit(u):
                    blk, g, q0, nq, k0, nk, per_bank = units_of(u)
                    d = slice(g * DH_A, (g + 1) * DH_A)
                    pe.wait_ge(pt_ready, value("pt_ready", l, PT_THROUGH[u]))
                    if u == 0:
                        pe.wait_ge(kv_ready, value("kv_ready", l, 2))
                    elif g == 0:
                        pe.wait_ge(att_lo_ready, value("att_lo_ready", l, blk))
                    chunks = key_chunks(nk)
                    for i, (c, n) in enumerate(chunks):
                        m = mm(work[4][d, 0:R_A * nq], va_rows[0:n, (k0 + c) // P, d], probs_t[0:n, u % 2, i * 512:i * 512 + R_A * nq],
                               start=(i == 0), stop=(i == len(chunks) - 1))
                    m.then_inc(pv_done, 1)

                def turn_ml(i):
                    t0, n = BLOCKS[i]
                    bk, bv = ((0, 1), (2, 3), (0, 1))[i]
                    if i == 0:
                        pe.wait_ge(took_act, value("took_act", l, ACT_NO["vm", 3] + 1))
                        pe.wait_ge(masked, value("masked", l, MASKS_THROUGH[-1]))
                    if i == 1:
                        pe.wait_ge(pt_ready, value("pt_ready", l, PT_THROUGH[-1]))
                    if i == 2:
                        pe.wait_ge(km_rows_ready, value("km_rows_ready", l, 1))
                        pe.wait_ge(ml_rows_ready, value("ml_rows_ready", l, 1))
                    for h in range(NH_M):
                        turn(work[bk][0:n, h * P:(h + 1) * P], km_t[:, h, t0:t0 + n], ident)
                    for h in range(NH_M):
                        m = turn(work[bv][0:n, h * P:(h + 1) * P], vm_t[:, h, t0:t0 + n], ident)
                    m.then_inc(ml_turned, 1)

                def turn_a_wt():
                    pe.wait_ge(dw_ready, value("dw_ready", l, 2))
                    pe.wait_ge(att_lo_ready, value("att_lo_ready", l, 3))
                    for i, (t0, n) in enumerate(BLOCKS):
                        for c, row in ((8 * i, a_row), (8 * i + 4, wt_row)):
                            mm(work[4][0:n, c:c + 4], row[:, t0:t0 + n], ident[0:4, 0:4], start=True, stop=True)

                def spread_dw():
                    for h in range(NH_M):
                        m = mm(work[4][:, 32 + 16 * h:48 + 16 * h], con("sel", 4)[:, h * P:(h + 1) * P], cdw_row[:, NP:NP + 2 * NS],
                               start=True, stop=True)
                    m.then_inc(dw_spread, 1)

                def turn_sample_ml():
                    pe.wait_ge(dk_ready, value("dk_ready", l, 2))
                    pe.wait_ge(km_rows_ready, value("km_rows_ready", l, 2))
                    pe.wait_ge(ml_rows_ready, value("ml_rows_ready", l, 2))
                    for h in range(NH_M):
                        turn(work[2][0:NS, h * P:(h + 1) * P], dk_t[:, h, :], ident)
                    for h in range(NH_M):
                        m = turn(work[3][0:NS, h * P:(h + 1) * P], vm_t[:, h, NP:T], ident)
                    m.then_inc(sk_turned, 1)

                def outer(i):
                    h, half = divmod(i, 2)
                    pe.wait_ge(vd_ready, value("vd_ready", l, h + 1))
                    if i == 0:
                        pe.wait_ge(sk_rows_ready, value("sk_rows_ready", l, 2))
                    else:
                        pe.wait_ge(c_new, value("c_new", l, i))
                    mm(work[3][:, 0:512], dk_rows[:, h * P:(h + 1) * P],
                       vd[:, 4 * half:4 * half + 4, :].rearrange("p b v -> p (b v)"), start=True, stop=True).then_inc(outer_done, 1)

                def nums_sample(h):
                    pe.wait_ge(c_new, value("c_new", l, 2 * h + 2))
                    for b in range(NS):
                        m = mm(work[4][:, T + h * NS + b:T + h * NS + b + 1], c_head[h % 2][:, b, :], qm_t[:, h, NP + b:NP + b + 1],
                               start=True, stop=True)
                    m.then_inc(nums_done, 1)

                def score_ml(h):
                    if h == 0:
                        pe.wait_ge(km_rows_ready, value("km_rows_ready", l, 3))
                        pe.wait_ge(ml_rows_ready, value("ml_rows_ready", l, 3))
                    else:
                        pe.wait_ge(ml_p_ready, value("ml_p_ready", l, 2 * h))
                    mm(work[0][:, 0:NP], con("sel", 4)[:, h * P:(h + 1) * P], cdw_row[:, 0:NP], start=True, stop=True)
                    for blk, ns, t0, nt, c in SOURCES:
                        m = mm(work[1][0:ns, c:c + nt], km_t[:, h, blk * P:blk * P + ns], qm_t[:, h, t0:t0 + nt], start=True, stop=True)
                    m.then_inc(ml_scored, 1)

                def nums_prompt(h):
                    pe.wait_ge(ml_p_ready, value("ml_p_ready", l, 2 * h + 2))
                    if h == 0:
                        pe.wait_ge(sk_rows_ready, value("sk_rows_ready", l, 1))
                        pe.wait_ge(dk_ready, value("dk_ready", l, 5))
                    else:
                        pe.wait_ge(c_prompt_ready, value("c_prompt_ready", l, h))
                        pe.wait_ge(n_kept, value("n_kept", l, h))
                    v = [vm_rows[0:ns, blk, h * P:(h + 1) * P] for blk, ns, _, _, _ in SOURCES]
                    k = [km_rows[0:ns, blk, h * P:(h + 1) * P] for blk, ns, _, _, _ in SOURCES]
                    for blk, ns, t0, nt, c in SOURCES:
                        mm(work[2][:, t0:NP], v[blk], decay_d[0:ns, c:c + nt], start=(blk == 0), stop=(blk == 2))
                    for blk, ns, t0, nt, c in SOURCES:
                        mm(work[2][:, NP:NP + P], k[blk], v[blk], start=(blk == 0), stop=(blk == 2), skip_group_check=True)
                    for blk, ns, t0, nt, c in SOURCES:
                        m = mm(work[2][:, NP + P:NP + P + 1], k[blk], ones[0:ns, 0:1], start=(blk == 0), stop=(blk == 2),
                               skip_group_check=True)
                    m.then_inc(num_done, 1)
                    rows = slice(32 * h, 32 * h + 32)
                    for blk, ns, t0, nt, c in SOURCES:
                        mm(work[4][rows, t0:NP], ones[0:ns, 0:32], decay_d[0:ns, c:c + nt], start=(blk == 0), stop=(blk == 2))
                    m = mm(work[4][rows, NP:T], ones[:, 0:32], qn_t[:, h, :], start=True, stop=True)
                    m.then_inc(dots_done, 1)

                def sum_conv():
                    pe.wait_ge(tap_done, value("tap_done", l, KC * CONV_W))
                    pe.wait_ge(hist_sum, value("hist_sum", l, 5))
                    pe.wait_ge(ml_p_ready, value("ml_p_ready", l, 8))
                    for c in range(KC):
                        m = mm(work[0][:, 0:T], ones[:, 0:P], uc[:, c, :], start=(c == 0), stop=(c == KC - 1))
                    m.then_inc(ln_summed, 1)

                def sum_conv_squares():
                    pe.wait_ge(ln_sq, value("ln_sq", l, 1))
                    for c in range(KC):
                        m = mm(work[1][:, 0:T], ones[:, 0:P], conv_sq[:, c, :], start=(c == 0), stop=(c == KC - 1))
                    m.then_inc(ln_summed, 1)

                def spread_m():
                    pe.wait_ge(centred, value("centred", l, 4))
                    mm(work[0][:, 0:T], con("sel32", 4), m_row[:, :], start=True, stop=True).then_inc(m_spread, 1)

                def turn_n():
                    pe.wait_ge(n_kept, value("n_kept", l, 4))
                    pe.wait_ge(c_new, value("c_new", l, 8))
                    mm(work[3][0:36, 0:P], n_all, ident, start=True, stop=True).then_inc(n_turned, 1)

                def spread_inverse():
                    pe.wait_ge(dots_inv, value("dots_inv", l, 2))
                    pe.wait_ge(ln_std, value("ln_std", l, 1))
                    pe.wait_ge(num_ready, value("num_ready", l, 4))
                    pe.wait_ge(n_ready, value("n_ready", l, 1))
                    for h in range(NH_M):
                        mm(work[h][:, 0:T], ones[32 * h:32 * h + 1, 0:P], km_t[32 * h:32 * h + 1, 2, :], start=True, stop=True)\
                            .then_inc(inv_spread, 1)

                def turn_gates():
                    pe.wait_ge(last_gate_kept, value("last_gate_kept", l, KF))
                    for half in range(2):
                        m = turn(work[0][0:110, half * P:(half + 1) * P],
                                 last_gates[:, 5 * half:5 * half + 5, :].rearrange("p t c -> p (t c)"), ident)
                    m.then_inc(gates_turned, 1)

                def sum_squares_2():
                    sum_squares(value("sq_act", l, 2), value("sq_dve", l, 2))

                sum_squares(value("sq_act", l, 1), value("sq_dve", l, 1))
                for n in range(N_PIECES):
                    if n == STEP["gate", 0]:
                        sum_squares_2()
                    project(n)
                    if n == 2:
                        turn_conv_history()
                    if n == 3:
                        turn_new_conv()
                        turn_keys()
                    if n == 6:
                        rotate()
                    if n == 7:
                        move_f()
                    if n == 8:
                        turn_kv()
                        score_sample()
                    if n == 9:
                        turn_sample_scores()
                    if n == 10:
                        turn_sample_probs()
                    if n == 11:
                        values_sample()
                    if 13 <= n < 19:
                        values_unit(n - 13)
                    if 12 <= n < 18:
                        turn_probs(n - 12)
                    if 11 <= n < 17:
                        score_unit(n - 11)
                    if n == 18:
                        turn_ml(0)
                        turn_ml(1)
                        turn_a_wt()
                        spread_dw()
                    if n == 19:
                        turn_ml(2)
                        turn_sample_ml()
                    if 22 <= n < 30 and n % 2 == 0:
                        nums_sample((n - 22) // 2)
                    if 20 <= n < 28:
                        outer(n - 20)
                    if 21 <= n < 25:
                        nums_prompt(n - 21)
                    if 20 <= n < 24:
                        score_ml(n - 20)
                    if n == 24:
                        sum_conv()
                    if n == 25:
                        sum_conv_squares()
                    if n == 26:
                        spread_m()
                    if n == 28:
                        turn_n()
                    if n == 29:
                        spread_inverse()
                    if n == STEP["down", 1]:
                        turn_gates()

            sum_squares(value("sq_act", DEPTH, 1), value("sq_dve", DEPTH, 1))
            for i, (t0, n) in enumerate(Y_BLOCKS):
                for half in range(2):
                    j = 2 * i + half
                    if j >= 4:
                        pe.wait_ge(y_rows_half, j - 3)
                    for c in range(4):
                        pe.wait_ge(h_ready, value("h_ready", DEPTH, 4 * half + c + 1))
                        m = turn(work[1 + j % 4][0:n, c * P:(c + 1) * P], h_full[:, 4 * half + c, t0:t0 + n], ident)
                    m.then_inc(y_turned, 1)

        def split_views(n, k0, k1):
            kind, i, nk, ncol, _ = PIECES[n]
            r, h, lo = raw[n % RAW_SLOTS], w_hi[n % SPLIT_SLOTS], w_lo[n % SPLIT_SLOTS]
            if kind != "qa":
                s = slice(k0 * ncol, k1 * ncol)
                return [(r[:, s], h[:, s], lo[:, s])]
            r4 = r[:, :].rearrange("p (k g j d) -> p k g j d", k=nk, g=2, j=2)
            h4 = h[:, :].rearrange("p (k j g d) -> p k g j d", k=nk, g=2, j=2)
            l4 = lo[:, :].rearrange("p (k j g d) -> p k g j d", k=nk, g=2, j=2)
            return [tuple(v[:, k0:k1, :, j, :] for v in (r4, h4, l4)) for j in range(2)]

        def tile_ready(eng, l, tile):
            eng.wait_ge(runs_done, value("runs_done", l, LAST_RUN[tile] + 1))

        @block.scalar
        def _(act):
            go = nc.scalar.activation

            def root_mean(w_sum, n, eps, src, dst, signal):
                act.wait_ge(*w_sum)
                go(dst, src, ACT.Sqrt, bias=eps, scale=1.0 / n).then_inc(signal, 1)

            with nc.scalar.Fori(0, DEPTH) as l:
                def split_hi(n):
                    act.wait_ge(raw_in[n % RAW_SLOTS], value(f"raw_in{n % RAW_SLOTS}", l, RAW_THROUGH[n]))
                    used = RUNS_THROUGH[n - SPLIT_SLOTS] if n >= SPLIT_SLOTS else 0
                    act.wait_ge(runs_done, value("runs_done", l, used))
                    for r, h, _ in split_views(n, 0, PIECES[n][2]):
                        o = go(h, r, ACT.Copy)
                    o.then_inc(w_hi_ready, 1)

                def norm(k):
                    root_mean((squares_summed, value("squares_summed", l, k + 1)), D_MODEL, RMS_EPS, work[0][:, 0:T], rms[:, :], rms_ready)
                    for c in range(KD):
                        act.wait_ge(h_ready, value("h_ready", l, KD * k + c + 1))
                        go(h_hi[:, c, :], h_full[:, c, :], ACT.Copy).then_inc(h_hi_ready, 1)

                def take(tile):
                    kind, t = tile
                    src = ps_tile[TILE_NO[tile] % 3]
                    if kind == "gate":
                        tile_ready(act, l, tile)
                        if t >= 4:
                            act.wait_ge(act_lo_ready, value("act_lo_ready", l, t - 3))
                        go(last_gates[:, :, t], src[:, T - 10:T], ACT.Copy).then_inc(last_gate_kept, 1)
                        go(gate_buf[:, t % 4, :], src[:, 0:T], ACT.Identity, bias=vcol("b_ffn", t),
                           scale=vcol("w_ffn", 2 * KF + t)).then_inc(gate_first, 1)
                        return
                    if tile not in ACT_NO:
                        return
                    tile_ready(act, l, tile)
                    src = src[:, 0:T]
                    if kind == "glub":
                        o = go(sig_b[:, t, :], src, ACT.Sigmoid)
                    elif kind == "o":
                        o = go(o_sig[:, t, :], src, ACT.Sigmoid)
                    elif kind == "g":
                        o = go(gates[:, t, :], src, ACT.Sigmoid, bias=vcol("b_merge", t))
                    elif kind == "km":
                        o = go(km_t[:, t, :], src, ACT.Copy, scale=DH_M ** -0.5)
                    else:
                        dst = {"ka": ka_t[:, :], "va": va_t[:, :], "qa": qa_t[:, t % R_A, :], "vm": vm_t[:, t % NH_M, :],
                               "qm": qm_t[:, t % NH_M, :]}[kind]
                        o = go(dst, src, ACT.Copy)
                    o.then_inc(took_act, 1)

                def take_vectors():
                    act.wait_ge(vec_turned, value("vec_turned", l, 1))
                    go(vec[:, :], work[1][:, 0:VEC_COLS], ACT.Copy).then_inc(vec_ready, 1)
                    act.wait_ge(vec_turned, value("vec_turned", l, 2))
                    go(ffn_hist[:, :], work[2][:, 0:NS * 2 * KF], ACT.Copy).then_inc(vec_ready, 1)

                def take_history():
                    for half in range(2):
                        act.wait_ge(conv_turned, value("conv_turned", l, half + 1))
                        go(u_hist[:, 4 * half:4 * half + 4, :, :].rearrange("p b t c -> p (b t c)"), work[3 + half][:, 0:480],
                           ACT.Copy).then_inc(hist_ready, 1)

                def take_conv_rows():
                    act.wait_ge(conv_turned, value("conv_turned", l, 3))
                    go(conv_rows[:, :], work[0][0:HIST, :], ACT.Copy)
                    go(conv_rows_s[:, :], work[3][0:NS, :], ACT.Copy).then_inc(hist_ready, 1)

                def take_keys():
                    for half in range(2):
                        act.wait_ge(keys_turned, value("keys_turned", l, half + 1))
                        go(key_t[:, 4 * half:4 * half + 4, :].rearrange("p b k -> p (b k)"), work[1 + half][:, :], ACT.Copy)\
                            .then_inc(keys_ready, 1)

                def take_kv():
                    act.wait_ge(kv_turned, value("kv_turned", l, 1))
                    go(kv_rows[:, 0:2 * P], work[3][:, 0:2 * P], ACT.Copy)
                    go(kv_rows[0:NS, 2 * P:4 * P], work[3][0:NS, 2 * P:4 * P], ACT.Copy).then_inc(kv_ready, 1)
                    act.wait_ge(kv_turned, value("kv_turned", l, 2))
                    go(va_rows[:, 0:2, :].rearrange("p i d -> p (i d)"), work[4][:, 0:2 * P], ACT.Copy)
                    go(va_rows[0:N_META, 2, :], work[4][0:N_META, 2 * P:3 * P], ACT.Copy).then_inc(kv_ready, 1)

                def log_forget():
                    act.wait_ge(f_moved, value("f_moved", l, 1))
                    go(lf_row[:, :], work[0][0:4, 0:T], ACT.Abs).then_inc(log_step, 1)
                    act.wait_ge(log_step, value("log_step", l, 1))
                    go(lf_row[:, :], lf_row[:, :], ACT.Exp, scale=-1.0).then_inc(log_step, 1)
                    act.wait_ge(log_step, value("log_step", l, 2))
                    go(lf_row[:, :], lf_row[:, :], ACT.Ln, bias=1.0).then_inc(log_step, 1)

                def weights_ml():
                    act.wait_ge(row_step, value("row_step", l, 10))
                    go(cdw_row[:, NP:NP + 2 * NS], cdw_row[:, NP:NP + 2 * NS], ACT.Exp).then_inc(dw_ready, 1)
                    go(wt_row[:, :], a_row[:, :], ACT.Exp, bias=cm_last).then_inc(dw_ready, 1)

                def take_sample_scores():
                    act.wait_ge(s_scored, value("s_scored", l, 1))
                    go(s_keys[:, 0:32], work[1][:, P:P + 32], ACT.Copy)
                    go(s_keys[:, 32:64], work[2][:, P:P + 32], ACT.Copy).then_inc(s_keys_ready, 1)

                def exp_sample():
                    act.wait_ge(s_max, value("s_max", l, 6))
                    go(s_rows[:, 0:WINDOW + 1], s_rows[:, 0:WINDOW + 1], ACT.Exp, bias=samp_small[:, 1:2],
                       accum_out=samp_small[:, 2:3]).then_inc(s_exp, 1)
                    go(samp_small[:, 3:4], sink_s, ACT.Exp, bias=samp_small[:, 1:2]).then_inc(s_exp, 1)

                def take_sample_probs():
                    act.wait_ge(s_turned, value("s_turned", l, 2))
                    go(p_keys[:, :], work[1][:, P:P + 64], ACT.Copy).then_inc(s_p_ready, 1)

                def sample_att_hi():
                    act.wait_ge(s_out, value("s_out", l, 2))
                    go(att_hi[:, :, NP:T], att_s[:, :, :], ACT.Copy).then_inc(att_hi_ready, 1)

                def exp_unit(u):
                    blk, g, q0, nq, k0, nk, _ = units_of(u)
                    sm = unit_small[u % 2]
                    act.wait_ge(unit_max, value("unit_max", l, 4 * u + 4))
                    if u >= 2:
                        act.wait_ge(unit_p, value("unit_p", l, 3 * u - 5))
                    for j in range(R_A):
                        s = scores[0:nq, u % 2, j * nk:(j + 1) * nk]
                        go(s, s, ACT.Exp, bias=sm[0:nq, 4 + j:5 + j], accum_out=sm[0:nq, 8 + j:9 + j]).then_inc(unit_exp, 1)
                    go(sm[0:nq, 12:16], sm[0:nq, 12:16], ACT.Exp).then_inc(unit_exp, 1)

                def take_probs(u):
                    blk, g, q0, nq, k0, nk, _ = units_of(u)
                    act.wait_ge(probs_turned, value("probs_turned", l, u + 1))
                    if u == 0:
                        act.wait_ge(kv_stored, value("kv_stored", l, 16 * 4))
                    if u >= 2:
                        act.wait_ge(pv_done, value("pv_done", l, u - 1))
                    for i, (c, n) in enumerate(key_chunks(nk)):
                        go(probs_t[0:n, u % 2, i * 512:i * 512 + R_A * nq], work[2 + i][0:n, 0:R_A * nq], ACT.Copy).then_inc(pt_ready, 1)

                def block_att_hi(blk):
                    q0, nq = BLOCKS[blk]
                    act.wait_ge(pv_done, value("pv_done", l, 2 * blk + 2))
                    go(att_hi[:, :, q0:q0 + nq], work[4][:, 0:R_A * nq].rearrange("p (j q) -> p j q", j=R_A), ACT.Copy)\
                        .then_inc(att_hi_ready, 1)

                def take_ml_rows(i):
                    n = BLOCKS[i][1]
                    act.wait_ge(ml_turned, value("ml_turned", l, i + 1))
                    go(vm_rows[0:n, i, :], work[(1, 3, 1)[i]][0:n, :], ACT.Copy).then_inc(ml_rows_ready, 1)

                def take_sample_ml():
                    act.wait_ge(sk_turned, value("sk_turned", l, 1))
                    go(dk_rows[:, :], work[2][0:NS, :], ACT.Copy).then_inc(sk_rows_ready, 1)
                    go(v_rows_s[:, :], work[3][0:NS, :], ACT.Copy).then_inc(sk_rows_ready, 1)

                def exp_decay(h):
                    act.wait_ge(decay_arg, value("decay_arg", l, 3 * h + 3))
                    go(decay_d[:, 0:416], decay_d[:, 0:416], ACT.Exp, scale=-1.0).then_inc(decay_ready, 1)
                    go(decay_d[0:N_META, 416:432], decay_d[0:N_META, 416:432], ACT.Exp, scale=-1.0).then_inc(decay_ready, 1)

                def take_nums(h):
                    act.wait_ge(num_done, value("num_done", l, h + 1))
                    go(num_all[:, h, 0:NP], work[2][:, 0:NP], ACT.Copy).then_inc(num_ready, 1)
                    go(c_prompt[:, h, :], work[2][:, NP:NP + P], ACT.Copy).then_inc(c_prompt_ready, 1)
                    go(n_all[:, 32 + h:33 + h], work[2][:, NP + P:NP + P + 1], ACT.Copy).then_inc(n_kept, 1)

                def square_conv():
                    act.wait_ge(centred, value("centred", l, 4))
                    go(conv_sq[:, :, :], uc[:, :, :], ACT.Square).then_inc(ln_sq, 1)

                def silu_conv():
                    for c in range(KC):
                        act.wait_ge(ln_inv, value("ln_inv", l, c + 2))
                        go(uc[:, c, :], uc[:, c, :], ACT.Silu, bias=vcol("ln_b", c)).then_inc(conv_silu, 1)
                    for c in range(KC):
                        act.wait_ge(conv_silu, value("conv_silu", l, c + 1))
                        go(conv_hi[:, c, :], uc[:, c, :], ACT.Copy).then_inc(conv_hi_ready, 1)

                def sample_nums():
                    act.wait_ge(nums_done, value("nums_done", l, 4))
                    go(num_all[:, :, NP:T], work[4][:, T:T + 32].rearrange("p (h b) -> p h b", h=NH_M), ACT.Copy).then_inc(num_ready, 1)

                def denominators():
                    act.wait_ge(m_spread, value("m_spread", l, 1))
                    go(km_t[:, 0, :], work[0][:, 0:T], ACT.Exp, scale=-1.0).then_inc(inv_m, 1)
                    act.wait_ge(dots_done, value("dots_done", l, 4))
                    go(km_t[:, 1, :], work[4][:, 0:T], ACT.Abs).then_inc(inv_m, 1)

                def take_n():
                    act.wait_ge(n_turned, value("n_turned", l, 1))
                    go(n_rows[:, :], work[3][0:36, 0:P], ACT.Copy).then_inc(n_ready, 1)

                def ml_his():
                    for h in range(NH_M):
                        act.wait_ge(hm_ready, value("hm_ready", l, h + 1))
                        go(ml_hi[:, h, :], num_all[:, h, :], ACT.Copy).then_inc(ml_hi_ready, 1)

                def merged_his(n):
                    for kind, t in PIECES[n][4]:
                        act.wait_ge(merged_ready, value("merged_ready", l, KD + t + 1))
                        go(h_hi[:, t, :], merged[:, t, :], ACT.Copy).then_inc(merged_hi_ready, 1)

                def silus(n):
                    for _, t in PIECES[n][4]:
                        act.wait_ge(took_dve, value("took_dve", l, DVE_NO["gate", t] + 1))
                        go(gate_buf[:, t % 4, :], gate_buf[:, t % 4, :], ACT.Silu).then_inc(gate_silu, 1)

                def act_his(n):
                    for _, t in PIECES[n][4]:
                        act.wait_ge(took_dve, value("took_dve", l, DVE_NO["up", t] + 1))
                        go(act_hi[:, t, :], gate_buf[:, t % 4, :], ACT.Copy).then_inc(act_hi_ready, 1)

                def take_gate_rows():
                    act.wait_ge(gates_turned, value("gates_turned", l, 1))
                    go(gate_rows[:, :, :].rearrange("p i c -> p (i c)"), work[0][0:110, 0:2 * P], ACT.Copy).then_inc(gate_rows_ready, 1)

                act.wait_ge(took_dve, value("took_dve", l, 0))
                go(squares[:, 0:4, :], x[:, 0:4, :], ACT.Square).then_inc(sq_act, 1)
                take_vectors()
                split_hi(0)
                split_hi(1)
                norm(0)
                for n in range(N_PIECES):
                    if n == STEP["gate", 0]:
                        act.wait_ge(took_dve, value("took_dve", l, DVE_NO["out", KD - 1] + 1))
                        go(squares[:, 0:4, :], x[:, 0:4, :], ACT.Square).then_inc(sq_act, 1)
                        norm(1)
                    for tile in PIECES[n][4]:
                        if LAST_RUN[tile] < RUNS_THROUGH[n]:
                            take(tile)
                    if n + SPLIT_SLOTS < N_PIECES:
                        split_hi(n + SPLIT_SLOTS)
                    kind = PIECES[n][0]
                    if n == 2:
                        take_history()
                    if n == 3:
                        take_conv_rows()
                        take_keys()
                    if n == 8:
                        log_forget()
                        take_kv()
                        take_sample_scores()
                        weights_ml()
                    if n == 9:
                        exp_sample()
                    if n == 10:
                        take_sample_probs()
                    if n == 11:
                        sample_att_hi()
                    if n in (14, 16, 18):
                        block_att_hi((n - 14) // 2)
                    if 12 <= n < 18:
                        take_probs(n - 12)
                    if 11 <= n < 17:
                        exp_unit(n - 11)
                    if n == 18:
                        take_ml_rows(0)
                        take_ml_rows(1)
                    if n == 19:
                        take_ml_rows(2)
                        take_sample_ml()
                    if 21 <= n < 25:
                        take_nums(n - 21)
                    if 20 <= n < 24:
                        exp_decay(n - 20)
                    if n == 24:
                        square_conv()
                    if n == 25:
                        root_mean((ln_summed, value("ln_summed", l, 2)), C_CONV, LN_EPS, work[1][:, 0:T], u_pad[:, 0, 0:T], ln_std)
                        silu_conv()
                    if n == 28:
                        sample_nums()
                        denominators()
                        take_n()
                    if n == 29:
                        ml_his()
                    if kind == "ya":
                        merged_his(n)
                    if kind == "gate":
                        silus(n)
                    if kind == "up":
                        act_his(n)
                    if n == STEP["down", 1]:
                        take_gate_rows()

            act.wait_ge(took_dve, value("took_dve", DEPTH, 0))
            go(squares[:, 0:4, :], x[:, 0:4, :], ACT.Square).then_inc(sq_act, 1)
            root_mean((squares_summed, value("squares_summed", DEPTH, 1)), D_MODEL, RMS_EPS, work[0][:, 0:T], rms[:, :], rms_ready)
            for j in range(6):
                n = Y_BLOCKS[j // 2][1]
                act.wait_ge(y_turned, j + 1)
                o = go(y_rows[0:n, j // 2, (j % 2) * 512:(j % 2 + 1) * 512], work[1 + j % 4][0:n, :], ACT.Copy)
                o.then_inc(y_rows_half, 1)

        @block.gpsimd
        def _(pool):
            tt = nc.gpsimd.tensor_tensor
            pool.memset(nothing, 0.0).then_inc(w_split[1], 1)
            with nc.gpsimd.Fori(0, DEPTH) as l:
                def split_lo(n):
                    nk, ncol = PIECES[n][2], PIECES[n][3]
                    if dve_share(nk, ncol) < nk:
                        pool.wait_ge(w_hi_ready, value("w_hi_ready", l, n + 1))
                        for r, h, lo in split_views(n, dve_share(nk, ncol), nk):
                            o = tt(lo, r, h.bitcast(F32), ALU.subtract)
                        o.then_inc(w_split[n % SPLIT_SLOTS], 1)

                def scale_c(h):
                    pool.wait_ge(c_in[h % 2], value(f"c_in{h % 2}", l, 16 * (h // 2 + 1)))
                    pool.wait_ge(dk_ready, value("dk_ready", l, 1))
                    c = c_head[h % 2][:, :, :]
                    tt(c, c, dw_b[:, h, NS:2 * NS].unsqueeze(2).to_broadcast([P, NS, P]), ALU.mult).then_inc(c_scaled, 1)

                def spread_v(h):
                    if h == 0:
                        pool.wait_ge(sk_rows_ready, value("sk_rows_ready", l, 2))
                    else:
                        pool.wait_ge(outer_done, value("outer_done", l, 2 * h))
                    tt(vd[:, :, :], v_rows_s[:, h * P:(h + 1) * P].unsqueeze(1).to_broadcast([NS, NS, P]),
                       ident[0:NS, 0:NS].unsqueeze(2).to_broadcast([NS, NS, P]), ALU.mult).then_inc(vd_ready, 1)

                def gate_nums():
                    pool.wait_ge(num_ready, value("num_ready", l, 5))
                    for h in range(NH_M):
                        tt(num_all[:, h, :], num_all[:, h, :], o_sig[:, h, :], ALU.mult).then_inc(num_gated, 1)

                split_lo(0)
                split_lo(1)
                for n in range(N_PIECES):
                    if n + SPLIT_SLOTS < N_PIECES:
                        split_lo(n + SPLIT_SLOTS)
                    if n in (19, 21, 23, 25):
                        scale_c((n - 19) // 2)
                        spread_v((n - 19) // 2)
                    if n == 28:
                        gate_nums()

        @block.vector
        def _(dve):
            tt, ts, stt = nc.vector.tensor_tensor, nc.vector.tensor_scalar, nc.vector.scalar_tensor_tensor
            dve.wait_ge(const_in, 16)
            dve.memset(small[:, 0:1], 0.0).then_inc(w_split[0], 1)
            for c in range(KD):
                dve.wait_ge(x_turned, c + 1)
                dve.tensor_copy(x[:, c, :], work[c % 4][:, 0:T]).then_inc(took_dve, 1)

            def square_half(w):
                dve.wait_ge(took_dve, w)
                tt(squares[:, 4:8, :], x[:, 4:8, :], x[:, 4:8, :], ALU.mult).then_inc(sq_dve, 1)

            def inverse_root(w):
                dve.wait_ge(rms_ready, w)
                dve.reciprocal(rms_inv[:, :], rms[:, :]).then_inc(rms_inv_ready, 1)

            with nc.vector.Fori(0, DEPTH) as l:
                def split_lo(n):
                    nk, ncol = PIECES[n][2], PIECES[n][3]
                    dve.wait_ge(w_hi_ready, value("w_hi_ready", l, n + 1))
                    for r, h, lo in split_views(n, 0, dve_share(nk, ncol)):
                        o = tt(lo, r, h.bitcast(F32), ALU.subtract)
                    o.then_inc(w_split[n % SPLIT_SLOTS], 1)

                def norm(k):
                    inverse_root(value("rms_ready", l, k + 1))
                    dve.wait_ge(rms_inv_ready, value("rms_inv_ready", l, k + 1))
                    if k == 0:
                        dve.wait_ge(vec_ready, value("vec_ready", l, 1))

                    def lo(c):
                        dve.wait_ge(h_hi_ready, value("h_hi_ready", l, KD * k + c + 1))
                        tt(h_lo[:, c, :], h_full[:, c, :], h_hi[:, c, :].bitcast(F32), ALU.subtract).then_inc(h_lo_ready, 1)

                    for c in range(KD):
                        stt(h_full[:, c, :], x[:, c, :], vcol("norm1" if k == 0 else "norm2", c), rms_inv[:, :], ALU.mult, ALU.mult)\
                            .then_inc(h_ready, 1)
                        if c >= 1:
                            lo(c - 1)
                    lo(KD - 1)

                def take(tile):
                    kind, t = tile
                    if tile not in DVE_NO:
                        return
                    bank = ps_tile[TILE_NO[tile] % 3]
                    src = bank[:, 0:T]
                    tile_ready(dve, l, tile)
                    if kind == "glua":
                        dve.wait_ge(took_act, value("took_act", l, ACT_NO["glub", t] + 1))
                        tt(u_pad[:, t, HIST:HIST + NP], src[:, 0:NP], sig_b[:, t, 0:NP], ALU.mult)
                        o = tt(u_new[:, t, :], src[:, NP:T], sig_b[:, t, NP:T], ALU.mult)
                    elif kind == "if":
                        dve.wait_ge(tiny_in, value("tiny_in", l, 16 * 5))
                        o = ts(if_rows[:, :], bank[0:8, 0:T], bias_if, None, ALU.add)
                    elif kind == "yb":
                        o = tt(merged[:, t, :], src, gates[:, KD + t, :], ALU.mult)
                    elif kind in ("yc", "ya"):
                        u = t if kind == "yc" else KD + t
                        if u >= 2:
                            dve.wait_ge(merged_ready, value("merged_ready", l, u - 1))
                        else:
                            dve.wait_ge(took_dve, value("took_dve", l, DVE_NO["yb", KD - 1] + 1))
                        o = tt(prod[:, t % 2, :], src, gates[:, (2 * KD if kind == "yc" else 0) + t, :], ALU.mult)
                    elif kind in ("out", "down"):
                        o = tt(x[:, t, :], x[:, t, :], src, ALU.add)
                    elif kind == "gate":
                        buf = gate_buf[:, t % 4, :]
                        hist = ffn_hist[:, :].rearrange("p (b w c) -> p b w c", b=NS, w=2)
                        dve.wait_ge(gate_first, value("gate_first", l, t + 1))
                        stt(buf[:, NP:T], hist[:, :, 0, t], vcol("w_ffn", t), buf[:, NP:T], ALU.mult, ALU.add).then_inc(gate_conv, 1)
                        stt(buf[:, 1:NP], src[:, 0:NP - 1], vcol("w_ffn", KF + t), buf[:, 1:NP], ALU.mult, ALU.add).then_inc(gate_conv, 1)
                        dve.wait_ge(gate_conv, value("gate_conv", l, 3 * t + 1))
                        stt(buf[:, NP:T], hist[:, :, 1, t], vcol("w_ffn", KF + t), buf[:, NP:T], ALU.mult, ALU.add).then_inc(gate_conv, 1)
                        dve.wait_ge(gate_conv, value("gate_conv", l, 3 * t + 2))
                        o = stt(buf[:, 2:NP], src[:, 0:NP - 2], vcol("w_ffn", t), buf[:, 2:NP], ALU.mult, ALU.add)
                    elif kind == "up":
                        dve.wait_ge(gate_silu, value("gate_silu", l, t + 1))
                        o = tt(gate_buf[:, t % 4, :], gate_buf[:, t % 4, :], src, ALU.mult)
                    o.then_inc(took_dve, 1)
                    if kind in ("yc", "ya"):
                        dve.wait_ge(took_dve, value("took_dve", l, DVE_NO[tile] + 1))
                        tt(merged[:, t, :], merged[:, t, :], prod[:, t % 2, :], ALU.add).then_inc(merged_ready, 1)

                def taps(first, count):
                    for i in range(first, min(first + count, KC * CONV_W)):
                        tap, c = divmod(i, KC)
                        w, dst, src = vcol("w_dconv", i), uc[:, c, 0:NP], u_pad[:, c, tap:tap + NP]
                        if tap == 0:
                            if c == 0:
                                dve.wait_ge(took_dve, value("took_dve", l, DVE_NO["glua", KC - 1] + 1))
                                dve.wait_ge(pad_zero, value("pad_zero", l, 1))
                            ts(dst, src, w, vcol("b_dconv", c), ALU.mult, ALU.add).then_inc(tap_done, 1)
                        else:
                            dve.wait_ge(tap_done, value("tap_done", l, i - KC + 1))
                            stt(dst, src, w, dst, ALU.mult, ALU.add).then_inc(tap_done, 1)

                def conv_sample():
                    flat = u_hist[:, :, :, :].rearrange("p b t c -> p b (t c)")
                    dst = uc[:, :, NP:T]
                    dve.wait_ge(hist_ready, value("hist_ready", l, 3))
                    tt(flat, flat, vcol("w_dconv", 0, 120).unsqueeze(1).to_broadcast([P, NS, 120]), ALU.mult).then_inc(hist_sum, 1)
                    tt(u_new[:, :, :], u_new[:, :, :], vcol("w_dconv", 120, 4).unsqueeze(2).to_broadcast([P, KC, NS]), ALU.mult)\
                        .then_inc(hist_sum, 1)
                    for c in range(KC):
                        if c == 0:
                            dve.wait_ge(hist_sum, value("hist_sum", l, 1))
                        o = nc.vector.tensor_reduce(uc[:, c, NP:T], u_hist[:, :, :, c], AX.X, ALU.add)
                    o.then_inc(hist_sum, 1)
                    dve.wait_ge(hist_sum, value("hist_sum", l, 3))
                    tt(dst, dst, u_new[:, :, :], ALU.add).then_inc(hist_sum, 1)
                    dve.wait_ge(hist_sum, value("hist_sum", l, 4))
                    tt(dst, dst, vcol("b_dconv", 0, 4).unsqueeze(2).to_broadcast([P, KC, NS]), ALU.add).then_inc(hist_sum, 1)

                def rope():
                    for i, bank in enumerate((0, 3, 4, 1, 2)):
                        q = qa_t[:, i, :] if i < R_A else ka_t[:, :]
                        tmp = probs_t[:, 1, (i % 2) * T:(i % 2 + 1) * T]
                        dve.wait_ge(rotated, value("rotated", l, i + 1))
                        if i >= 2:
                            dve.wait_ge(roped, value("roped", l, i - 1))
                        tt(tmp, work[bank][:, 0:T], con("sin"), ALU.mult).then_inc(rope_sin, 1)
                        tt(q, q, con("cos"), ALU.mult).then_inc(rope_cos, 1)
                        dve.wait_ge(rope_cos, value("rope_cos", l, i + 1))
                        tt(q, q, tmp, ALU.add).then_inc(roped, 1)

                def self_products():
                    dve.wait_ge(roped, value("roped", l, 5))
                    tt(qk_self[:, :, :], qa_t[:, :, NP:T], ka_t[:, NP:T].unsqueeze(1).to_broadcast([P, R_A, NS]), ALU.mult)\
                        .then_inc(qk_ready, 1)

                def row_stage():
                    steps = [0]

                    def step(ins, wait=True):
                        steps[0] += 1
                        ins.then_inc(row_step, 1)
                        if wait:
                            dve.wait_ge(row_step, value("row_step", l, steps[0]))

                    one = con("ones", 4)
                    cm, d, w = cdw_row[:, 0:NP], cdw_row[:, NP:NP + NS], cdw_row[:, NP + NS:NP + 2 * NS]
                    ig = if_rows[0:4, :]
                    dve.wait_ge(log_step, value("log_step", l, 3))
                    step(stt(lf_row[:, :], work[0][0:4, 0:T], 0.0, lf_row[:, :], ALU.min, ALU.subtract))
                    step(nc.vector.tensor_tensor_scan(b_row[:, :], one, lf_row[:, 0:NP], 0.0, ALU.mult, ALU.add))
                    step(tt(a_row[:, :], ig[:, 0:NP], b_row[:, :], ALU.subtract))
                    step(nc.vector.tensor_tensor_scan(cm, one, a_row[:, :], 0.0, ALU.mult, ALU.max))
                    step(tt(m_row[:, 0:NP], b_row[:, :], cm, ALU.add), wait=False)
                    step(ts(cm_last, cm[:, NP - 1:NP], -1.0, None, ALU.mult), wait=False)
                    step(tt(w, lf_row[:, NP:T], m_old, ALU.add))
                    step(tt(m_row[:, NP:T], w, ig[:, NP:T], ALU.max))
                    step(tt(d, ig[:, NP:T], m_row[:, NP:T], ALU.subtract), wait=False)
                    step(tt(w, w, m_row[:, NP:T], ALU.subtract))

                def softmax_sample_1():
                    sm = samp_small
                    dve.wait_ge(s_turned, value("s_turned", l, 1))
                    ts(s_rows[:, 0:P], work[2][0:64, 0:P], DH_A ** -0.5, None, ALU.mult).then_inc(s_max, 1)
                    for g in range(KV_A):
                        r = slice(32 * g, 32 * g + 32)
                        ts(s_rows[r, P:P + 1], work[1 + g][r, P + 32:P + 33], DH_A ** -0.5, None, ALU.mult).then_inc(s_max, 1)
                    dve.wait_ge(s_max, value("s_max", l, 3))
                    nc.vector.tensor_reduce(sm[:, 0:1], s_rows[:, 0:P + 1], AX.X, ALU.max).then_inc(s_max, 1)
                    dve.wait_ge(s_max, value("s_max", l, 4))
                    tt(sm[:, 0:1], sm[:, 0:1], sink_s, ALU.max).then_inc(s_max, 1)
                    dve.wait_ge(s_max, value("s_max", l, 5))
                    ts(sm[:, 1:2], sm[:, 0:1], -1.0, None, ALU.mult).then_inc(s_max, 1)

                def softmax_sample_2():
                    sm = samp_small
                    dve.wait_ge(s_exp, value("s_exp", l, 2))
                    tt(sm[:, 4:5], sm[:, 2:3], sm[:, 3:4], ALU.add).then_inc(s_max, 1)
                    dve.wait_ge(s_max, value("s_max", l, 7))
                    dve.reciprocal(sm[:, 5:6], sm[:, 4:5]).then_inc(s_max, 1)
                    dve.wait_ge(s_max, value("s_max", l, 8))
                    ts(s_rows[:, 0:P + 1], s_rows[:, 0:P + 1], sm[:, 5:6], None, ALU.mult).then_inc(s_max, 1)
                    dve.wait_ge(s_max, value("s_max", l, 9))
                    ts(p_self[:, :], con("eye32", 64), s_rows[:, P:P + 1], None, ALU.mult).then_inc(s_self, 1)

                def output_sample():
                    dve.wait_ge(s_pv_done, value("s_pv_done", l, 1))
                    tt(att_s[:, :, :], work[1][:, P + 64:P + 96].rearrange("p (j b) -> p j b", j=R_A),
                       va_t[:, NP:T].unsqueeze(1).to_broadcast([P, R_A, NS]), ALU.mult).then_inc(s_out, 1)
                    dve.wait_ge(s_out, value("s_out", l, 1))
                    tt(att_s[:, :, :], att_s[:, :, :], work[2][:, 2 * P:2 * P + 32].rearrange("p (j b) -> p j b", j=R_A), ALU.add)\
                        .then_inc(s_out, 1)
                    dve.wait_ge(att_hi_ready, value("att_hi_ready", l, 1))
                    tt(att_lo[:, :, NP:T], att_s[:, :, :], att_hi[:, :, NP:T].bitcast(F32), ALU.subtract).then_inc(s_lo, 1)

                def softmax_unit_1(u):
                    blk, g, q0, nq, k0, nk, per_bank = units_of(u)
                    sm = unit_small[u % 2]
                    dve.wait_ge(scored, value("scored", l, u + 1))
                    if u == 0:
                        dve.wait_ge(conv_stored, value("conv_stored", l, 32))
                        dve.wait_ge(tiny_in, value("tiny_in", l, 16 * 5))
                    if u >= 2:
                        dve.wait_ge(probs_turned, value("probs_turned", l, u - 1))
                    mask = con("amask", nq)[:, P:2 * P] if blk == 0 else con("amask", nq)[:, 0:nk]
                    for bank in range(R_A // per_bank):
                        c = bank * per_bank * nk
                        stt(scores[0:nq, u % 2, c:c + per_bank * nk].rearrange("p (j k) -> p j k", j=per_bank),
                            work[bank][0:nq, 0:per_bank * nk].rearrange("p (j k) -> p j k", j=per_bank), DH_A ** -0.5,
                            mask.unsqueeze(1).to_broadcast([nq, per_bank, nk]), ALU.mult, ALU.add).then_inc(masked, 1)
                    dve.wait_ge(masked, value("masked", l, MASKS_THROUGH[u]))
                    nc.vector.tensor_reduce(sm[0:nq, 0:4], scores[0:nq, u % 2, 0:R_A * nk].rearrange("p (j k) -> p j k", j=R_A),
                                            AX.X, ALU.max).then_inc(unit_max, 1)
                    sink = sink_b[0:nq, g * R_A:(g + 1) * R_A]
                    dve.wait_ge(unit_max, value("unit_max", l, 4 * u + 1))
                    tt(sm[0:nq, 0:4], sm[0:nq, 0:4], sink, ALU.max).then_inc(unit_max, 1)
                    dve.wait_ge(unit_max, value("unit_max", l, 4 * u + 2))
                    ts(sm[0:nq, 4:8], sm[0:nq, 0:4], -1.0, None, ALU.mult).then_inc(unit_max, 1)
                    tt(sm[0:nq, 12:16], sink, sm[0:nq, 0:4], ALU.subtract).then_inc(unit_max, 1)

                def softmax_unit_2(u):
                    blk, g, q0, nq, k0, nk, per_bank = units_of(u)
                    sm = unit_small[u % 2]
                    dve.wait_ge(unit_exp, value("unit_exp", l, 5 * u + 5))
                    tt(sm[0:nq, 8:12], sm[0:nq, 8:12], sm[0:nq, 12:16], ALU.add).then_inc(unit_p, 1)
                    dve.wait_ge(unit_p, value("unit_p", l, 3 * u + 1))
                    dve.reciprocal(sm[0:nq, 8:12], sm[0:nq, 8:12]).then_inc(unit_p, 1)
                    dve.wait_ge(unit_p, value("unit_p", l, 3 * u + 2))
                    s = scores[0:nq, u % 2, 0:R_A * nk].rearrange("p (j k) -> p j k", j=R_A)
                    tt(s, s, sm[0:nq, 8:12].unsqueeze(2).to_broadcast([nq, R_A, nk]), ALU.mult).then_inc(unit_p, 1)

                def block_att_lo(blk):
                    q0, nq = BLOCKS[blk]
                    dve.wait_ge(att_hi_ready, value("att_hi_ready", l, blk + 2))
                    tt(att_lo[:, :, q0:q0 + nq], work[4][:, 0:R_A * nq].rearrange("p (j q) -> p j q", j=R_A),
                       att_hi[:, :, q0:q0 + nq].bitcast(F32), ALU.subtract).then_inc(att_lo_ready, 1)

                def take_a_wt():
                    dve.wait_ge(dw_spread, value("dw_spread", l, 1))
                    dve.tensor_copy(small[:, 56:72], work[4][:, 0:16]).then_inc(a_wt_ready, 1)
                    dve.tensor_copy(small[0:N_META, 72:80], work[4][0:N_META, 16:24]).then_inc(a_wt_ready, 1)

                def km_weighted(i):
                    n = BLOCKS[i][1]
                    dve.wait_ge(ml_turned, value("ml_turned", l, i + 1))
                    dve.wait_ge(a_wt_ready, value("a_wt_ready", l, 2))
                    tt(km_rows[0:n, i, :].rearrange("p (h d) -> p h d", h=NH_M),
                       work[(0, 2, 0)[i]][0:n, :].rearrange("p (h d) -> p h d", h=NH_M),
                       a_wt[0:n, i, 4:8].unsqueeze(2).to_broadcast([n, NH_M, P]), ALU.mult).then_inc(km_rows_ready, 1)

                def sample_dk():
                    dve.tensor_copy(dw_b[:, :, :].rearrange("p h c -> p (h c)"), work[4][:, 32:96]).then_inc(dk_ready, 1)
                    dve.wait_ge(dk_ready, value("dk_ready", l, 1))
                    tt(dk_t[:, :, :], km_t[:, :, NP:T], dw_b[:, :, 0:NS], ALU.mult).then_inc(dk_ready, 1)
                    n_new = n_all[:, 0:32].rearrange("p (b h) -> p h b", h=NH_M)
                    n_old = vcol("state_n", 0, 32).rearrange("p (b h) -> p h b", h=NH_M)
                    tt(n_new, n_old, dw_b[:, :, NS:2 * NS], ALU.mult).then_inc(dk_ready, 1)
                    dve.wait_ge(dk_ready, value("dk_ready", l, 3))
                    tt(n_new, n_new, dk_t[:, :, :], ALU.add).then_inc(dk_ready, 1)
                    dve.wait_ge(dk_ready, value("dk_ready", l, 4))
                    tt(qn_t[:, :, :], qm_t[:, :, NP:T], n_new, ALU.mult).then_inc(dk_ready, 1)

                def decay_args(h):
                    dve.wait_ge(ml_scored, value("ml_scored", l, h + 1))
                    if h >= 1:
                        dve.wait_ge(dots_done, value("dots_done", l, h))
                    for blk, ns, t0, nt, c in SOURCES:
                        stt(decay_d[0:ns, c:c + nt], work[0][0:ns, t0:t0 + nt], a_wt[0:ns, blk, h:h + 1], con("pmask", ns)[:, 0:nt],
                            ALU.subtract, ALU.add).then_inc(decay_arg, 1)

                def decayed_scores(h):
                    dve.wait_ge(decay_ready, value("decay_ready", l, 2 * h + 2))
                    tt(decay_d[:, 0:416], decay_d[:, 0:416], work[1][:, 0:416], ALU.mult).then_inc(ml_p_ready, 1)
                    tt(decay_d[0:N_META, 416:432], decay_d[0:N_META, 416:432], work[1][0:N_META, 416:432], ALU.mult)\
                        .then_inc(ml_p_ready, 1)

                def add_outer(i):
                    h, half = divmod(i, 2)
                    dve.wait_ge(outer_done, value("outer_done", l, i + 1))
                    dve.wait_ge(c_scaled, value("c_scaled", l, h + 1))
                    c = c_head[h % 2][:, 4 * half:4 * half + 4, :].rearrange("p b v -> p (b v)")
                    tt(c, c, work[3][:, :], ALU.add).then_inc(c_new, 1)

                def centre():
                    dve.wait_ge(ln_summed, value("ln_summed", l, 1))
                    for c in range(KC):
                        stt(uc[:, c, :], work[0][:, 0:T], -1.0 / C_CONV, uc[:, c, :], ALU.mult, ALU.add).then_inc(centred, 1)

                def norm_conv():
                    inv = u_pad[:, 1, 0:T]
                    dve.wait_ge(ln_std, value("ln_std", l, 1))
                    dve.reciprocal(inv, u_pad[:, 0, 0:T]).then_inc(ln_inv, 1)
                    dve.wait_ge(ln_inv, value("ln_inv", l, 1))
                    for c in range(KC):
                        stt(uc[:, c, :], uc[:, c, :], vcol("ln_g", c), inv, ALU.mult, ALU.mult).then_inc(ln_inv, 1)

                def conv_los():
                    for c in range(KC):
                        dve.wait_ge(conv_hi_ready, value("conv_hi_ready", l, c + 1))
                        tt(conv_lo[:, c, :], uc[:, c, :], conv_hi[:, c, :].bitcast(F32), ALU.subtract).then_inc(conv_lo_ready, 1)

                def invert_dots():
                    dve.wait_ge(inv_m, value("inv_m", l, 2))
                    tt(km_t[:, 2, :], km_t[:, 0, :], km_t[:, 1, :], ALU.max).then_inc(dots_inv, 1)
                    dve.wait_ge(dots_inv, value("dots_inv", l, 1))
                    dve.reciprocal(km_t[:, 2, :], km_t[:, 2, :]).then_inc(dots_inv, 1)

                def divide_nums():
                    for h in range(NH_M):
                        dve.wait_ge(inv_spread, value("inv_spread", l, h + 1))
                        dve.wait_ge(num_gated, value("num_gated", l, h + 1))
                        tt(num_all[:, h, :], num_all[:, h, :], work[h][:, 0:T], ALU.mult).then_inc(hm_ready, 1)
                    for h in range(NH_M):
                        dve.wait_ge(ml_hi_ready, value("ml_hi_ready", l, h + 1))
                        tt(ml_lo[:, h, :], num_all[:, h, :], ml_hi[:, h, :].bitcast(F32), ALU.subtract).then_inc(ml_lo_ready, 1)

                def merged_los(n):
                    for kind, t in PIECES[n][4]:
                        dve.wait_ge(merged_hi_ready, value("merged_hi_ready", l, t + 1))
                        tt(h_lo[:, t, :], merged[:, t, :], h_hi[:, t, :].bitcast(F32), ALU.subtract).then_inc(merged_lo_ready, 1)

                def act_los(n):
                    for _, t in PIECES[n][4]:
                        dve.wait_ge(act_hi_ready, value("act_hi_ready", l, t + 1))
                        tt(act_lo[:, t, :], gate_buf[:, t % 4, :], act_hi[:, t, :].bitcast(F32), ALU.subtract).then_inc(act_lo_ready, 1)

                square_half(value("took_dve", l, 0))
                split_lo(0)
                split_lo(1)
                norm(0)
                nc.vector.memset(u_pad[:, :, 0:HIST], 0.0).then_inc(pad_zero, 1)
                for n in range(N_PIECES):
                    kind = PIECES[n][0]
                    if n == STEP["gate", 0]:
                        square_half(value("took_dve", l, DVE_NO["out", KD - 1] + 1))
                        norm(1)
                    for tile in PIECES[n][4]:
                        if LAST_RUN[tile] < RUNS_THROUGH[n]:
                            take(tile)
                    if n == 4:
                        conv_sample()
                    if n == 6:
                        rope()
                        self_products()
                    if n == 8:
                        row_stage()
                    if n == 9:
                        softmax_sample_1()
                        softmax_sample_2()
                    if n == 11:
                        output_sample()
                    if 12 <= n < 18:
                        softmax_unit_2(n - 12)
                    if n in (14, 16, 18):
                        block_att_lo((n - 14) // 2)
                    if 11 <= n < 17:
                        softmax_unit_1(n - 11)
                    if n == 18:
                        take_a_wt()
                        sample_dk()
                        km_weighted(0)
                        km_weighted(1)
                    if n == 19:
                        km_weighted(2)
                    if 20 <= n < 24:
                        decay_args(n - 20)
                    if 20 <= n < 28:
                        add_outer(n - 20)
                    if 20 <= n < 24:
                        decayed_scores(n - 20)
                    if n == 24:
                        centre()
                    if n == 25:
                        norm_conv()
                    if n == 26:
                        conv_los()
                    if n == 28:
                        invert_dots()
                    if n == 29:
                        divide_nums()
                    if kind == "ya":
                        merged_los(n)
                    if n + SPLIT_SLOTS < N_PIECES:
                        split_lo(n + SPLIT_SLOTS)
                    if kind == "up":
                        act_los(n)
                    if CONV_FROM <= n < CONV_FROM + CONV_STEPS:
                        taps((n - CONV_FROM) * TAPS_A_STEP, TAPS_A_STEP)

            square_half(value("took_dve", DEPTH, 0))
            inverse_root(value("rms_ready", DEPTH, 1))
            dve.wait_ge(rms_inv_ready, value("rms_inv_ready", DEPTH, 1))
            for c in range(KD):
                stt(h_full[:, c, :], x[:, c, :], vcol("final", c), rms_inv[:, :], ALU.mult, ALU.mult).then_inc(h_ready, 1)


INPUTS = ["x_prompt", "x_sample", "state_mlstm_c", "state_mlstm_n", "state_mlstm_m", "state_conv", "cache_swa_k",
          "cache_swa_v", "state_ffn_conv", "meta_tokens", "norm1_g", "w_in", "b_igate", "b_fgate", "w_mlstm_out",
          "w_dconv", "b_dconv", "ln_conv_g", "ln_conv_b", "w_conv_out", "attn_sinks", "w_attn_out", "b_merge",
          "w_out", "norm2_g", "w_ffn_gate", "w_ffn_up", "w_ffn_conv", "b_ffn_conv", "w_ffn_down", "final_norm_g"]
OUTPUTS = [(1, SEQ, D_MODEL), (NS, 1, D_MODEL)] + [
    shape for b, prompt in ((1, True), (NS, False)) for shape in (
        (DEPTH, b, NH_M, DH_M, DH_M), (DEPTH, b, NH_M, DH_M), (DEPTH, b, NH_M), (DEPTH, b, HIST, C_CONV),
        (DEPTH, b, WINDOW, KV_A, DH_A), (DEPTH, b, WINDOW, KV_A, DH_A), (DEPTH, b, FFN_CONV_W - 1, D_FF))]


def kernel(**inputs):
    import concourse.bacc as bacc
    from concourse.bass_utils import run_bass_kernel_spmd

    nc = bacc.Bacc("TRN2", target_bir_lowering=False, num_devices=1)
    arrays, ins, outs = {}, [], []
    for name in INPUTS:
        arrays[f"in_{name}"] = np.ascontiguousarray(inputs[name])
    arrays["in_constants"] = constants()
    for name, a in arrays.items():
        ins.append(nc.dram_tensor(name, a.shape, F32, kind="ExternalInput").ap())
    for i, shape in enumerate(OUTPUTS):
        outs.append(nc.dram_tensor(f"out_{i}", shape, F32, kind="ExternalOutput").ap())
    program(nc, ins, outs)
    r = run_bass_kernel_spmd(nc, [arrays], core_ids=[0])
    return tuple(r.results[0][f"out_{i}"] for i in range(len(OUTPUTS)))
```

```python
from contextlib import ExitStack

import numpy as np

import concourse.bass as bass
from concourse import mybir

F32 = mybir.dt.float32
F32R = mybir.dt.float32r
ALU = mybir.AluOpType
ACT = mybir.ActivationFunctionType
AX = mybir.AxisListType

P = 128
D_MODEL = 1024
SEQ = 256
DEPTH = 2
NS = 8
PAST_LEN = 2048
N_META = 16
NH_M = 4
DH_M = 128
W_M = NH_M * DH_M
C_CONV = 512
CONV_W = 31
HIST = CONV_W - 1
H_A = 8
KV_A = 2
R_A = H_A // KV_A
DH_A = 64
ROT_DIM = DH_A // 4
ROPE_THETA = 500000.0
WINDOW = 128
D_FF = 2816
FFN_CONV_W = 3
RMS_EPS = 1e-6
LN_EPS = 1e-5
NP = N_META + SEQ
T = NP + NS
KD = D_MODEL // P
KC = C_CONV // P
KF = D_FF // P
BLOCKS = [(0, 128), (128, 128), (256, 16)]
MASKED = 1e30

Q_M, K_M, V_M = 0, W_M, 2 * W_M
IF_G = 3 * W_M
O_G = IF_G + 2 * NH_M
GLU_A = O_G + W_M
GLU_B = GLU_A + C_CONV
Q_A = GLU_B + C_CONV
K_A = Q_A + H_A * DH_A
G_PRE = K_A + 2 * KV_A * DH_A

CONST_WIDTHS = [("ident", P), ("ones", NP), ("rot", P), ("cos", T), ("sin", T), ("amask", 2 * P),
                ("pmask", NP), ("sel", NH_M * P), ("sel32", P), ("sel_f", 64),
                ("half", P), ("eye32", R_A * NS)]
CONST_AT = {}
_at = 0
for _name, _w in CONST_WIDTHS:
    CONST_AT[_name] = (_at, _at + _w)
    _at += _w
CONST_COLS = _at

VEC_ROWS = [[("norm1", 8), ("norm2", 8), ("b_merge", 24), ("b_dconv", 4), ("ln_g", 4), ("ln_b", 4),
             ("state_n", 32), ("final", 8)],
            [("b_ffn", 22), ("w_ffn", 66)],
            [("w_dconv", 124)]]
VEC_AT = {}
_at = 0
for _block in VEC_ROWS:
    for _name, _w in _block:
        VEC_AT[_name] = (_at, _at + _w)
        _at += _w
VEC_COLS = _at
VEC_DMAS = sum(len(b) for b in VEC_ROWS) - 1


def constants():
    c = np.zeros((P, CONST_COLS), np.float32)

    def part(name):
        a, b = CONST_AT[name]
        return c[:, a:b]

    part("ident")[:] = np.eye(P)
    part("ones")[:] = 1.0
    half = ROT_DIM // 2
    pos = np.concatenate([np.arange(NP), np.full(NS, PAST_LEN)]).astype(np.float32)
    inv = np.power(np.float32(ROPE_THETA), -np.arange(half, dtype=np.float32) / half).astype(np.float32)
    ang = (pos[None, :] * inv[:, None]).astype(np.float32).astype(np.float64)
    part("cos")[:] = 1.0
    for head in range(2):
        base = head * DH_A
        part("cos")[base:base + half] = np.cos(ang)
        part("cos")[base + half:base + ROT_DIM] = np.cos(ang)
        part("sin")[base:base + half] = -np.sin(ang)
        part("sin")[base + half:base + ROT_DIM] = np.sin(ang)
        for i in range(half):
            part("rot")[base + i, base + half + i] = 1.0
            part("rot")[base + half + i, base + i] = 1.0
    q = np.arange(P)[:, None]
    k = np.arange(P)[None, :]
    part("amask")[:, :P] = np.where(k >= q, 0.0, -MASKED)
    part("amask")[:, P:] = np.where(k <= q, 0.0, -MASKED)
    part("pmask")[:, :P] = np.where(q <= k, 0.0, MASKED)
    for h in range(NH_M):
        part("sel")[h, h * P:(h + 1) * P] = 1.0
        part("sel32")[h, 32 * h:32 * h + 32] = 1.0
        part("sel_f")[NH_M + h, h] = 1.0
    for r in range(2 * R_A * NS):
        g, jb = divmod(r, R_A * NS)
        part("half")[r, g * DH_A:(g + 1) * DH_A] = 1.0
        part("eye32")[r, jb] = 1.0
    return c


def weight_pieces():
    out = []

    def add(kind, i, nk, ncol, tiles, k0=0):
        out.append((kind, i, nk, ncol, tiles, k0))

    for kind, count in (("glub", 4), ("glua", 4), ("ka", 1), ("va", 1), ("qa", 4)):
        for i in range(count):
            add(kind, i, KD, P, [(kind, i)])
    add("if", 0, KD, 8, [("if", 0)])
    for kind, count in (("km", 4), ("vm", 4), ("qm", 4), ("o", 4), ("g", 24)):
        for i in range(count):
            add(kind, i, KD, P, [(kind, i)])
    for kind in ("yc", "yb", "ya"):
        for i in range(4):
            add(kind, i, KC, 2 * P, [(kind, 2 * i), (kind, 2 * i + 1)])
    for i in range(KD):
        add("out", i, KD, P, [("out", i)])
    for i in range(KF):
        add("gate", i, KD, P, [("gate", i)])
        add("up", i, KD, P, [("up", i)])
    for i in range(KD):
        k0 = 0
        for nk in ((8, 8, 6) if i < KD - 1 else (8, 8, 3, 3)):
            add("down", i, nk, P, [("down", i)], k0)
            k0 += nk
    return out


PIECES = weight_pieces()
N_PIECES = len(PIECES)
SLOTS = 6
AHEAD = 4
assert N_PIECES % SLOTS == 0
W_COLS = {"glub": GLU_B, "glua": GLU_A, "ka": K_A, "va": K_A + P, "if": IF_G, "km": K_M, "vm": V_M, "qm": Q_M,
          "o": O_G, "g": G_PRE}
STEP = {(p[0], p[1]): n for n, p in reversed(list(enumerate(PIECES)))}
RUNS = [(n, kind, t) for n, p in enumerate(PIECES) for kind, t in p[4]]
N_RUNS = len(RUNS)
RUNS_THROUGH = [sum(1 for r in RUNS if r[0] <= n) for n in range(N_PIECES)]
LAST_RUN = {(kind, t): r for r, (n, kind, t) in enumerate(RUNS)}
FIRST_RUN = {(kind, t): r for r, (n, kind, t) in reversed(list(enumerate(RUNS)))}
TILES = sorted(LAST_RUN, key=lambda k: LAST_RUN[k])
TILE_NO = {k: i for i, k in enumerate(TILES)}
ON_ACT = ("glub", "ka", "va", "qa", "km", "vm", "qm", "o", "g")
ACT_NO, DVE_NO = {}, {}
for _k in TILES:
    _d = ACT_NO if _k[0] in ON_ACT else DVE_NO
    _d[_k] = len(_d)
DMAS = [2 if k[0] in ("qa", "yc") or k[:2] == ("qm", 0) else 1 for k in PIECES]
RAW_THROUGH = []
for _n in range(N_PIECES):
    RAW_THROUGH.append((RAW_THROUGH[_n - SLOTS] if _n >= SLOTS else 0) + 16 * DMAS[_n])
SQ_STEPS = 2 * KD - 2
GROUPS = [STEP["glub", 0], STEP["out", 0], STEP["gate", 0]]
UNITS = [(blk, g) for blk in range(3) for g in range(2)]
CONV_FROM, CONV_TO = 8, 51
BUSY = {10: 2, 14: 0, 15: 0, 16: 3, 17: 1, 18: 1, 19: 0, 20: 1, 39: 0, 40: 3, 41: 1, **{n: 2 for n in range(21, 37, 2)}}
TAPS_AT = [BUSY.get(n, 4) if CONV_FROM <= n < CONV_TO else 0 for n in range(N_PIECES)]
assert sum(TAPS_AT) >= KC * CONV_W
SCORES_AT = [21 + 2 * u for u in range(6)]
TURN_AT = [s + 3 for s in SCORES_AT]
VALUES_AT = [s + 5 for s in SCORES_AT]
ML_AT = [43 + 2 * h for h in range(4)]
OUTER_AT = [44, 45, 46, 47, 50, 51, 52, 53]
NUMS_AT = [OUTER_AT[2 * h + 1] + 1 for h in range(4)]


def dve_share(n):
    nk, ncol = PIECES[n][2:4]
    if ncol == 8:
        return nk
    busy = CONV_FROM + AHEAD <= n < STEP["gate", 0] + AHEAD
    return nk - (nk * (6 if busy else 4)) // 8


SPLIT_THROUGH = []
for _n, _p in enumerate(PIECES):
    _old = SPLIT_THROUGH[_n - SLOTS] if _n >= SLOTS else 0
    SPLIT_THROUGH.append(_old + 1 + (dve_share(_n) < _p[2]))
MASKS_THROUGH = [1, 2, 4, 6, 8, 10]
PT_THROUGH = [1, 2, 4, 6, 8, 10]
STORES = 2 + 1 + 2 + 1 + NS
Y_BLOCKS = [(N_META, P), (N_META + P, P), (NP, NS)]


def program(nc, ins, outs):
    (x_prompt, x_sample, state_c, state_n, state_m, state_conv, cache_k, cache_v, state_ffn, meta, norm1_g, w_in,
     b_igate, b_fgate, w_mlstm_out, w_dconv, b_dconv, ln_g, ln_b, w_conv_out, attn_sinks, w_attn_out, b_merge,
     w_out, norm2_g, w_ffn_gate, w_ffn_up, w_ffn_conv, b_ffn_conv, w_ffn_down, final_g, consts) = ins
    (y_prompt, y_sample, p_c, p_n, p_m, p_conv, p_k, p_v, p_ffn, s_c, s_n, s_m, s_conv, s_k, s_v, s_ffn) = outs

    with ExitStack() as ctx:
        def sb(name, shape, dt=F32):
            return ctx.enter_context(nc.sbuf_tensor(name, shape, dt))

        w_at = (nc.sbuf_base + 31) // 32 * 32
        w_raw = [sb(f"w_raw{i}", [P, 1024]) for i in range(SLOTS)]
        w_lo = [nc.alloc_sbuf_tensor_at(f"w_lo{i}", [P, 1024], F32R, offset=w_at + 4096 * i) for i in range(SLOTS)]
        w_hi = [sb(f"w_hi{i}", [P, 1024], F32R) for i in range(SLOTS)]
        x = sb("x", [P, KD, T])
        h_hi = sb("h_hi", [P, KD, T], F32R)
        h_lo = sb("h_lo", [P, KD, T], F32R)
        const = sb("const", [P, CONST_COLS])
        vec_raw = sb("vec_raw", [P, 3, P])
        vec = sb("vec", [P, VEC_COLS])
        ffn_raw = sb("ffn_raw", [P, 3, P])
        ffn_hist = sb("ffn_hist", [P, NS * 2 * KF])
        small = sb("small", [P, 128])

        zone = {}
        arena_at = (nc.sbuf_base + 31) // 32 * 32
        arena_floats = 30100
        sb("arena", [P, arena_floats])

        def at(name, shape, offset_floats, dt=F32):
            size = int(np.prod(shape[1:]))
            assert offset_floats + size <= arena_floats, (name, offset_floats, size)
            zone[name] = (offset_floats, offset_floats + size)
            return nc.alloc_sbuf_tensor_at(name, shape, dt, offset=arena_at + 4 * offset_floats)

        TK = KC * T
        gates = at("gates", [P, 24, T], 0)
        h_full = at("h_full", [P, KD, T], KD * T)
        rms = at("rms", [P, T], 16 * T)
        rms_inv = at("rms_inv", [P, T], 17 * T)
        x_rows = at("x_rows", [P, 3, D_MODEL], 0)
        o = 24 * T
        conv_hi = at("conv_hi", [P, KC, T], o, F32R)
        conv_lo = at("conv_lo", [P, KC, T], o + TK, F32R)
        sig_b = at("sig_b", [P, KC, T], o)
        conv_total = at("conv_total", [P, 2, T], o)
        conv_sq = at("conv_sq", [P, KC, T], o + TK)
        o += 2 * TK
        merged = at("merged", [P, KD, T], o)
        x_squares = at("x_squares", [P, KD, T], o)
        u_pad = at("u_pad", [P, KC, HIST + NP], o)
        u_new = at("u_new", [P, KC, NS], o + KC * (HIST + NP))
        u_hist = at("u_hist", [P, NS, HIST, KC], o + KC * (HIST + NP + NS))
        assert KC * (HIST + NP + NS) + 960 <= KD * T
        o += KD * T
        uc = at("uc", [P, KC, T], o)
        o += TK
        ffn_end = o
        act_hi = at("act_hi", [P, KF, T], 0, F32R)
        act_lo = at("act_lo", [P, KF, T], KF * T, F32R)
        assert 2 * KF * T <= ffn_end, (2 * KF * T, ffn_end)
        zb = ffn_end
        o = zb
        qa_t = at("qa_t", [P, R_A, T], o); o += TK
        ka_t = at("ka_t", [P, T], o); o += T
        va_t = at("va_t", [P, T], o); o += T
        cache_k_rows = at("cache_k_rows", [P, NS, P], o)
        att_hi = at("att_hi", [P, R_A, T], o, F32R); o += TK
        cache_v_rows = at("cache_v_rows", [P, NS, P], o); o += NS * P
        key_t = at("key_t", [P, NS, P], o)
        att_lo = at("att_lo", [P, R_A, T], o, F32R); o += TK
        va_rows = at("va_rows", [P, 3, P], o); o += 3 * P
        scores = at("scores", [P, 2, 1024], o); o += 2048
        probs_t = at("probs_t", [P, 2, 1024], o); o += 2048
        zb_end = o
        o = zb
        dk_rows = at("dk_rows", [NS, W_M], o); o += W_M
        v_rows_s = at("v_rows_s", [NS, W_M], o); o += W_M
        assert o <= zone["cache_k_rows"][0]
        prod = at("prod", [P, 2, T], zb)
        squares = at("squares", [P, 2, T], zb + 2 * T)
        vd = at("vd", [NS, NS, P], zone["cache_v_rows"][0])
        conv_rows = at("conv_rows", [HIST, C_CONV], zone["scores"][0])
        conv_rows_s = at("conv_rows_s", [NS, C_CONV], zone["scores"][0] + C_CONV)
        kv_rows = at("kv_rows", [P, 4 * P], zone["probs_t"][0])
        o = zone["va_rows"][0]
        c_head = [at(f"c_head{i}", [P, NS, P], o + i * NS * P) for i in range(2)]
        o += 2 * NS * P
        decay_d = at("decay_d", [P, 432], o); o += 432
        km_rows = at("km_rows", [P, 3, W_M], o); o += 3 * W_M
        assert o <= zb_end
        zc = zb_end
        o = zc
        km_t = at("km_t", [P, NH_M, T], o)
        conv_raw = at("conv_raw", [120, NS, P], o); o += TK
        qm_t = at("qm_t", [P, NH_M, T], o); o += TK
        vm_t = at("vm_t", [P, NH_M, T], o)
        num_all = at("num_all", [P, NH_M, T], o); o += TK
        o_sig = at("o_sig", [P, NH_M, T], o); o += TK
        ml_hi = at("ml_hi", [P, NH_M, T], o, F32R)
        if_rows = at("if_rows", [8, T], o)
        m_row = at("m_row", [4, T], o + T)
        cdw_row = at("cdw_row", [4, NP + 2 * NS], o + 2 * T); o += TK
        ml_lo = at("ml_lo", [P, NH_M, T], o, F32R)
        lf_row = at("lf_row", [4, T], o)
        b_row = at("b_row", [4, NP], o + T)
        a_row = at("a_row", [4, NP], o + T + NP)
        wt_row = at("wt_row", [4, NP], o + T + 2 * NP); o += TK
        vm_rows = at("vm_rows", [P, 3, W_M], o); o += 3 * W_M
        y_rows = at("y_rows", [P, 3, D_MODEL], 18 * T)
        o = zb + 2 * W_M
        dk_t = at("dk_t", [P, NH_M, NS], o); o += NH_M * NS
        qn_t = at("qn_t", [P, NH_M, NS], o); o += NH_M * NS
        dw_b = at("dw_b", [P, NH_M, 2 * NS], o); o += 2 * NH_M * NS
        c_prompt = at("c_prompt", [P, NH_M, P], o); o += W_M
        assert o <= zone["cache_k_rows"][0]
        n_rows = at("n_rows", [36, P], zone["km_rows"][0])
        conv_std = at("conv_std", [P, 2, T], zone["km_rows"][0] + P)
        o = zone["o_sig"][0]
        s_keys = at("s_keys", [P, 2 * R_A * NS], o); o += 64
        s_rows = at("s_rows", [64, WINDOW + 8], o); o += WINDOW + 8
        p_keys = at("p_keys", [P, 64], o); o += 64
        p_self = at("p_self", [64, 32], o); o += 32
        qk_self = at("qk_self", [P, R_A, NS], o); o += 32
        att_s = at("att_s", [P, R_A, NS], o); o += 32
        gate_buf = at("gate_buf", [P, 4, T], zone["o_sig"][0])
        last_gates = at("last_gates", [P, 10, KF], zone["ml_hi"][0])
        gate_raw = at("gate_raw", [P, 2, T], zone["ml_hi"][0] + 480)
        ffn_rms = at("ffn_rms", [P, T], zone["ml_lo"][0])
        ffn_rms_inv = at("ffn_rms_inv", [P, T], zone["ml_lo"][0] + T)
        xg_hi = at("xg_hi", [P, KD, T], zone["km_t"][0], F32R)
        xg_lo = at("xg_lo", [P, KD, T], zone["c_head0"][0], F32R)
        gate_rows = at("gate_rows", [110, 2, P], zone["ml_hi"][0] + 224)
        sink_b, sink_s, bias_if = small[:, 0:8], small[0:64, 8:9], small[0:8, 9:10]
        m_old, cm_last = small[0:4, 10:18], small[0:4, 18:19]
        n_all = small[:, 20:56]
        a_wt = small[:, 56:80].rearrange("p (b c) -> p b c", b=3)
        unit_small = [small[:, 80 + 16 * i:96 + 16 * i] for i in range(2)]
        samp_small = small[0:64, 112:120]

        ps_tile = [ctx.enter_context(nc.psum_tensor(f"ps_tile{i}", [P, 512], F32)) for i in range(3)]
        work = [ctx.enter_context(nc.psum_tensor(f"work{i}", [P, 512], F32)) for i in range(5)]

        def con(name, rows=P):
            a, b = CONST_AT[name]
            return const[0:rows, a:b]

        def vcol(name, i=0, n=1):
            a = VEC_AT[name][0] + i
            return vec[:, a:a + n]

        counts = {}

        def sem(name, per_layer, before=0):
            s = ctx.enter_context(nc.semaphore(name))
            counts[name] = (per_layer, before)
            return s

        def value(name, l, k):
            per_layer, before = counts[name]
            return l * per_layer + before + k

        const_in = sem("const_in", 0, 16)
        tables_in = sem("tables_in", 0, 16)
        x_in = sem("x_in", 0, 16 * 5)
        raw_in = [sem(f"raw_in{i}", RAW_THROUGH[N_PIECES - SLOTS + i]) for i in range(SLOTS)]
        vec_in = sem("vec_in", 16 * VEC_DMAS)
        norm_in = sem("norm_in", 16)
        ffn_in = sem("ffn_in", 32)
        conv_in = sem("conv_in", 16)
        keys_in = sem("keys_in", 16)
        values_in = sem("values_in", 16)
        tiny_in = sem("tiny_in", 16 * 5)
        c_in = [sem(f"c_in{i}", 32) for i in range(2)]
        shifted = sem("shifted", 64)
        conv_stored = sem("conv_stored", 32)
        kv_stored = sem("kv_stored", 64)
        stored = sem("stored", 16 * STORES)
        y_stored = sem("y_stored", 0, 64)
        c_stored = [sem(f"c_stored{i}", 32) for i in range(2)]
        runs_done = sem("runs_done", N_RUNS, SLOTS)
        vec_turned = sem("vec_turned", 3, 2)
        x_turned = sem("x_turned", 0, KD)
        squares_summed = sem("squares_summed", 4, 2)
        conv_turned = sem("conv_turned", 3)
        keys_turned = sem("keys_turned", 2)
        rotated = sem("rotated", 5)
        f_moved = sem("f_moved", 1)
        kv_turned = sem("kv_turned", 2)
        s_scored = sem("s_scored", 1)
        s_turned = sem("s_turned", 2)
        s_pv_done = sem("s_pv_done", 1)
        scored = sem("scored", 6)
        probs_turned = sem("probs_turned", 6)
        pv_done = sem("pv_done", 6)
        ln_summed = sem("ln_summed", 2)
        ml_turned = sem("ml_turned", 3)
        dw_spread = sem("dw_spread", 1)
        sk_turned = sem("sk_turned", 1)
        outer_done = sem("outer_done", 8)
        nums_done = sem("nums_done", 4)
        ml_scored = sem("ml_scored", 4)
        num_done = sem("num_done", 4)
        dots_done = sem("dots_done", 4)
        m_spread = sem("m_spread", 1)
        n_turned = sem("n_turned", 1)
        inv_spread = sem("inv_spread", 4)
        gates_turned = sem("gates_turned", 1)
        y_turned = sem("y_turned", 0, 6)
        took_act = sem("took_act", len(ACT_NO))
        x_squared = sem("x_squared", 0, KD)
        w_hi_ready = sem("w_hi_ready", N_PIECES)
        rms_ready = sem("rms_ready", 2)
        h_hi_ready = sem("h_hi_ready", 2 * KD)
        vec_ready = sem("vec_ready", 3)
        hist_ready = sem("hist_ready", 3)
        keys_ready = sem("keys_ready", 2)
        kv_ready = sem("kv_ready", 2)
        log_step = sem("log_step", 3)
        dw_ready = sem("dw_ready", 2)
        s_keys_ready = sem("s_keys_ready", 1)
        s_exp = sem("s_exp", 2)
        s_p_ready = sem("s_p_ready", 1)
        unit_exp = sem("unit_exp", 30)
        pt_ready = sem("pt_ready", PT_THROUGH[-1])
        att_hi_ready = sem("att_hi_ready", 4)
        ln_sq = sem("ln_sq", 1)
        ln_std = sem("ln_std", 1)
        conv_silu = sem("conv_silu", 4)
        conv_hi_ready = sem("conv_hi_ready", 4)
        ml_rows_ready = sem("ml_rows_ready", 3)
        sk_rows_ready = sem("sk_rows_ready", 2)
        decay_ready = sem("decay_ready", 8)
        num_ready = sem("num_ready", 5)
        c_prompt_ready = sem("c_prompt_ready", 4)
        inv_m = sem("inv_m", 2)
        n_kept = sem("n_kept", 4)
        n_ready = sem("n_ready", 1)
        ml_hi_ready = sem("ml_hi_ready", 4)
        gates_open = sem("gates_open", 3)
        merged_hi_ready = sem("merged_hi_ready", 8)
        gate_first = sem("gate_first", KF)
        last_gate_kept = sem("last_gate_kept", KF)
        gate_silu = sem("gate_silu", KF)
        act_hi_ready = sem("act_hi_ready", KF)
        gate_rows_ready = sem("gate_rows_ready", 1)
        y_rows_half = sem("y_rows_half", 0, 6)
        took_dve = sem("took_dve", len(DVE_NO), KD)
        squared = sem("squared", 2 * SQ_STEPS)
        rms_inv_ready = sem("rms_inv_ready", 2)
        h_ready = sem("h_ready", 2 * KD)
        h_lo_ready = sem("h_lo_ready", 2 * KD)
        pad_zero = sem("pad_zero", 1)
        tap_done = sem("tap_done", KC * CONV_W)
        hist_sum = sem("hist_sum", 5)
        rope_sin = sem("rope_sin", 5)
        roped = sem("roped", 5)
        row_step = sem("row_step", 10)
        qk_ready = sem("qk_ready", 1)
        s_max = sem("s_max", 9)
        s_self = sem("s_self", 1)
        s_out = sem("s_out", 2)
        s_lo = sem("s_lo", 1)
        masked = sem("masked", MASKS_THROUGH[-1])
        unit_max = sem("unit_max", 24)
        unit_p = sem("unit_p", 18)
        att_lo_ready = sem("att_lo_ready", 3)
        centred = sem("centred", 4)
        ln_inv = sem("ln_inv", 5)
        conv_lo_ready = sem("conv_lo_ready", 4)
        a_wt_ready = sem("a_wt_ready", 2)
        km_rows_ready = sem("km_rows_ready", 3)
        dk_ready = sem("dk_ready", 5)
        c_new = sem("c_new", 8)
        decay_arg = sem("decay_arg", 12)
        ml_p_ready = sem("ml_p_ready", 8)
        dots_inv = sem("dots_inv", 2)
        hm_ready = sem("hm_ready", 4)
        ml_lo_ready = sem("ml_lo_ready", 4)
        merged_ready = sem("merged_ready", 16)
        merged_lo_ready = sem("merged_lo_ready", 8)
        gate_conv = sem("gate_conv", 4 * KF)
        act_lo_ready = sem("act_lo_ready", KF)
        w_split = [sem(f"w_split{i}", SPLIT_THROUGH[N_PIECES - SLOTS + i]) for i in range(SLOTS)]
        rope_cos = sem("rope_cos", 5)
        conv_added = sem("conv_added", 6)
        gate_scaled = sem("gate_scaled", KF)
        c_scaled = sem("c_scaled", 4)
        vd_ready = sem("vd_ready", 4)
        num_gated = sem("num_gated", 4)

        block = ctx.enter_context(nc.Block())
        ident, ones = con("ident"), con("ones")

        def units_of(u):
            blk, g = UNITS[u]
            q0, nq = BLOCKS[blk]
            k0 = max(0, q0 - WINDOW)
            nk = q0 + nq - k0
            return blk, g, q0, nq, k0, nk, (4 if nk == P else 2)

        def key_chunks(nk):
            return [(0, P)] + ([(P, nk - P)] if nk > P else [])

        SOURCES = [(0, 128, 0, 272, 0), (1, 128, 128, 144, 272), (2, 16, 256, 16, 416)]

        def weight_source(l, n):
            kind, i, nk, ncol, _, k0 = PIECES[n]
            slot = w_raw[n % SLOTS]
            whole = slot[:, 0:nk * ncol].rearrange("p (k n) -> p k n", k=nk)
            if kind in W_COLS:
                c0 = W_COLS[kind] + i * ncol
                if DMAS[n] == 2:
                    return [(whole[:, k:k + nk // 2], w_in[l, k * P:(k + nk // 2) * P, c0:c0 + ncol].rearrange("(k p) n -> p k n", p=P))
                            for k in (nk // 2, 0)]
                return [(whole, w_in[l, :, c0:c0 + ncol].rearrange("(k p) n -> p k n", p=P))]
            if kind == "qa":
                return [(whole[:, :, g * DH_A:(g + 1) * DH_A],
                         w_in[l, :, c0:c0 + DH_A].rearrange("(k p) n -> p k n", p=P))
                        for g in range(KV_A) for c0 in [Q_A + (g * R_A + i) * DH_A]]
            if kind in ("yb", "ya"):
                w = w_conv_out if kind == "yb" else w_mlstm_out
                return [(whole, w[l, :, i * ncol:(i + 1) * ncol].rearrange("(k p) n -> p k n", p=P))]
            if kind == "yc":
                w = w_attn_out[l, :, i * ncol:(i + 1) * ncol].rearrange("(g j d) n -> g d j n", g=KV_A, j=R_A)
                return [(whole[g * DH_A:(g + 1) * DH_A], w[g]) for g in range(KV_A)]
            if kind == "down":
                rows = w_ffn_down[l, k0 * P:(k0 + nk) * P, i * ncol:(i + 1) * ncol]
                return [(whole, rows.rearrange("(k p) n -> p k n", p=P))]
            w = {"out": w_out, "gate": w_ffn_gate, "up": w_ffn_up}[kind]
            return [(whole, w[l, :, i * ncol:(i + 1) * ncol].rearrange("(k p) n -> p k n", p=P))]

        @block.sync
        def _(sp):
            sp.dma_start(const[:, 0:2 * P], consts[:, 0:2 * P]).then_inc(const_in, 16)
            sp.dma_start(x_rows[0:N_META, 0, :], meta).then_inc(x_in, 16)
            sp.dma_start(x_rows[N_META:P, 0, :], x_prompt[0, 0:P - N_META, :]).then_inc(x_in, 16)
            sp.dma_start(x_rows[:, 1, :], x_prompt[0, P - N_META:2 * P - N_META, :]).then_inc(x_in, 16)
            sp.dma_start(x_rows[0:N_META, 2, :], x_prompt[0, SEQ - N_META:SEQ, :]).then_inc(x_in, 16)
            sp.dma_start(x_rows[N_META:N_META + NS, 2, :], x_sample[:, 0, :]).then_inc(x_in, 16)
            with nc.sync.Fori(0, DEPTH) as l:
                def load_norm():
                    sp.wait_ge(vec_turned, value("vec_turned", l, 0))
                    sp.dma_start(vec_raw[0:KD, 0, :], norm1_g[l].rearrange("(r p) -> r p", p=P)).then_inc(norm_in, 16)

                def load_vectors():
                    sources = {
                        "norm2": norm2_g[l].rearrange("(r p) -> r p", p=P),
                        "b_merge": b_merge[l].rearrange("(r p) -> r p", p=P), "b_dconv": b_dconv[l].rearrange("(r p) -> r p", p=P),
                        "ln_g": ln_g[l].rearrange("(r p) -> r p", p=P), "ln_b": ln_b[l].rearrange("(r p) -> r p", p=P),
                        "state_n": state_n[l].rearrange("b h p -> (b h) p"), "final": final_g.rearrange("(r p) -> r p", p=P),
                        "b_ffn": b_ffn_conv[l].rearrange("(r p) -> r p", p=P),
                        "w_ffn": w_ffn_conv[l].rearrange("t (r p) -> (t r) p", p=P),
                        "w_dconv": w_dconv[l].rearrange("t (r p) -> (t r) p", p=P)}
                    for i, rows in enumerate(VEC_ROWS):
                        r0 = 0
                        for name, n in rows:
                            if name != "norm1":
                                sp.dma_start(vec_raw[r0:r0 + n, i, :], sources[name]).then_inc(vec_in, 16)
                            r0 += n
                    hist = state_ffn[l].rearrange("b w (c p) -> (b w c) p", p=P)
                    sp.dma_start(ffn_raw[:, 0:2, :], hist[0:2 * P].rearrange("(i p) c -> p i c", p=P)).then_inc(ffn_in, 16)
                    sp.dma_start(ffn_raw[0:NS * 2 * KF - 2 * P, 2, :], hist[2 * P:NS * 2 * KF]).then_inc(ffn_in, 16)

                def load_states():
                    sp.wait_ge(runs_done, value("runs_done", l, 0))
                    sp.dma_start(conv_raw[:, :, :], state_conv[l].rearrange("b t (c p) -> (t c) b p", p=P)).then_inc(conv_in, 16)
                    sp.dma_start(cache_k_rows[:, :, :], cache_k[l].rearrange("b t g d -> t b (g d)")).then_inc(keys_in, 16)
                    sp.dma_start(cache_v_rows[:, :, :], cache_v[l].rearrange("b t g d -> t b (g d)")).then_inc(values_in, 16)
                    with nc.allow_non_contiguous_dma(reason="a few words"):
                        sp.dma_start(bias_if[0:NH_M], b_igate[l].rearrange("(h a) -> h a", a=1)).then_inc(tiny_in, 16)
                        sp.dma_start(bias_if[NH_M:2 * NH_M], b_fgate[l].rearrange("(h a) -> h a", a=1)).then_inc(tiny_in, 16)
                        sp.dma_start(m_old, state_m[l].rearrange("b h -> h b")).then_inc(tiny_in, 16)
                        sp.dma_start(sink_b, attn_sinks[l].rearrange("(a h) -> a h", a=1).to_broadcast([P, H_A])).then_inc(tiny_in, 16)
                        sp.dma_start(sink_s, attn_sinks[l].rearrange("(h a c) -> h a c", a=1, c=1)
                                     .to_broadcast([H_A, NS, 1])).then_inc(tiny_in, 16)

                def shift_windows():
                    sp.dma_start(s_conv[l, :, 0:HIST - 1, :].rearrange("b t c -> b (t c)"),
                                 state_conv[l, :, 1:HIST, :].rearrange("b t c -> b (t c)")).then_inc(shifted, 16)
                    sp.dma_start(s_k[l, :, 0:WINDOW - 1].rearrange("b t g d -> b (t g d)"),
                                 cache_k[l, :, 1:WINDOW].rearrange("b t g d -> b (t g d)")).then_inc(shifted, 16)
                    sp.dma_start(s_v[l, :, 0:WINDOW - 1].rearrange("b t g d -> b (t g d)"),
                                 cache_v[l, :, 1:WINDOW].rearrange("b t g d -> b (t g d)")).then_inc(shifted, 16)
                    sp.dma_start(s_ffn[l, :, 0, :], state_ffn[l, :, 1, :]).then_inc(shifted, 16)

                def load_c(h):
                    if h == 0:
                        sp.wait_ge(att_lo_ready, value("att_lo_ready", l, 3))
                    if h >= 2:
                        sp.compute_val(value("nums_done", l, h - 1))
                        sp.wait_ge(c_stored[h % 2], value(f"c_stored{h % 2}", l, 16 * (h // 2)))
                        sp.wait_ge(nums_done, value("nums_done", l, h - 1))
                    sp.dma_start(c_head[h % 2][:, :, :], state_c[l, :, h].rearrange("b k v -> k b v")).then_inc(c_in[h % 2], 16)

                def store_c(h):
                    sp.wait_ge(c_new, value("c_new", l, 2 * h + 2))
                    sp.dma_start(s_c[l, :, h].rearrange("b k v -> k b v"), c_head[h % 2][:, :, :]).then_inc(c_stored[h % 2], 16)

                def store_conv():
                    sp.wait_ge(hist_ready, value("hist_ready", l, 3))
                    sp.dma_start(p_conv[l, 0], conv_rows[:, :]).then_inc(conv_stored, 16)
                    sp.dma_start(s_conv[l, :, HIST - 1, :], conv_rows_s[:, :]).then_inc(conv_stored, 16)

                def store_kv():
                    sp.wait_ge(kv_ready, value("kv_ready", l, 1))
                    sp.dma_start(p_k[l, 0].rearrange("t g d -> t (g d)"), kv_rows[:, 0:P]).then_inc(kv_stored, 16)
                    sp.dma_start(p_v[l, 0].rearrange("t g d -> t (g d)"), kv_rows[:, P:2 * P]).then_inc(kv_stored, 16)
                    sp.dma_start(s_k[l, :, WINDOW - 1].rearrange("b g d -> b (g d)"), kv_rows[0:NS, 2 * P:3 * P]).then_inc(kv_stored, 16)
                    sp.dma_start(s_v[l, :, WINDOW - 1].rearrange("b g d -> b (g d)"), kv_rows[0:NS, 3 * P:4 * P]).then_inc(kv_stored, 16)

                def store_m():
                    sp.wait_ge(row_step, value("row_step", l, 8))
                    with nc.allow_non_contiguous_dma(reason="a few words"):
                        sp.dma_start(p_m[l].rearrange("a h -> h a"), m_row[:, NP - 1:NP]).then_inc(stored, 16)
                        sp.dma_start(s_m[l].rearrange("b h -> h b"), m_row[:, NP:T]).then_inc(stored, 16)

                def store_c_prompt():
                    sp.wait_ge(c_prompt_ready, value("c_prompt_ready", l, 4))
                    sp.dma_start(p_c[l, 0].rearrange("h k v -> k h v"), c_prompt[:, :, :]).then_inc(stored, 16)

                def store_n():
                    sp.wait_ge(n_ready, value("n_ready", l, 1))
                    sp.dma_start(s_n[l].rearrange("b h p -> (b h) p"), n_rows[0:NS * NH_M, :]).then_inc(stored, 16)
                    sp.dma_start(p_n[l, 0], n_rows[NS * NH_M:36, :]).then_inc(stored, 16)

                def store_ffn():
                    sp.wait_ge(gate_rows_ready, value("gate_rows_ready", l, 1))
                    sp.dma_start(p_ffn[l, 0].rearrange("w (c p) -> (w c) p", p=P), gate_rows[0:2 * KF, 0, :]).then_inc(stored, 16)
                    for b in range(NS):
                        half, r = divmod((b + 2) * KF, 5 * KF)
                        sp.dma_start(s_ffn[l, b, 1, :].rearrange("(c p) -> c p", p=P),
                                     gate_rows[r:r + KF, half, :]).then_inc(stored, 16)

                def stores_done():
                    sp.compute_val(value("kv_stored", l, 64))
                    sp.compute_val(value("stored", l, 16 * STORES))
                    sp.compute_val(value("runs_done", l, RUNS_THROUGH[N_PIECES - 2 - SLOTS]))
                    sp.wait_ge(conv_stored, value("conv_stored", l, 32))
                    sp.wait_ge(c_stored[0], value("c_stored0", l, 32))
                    sp.wait_ge(c_stored[1], value("c_stored1", l, 32))
                    sp.wait_ge(kv_stored, value("kv_stored", l, 64))
                    sp.wait_ge(stored, value("stored", l, 16 * STORES))

                other = {0: [load_norm], 3: [load_vectors], 6: [load_states], 14: [store_conv], 24: [store_kv], 28: [store_m],
                         43: [lambda: load_c(0), lambda: load_c(1)],
                         50: [lambda: store_c(0)], 52: [lambda: load_c(2), lambda: store_c(1)], 54: [lambda: load_c(3)],
                         57: [lambda: store_c(2)], 59: [lambda: store_c(3)], 60: [store_c_prompt], 64: [store_n],
                         90: [shift_windows], 132: [store_ffn], N_PIECES - 2: [stores_done]}
                for n in range(N_PIECES):
                    for move in other.get(n, ()):
                        move()
                    used = RUNS_THROUGH[n - SLOTS] if n >= SLOTS else RUNS_THROUGH[n - SLOTS + N_PIECES] - N_RUNS
                    sp.wait_ge(runs_done, value("runs_done", l, used))
                    for dst, src in weight_source(l, n):
                        sp.dma_start(dst, src).then_inc(raw_in[n % SLOTS], 16)

            sp.wait_ge(shifted, value("shifted", DEPTH, 0))
            for half in range(2):
                cols = slice(half * 512, (half + 1) * 512)
                sp.wait_ge(y_rows_half, 3 * half + 2)
                sp.dma_start(y_prompt[0, :, cols].rearrange("(i p) d -> p i d", p=P), y_rows[:, 0:2, cols]).then_inc(y_stored, 16)
                sp.wait_ge(y_rows_half, 3 * half + 3)
                sp.dma_start(y_sample[:, 0, cols], y_rows[0:NS, 2, cols]).then_inc(y_stored, 16)
            sp.wait_ge(y_stored, 64)

        @block.tensor
        def _(pe):
            mm, turn = nc.tensor.matmul, nc.tensor.transpose
            pe.wait_ge(const_in, 16)
            pe.wait_ge(x_in, 16 * 5)
            for c in range(KD):
                if c >= 4:
                    pe.wait_ge(took_dve, c - 3)
                turn(work[c % 4][:, 0:P], x_rows[:, 0, c * P:(c + 1) * P], ident)
                turn(work[c % 4][:, P:2 * P], x_rows[:, 1, c * P:(c + 1) * P], ident)
                turn(work[c % 4][:, 2 * P:T], x_rows[0:T - 2 * P, 2, c * P:(c + 1) * P], ident[0:T - 2 * P, 0:T - 2 * P])\
                    .then_inc(x_turned, 1)

            def sum_squares(i, ready):
                pe.wait_ge(squared, ready)
                mm(work[0][:, 0:T], ones[:, 0:P], squares[:, 1 - i, :], start=(i == 0), stop=(i == 1), skip_group_check=True)\
                    .then_inc(squares_summed, 1)

            pe.wait_ge(took_dve, 5)
            for c in range(KD):
                pe.wait_ge(x_squared, c + 1)
                m = mm(work[0][:, 0:T], ones[:, 0:P], x_squares[:, c, :], start=(c == 0), stop=(c == KD - 1))
                if c >= KD - 2:
                    m.then_inc(squares_summed, 1)

            with nc.tensor.Fori(0, DEPTH) as l:
                def turn_norm():
                    pe.wait_ge(norm_in, value("norm_in", l, 16))
                    mm(work[1][:, 0:KD], vec_raw[0:KD, 0, :], ident[0:KD, 0:KD], start=True, stop=True).then_inc(vec_turned, 1)

                def turn_vectors():
                    pe.wait_ge(vec_in, value("vec_in", l, 16 * VEC_DMAS))
                    pe.wait_ge(ffn_in, value("ffn_in", l, 32))
                    pe.wait_ge(vec_ready, value("vec_ready", l, 1))
                    c0 = 0
                    for i, rows in enumerate(VEC_ROWS):
                        n = sum(w for _, w in rows)
                        m = turn(work[1][:, c0:c0 + n], vec_raw[0:n, i, :], ident[0:n, 0:n])
                        c0 += n
                    m.then_inc(vec_turned, 1)
                    for i, n in enumerate((P, P, NS * 2 * KF - 2 * P)):
                        m = turn(work[2][:, i * P:i * P + n], ffn_raw[0:n, i, :], ident[0:n, 0:n])
                    m.then_inc(vec_turned, 1)

                def sum_norm(norm):
                    sum_squares(0, value("squared", l, SQ_STEPS * norm + SQ_STEPS - 1))
                    sum_squares(1, value("squared", l, SQ_STEPS * norm + SQ_STEPS))

                def project(pieces):
                    runs = []
                    for n in pieces:
                        kind, i, nk, ncol, tiles, k0 = PIECES[n]
                        pe.wait_ge(w_split[n % SLOTS], value(f"w_split{n % SLOTS}", l, SPLIT_THROUGH[n]))
                        hi = w_hi[n % SLOTS][:, 0:nk * ncol].rearrange("p (k n) -> p k n", k=nk)
                        lo = w_lo[n % SLOTS][:, 0:nk * ncol].rearrange("p (k n) -> p k n", k=nk)
                        for j, tile in enumerate(tiles):
                            run = next(i for i, x in enumerate(RUNS) if x == (n,) + tile)
                            t = TILE_NO[tile]
                            bank = ps_tile[t % 3]
                            opens, closes = run == FIRST_RUN[tile], run == LAST_RUN[tile]
                            if opens and t >= 3:
                                old = TILES[t - 3]
                                if old in ACT_NO:
                                    pe.wait_ge(took_act, value("took_act", l, ACT_NO[old] + 1))
                                else:
                                    pe.wait_ge(took_dve, value("took_dve", l, DVE_NO[old] + 1))
                            cols = slice(0, 8) if kind == "if" else slice(j * P, (j + 1) * P)
                            out = bank[0:8, 0:T] if kind == "if" else bank[:, 0:T]
                            if len(pieces) == 1:
                                products(n, out, hi[:, :, cols], lo[:, :, cols], range(nk), opens, closes, j == 0)
                            else:
                                runs.append((n, out, hi[:, :, cols], lo[:, :, cols]))
                    for k in range(KD if runs else 0):
                        if pieces[0] == STEP["gate", 0] and k == 4:
                            sum_norm(0)
                        for n, out, hi, lo in runs:
                            products(n, out, hi, lo, [k], True, True, n == pieces[0])

                def products(n, out, hi, lo, ks, opens, closes, first_use):
                    kind, i, nk, ncol, tiles, k0 = PIECES[n]
                    a_hi, a_lo = {"yb": (conv_hi, conv_lo), "yc": (att_hi, att_lo), "ya": (ml_hi, ml_lo),
                                  "down": (act_hi, act_lo), "gate": (xg_hi, xg_lo), "up": (xg_hi, xg_lo)}.get(kind, (h_hi, h_lo))
                    for k in ks:
                        if first_use:
                            if n == 0:
                                pe.wait_ge(h_lo_ready, value("h_lo_ready", l, k + 1))
                            if n == STEP["gate", 0]:
                                pe.wait_ge(h_lo_ready, value("h_lo_ready", l, KD + k + 1))
                            if n == STEP["yb", 0]:
                                pe.wait_ge(conv_lo_ready, value("conv_lo_ready", l, k + 1))
                            if n == STEP["yc", 0] and k == 0:
                                pe.wait_ge(att_lo_ready, value("att_lo_ready", l, 3))
                                pe.wait_ge(s_lo, value("s_lo", l, 1))
                            if n == STEP["ya", 0]:
                                pe.wait_ge(ml_lo_ready, value("ml_lo_ready", l, k + 1))
                            if n == STEP["out", 0]:
                                pe.wait_ge(merged_lo_ready, value("merged_lo_ready", l, k + 1))
                            if kind == "down" and i == 0:
                                pe.wait_ge(act_lo_ready, value("act_lo_ready", l, k0 + k + 1))
                        first, last = opens and k == 0, closes and k == nk - 1
                        mm(out, hi[:, k, :], a_hi[:, k0 + k, :], start=first, stop=False, skip_group_check=True)
                        mm(out, hi[:, k, :], a_lo[:, k0 + k, :], start=False, stop=False, skip_group_check=True)
                        m = mm(out, lo[:, k, :], a_hi[:, k0 + k, :], start=False, stop=last, skip_group_check=True)
                        if k == nk - 1:
                            m.then_inc(runs_done, 1)

                def turn_conv_history():
                    pe.wait_ge(conv_in, value("conv_in", l, 16))
                    for half in range(2):
                        for b in range(4):
                            m = turn(work[3 + half][:, b * 120:(b + 1) * 120], conv_raw[:, 4 * half + b, :], ident[0:120, 0:120])
                        m.then_inc(conv_turned, 1)

                def turn_new_conv():
                    pe.wait_ge(took_dve, value("took_dve", l, DVE_NO["glua", KC - 1] + 1))
                    pe.wait_ge(hist_ready, value("hist_ready", l, 1))
                    for c in range(KC):
                        turn(work[0][0:HIST, c * P:(c + 1) * P], u_pad[:, c, NP:NP + HIST], ident)
                        m = turn(work[3][0:NS, c * P:(c + 1) * P], u_new[:, c, :], ident)
                    m.then_inc(conv_turned, 1)

                def turn_keys():
                    pe.wait_ge(keys_in, value("keys_in", l, 16))
                    pe.wait_ge(vec_ready, value("vec_ready", l, 3))
                    for half in range(2):
                        for b in range(4):
                            m = turn(work[1 + half][:, b * P:(b + 1) * P], cache_k_rows[:, 4 * half + b, :], ident)
                        m.then_inc(keys_turned, 1)

                def rotate():
                    pe.wait_ge(tables_in, 16)
                    pe.wait_ge(hist_ready, value("hist_ready", l, 3))
                    pe.wait_ge(took_act, value("took_act", l, ACT_NO["qa", 3] + 1))
                    for i, bank in enumerate((0, 3, 4, 1, 2)):
                        if bank == 1:
                            pe.wait_ge(keys_ready, value("keys_ready", l, 2))
                        src = qa_t[:, i, :] if i < R_A else ka_t[:, :]
                        mm(work[bank][:, 0:T], con("rot"), src, start=True, stop=True).then_inc(rotated, 1)

                def move_f():
                    pe.wait_ge(took_dve, value("took_dve", l, DVE_NO["if", 0] + 1))
                    pe.wait_ge(rope_sin, value("rope_sin", l, 1))
                    mm(work[0][0:64, 0:T], con("sel_f", 8), if_rows[:, :], start=True, stop=True).then_inc(f_moved, 1)

                def turn_kv():
                    pe.wait_ge(roped, value("roped", l, 5))
                    w0 = NP - WINDOW
                    turn(work[3][:, 0:P], ka_t[:, w0:NP], ident)
                    turn(work[3][:, P:2 * P], va_t[:, w0:NP], ident)
                    turn(work[3][0:NS, 2 * P:3 * P], ka_t[:, NP:T], ident)
                    turn(work[3][0:NS, 3 * P:4 * P], va_t[:, NP:T], ident).then_inc(kv_turned, 1)
                    for i, (t0, n) in enumerate(BLOCKS):
                        m = turn(work[4][0:n, i * P:(i + 1) * P], va_t[:, t0:t0 + n], ident)
                    m.then_inc(kv_turned, 1)

                def score_sample():
                    pe.wait_ge(qk_ready, value("qk_ready", l, 1))
                    for g in range(KV_A):
                        d = slice(g * DH_A, (g + 1) * DH_A)
                        for b in range(NS):
                            mm(work[1 + g][:, P + b:P + 32:NS], key_t[d, b, :], qa_t[d, :, NP + b], start=True, stop=True)
                    for g in range(KV_A):
                        d = slice(g * DH_A, (g + 1) * DH_A)
                        m = mm(work[1 + g][g * 32:(g + 1) * 32, P + 32:P + 33], qk_self[d, :, :].rearrange("p j b -> p (j b)"),
                               ones[d, 0:1], start=True, stop=True)
                    m.then_inc(s_scored, 1)

                def turn_sample_scores():
                    pe.wait_ge(s_keys_ready, value("s_keys_ready", l, 1))
                    mm(work[2][0:64, 0:P], s_keys[:, :], ident, start=True, stop=True).then_inc(s_turned, 1)

                def turn_sample_probs():
                    pe.wait_ge(s_self, value("s_self", l, 1))
                    mm(work[1][:, P:P + 64], s_rows[:, 0:P], ident[0:64, 0:64], start=True, stop=True)
                    mm(work[1][:, P + 64:P + 96], con("half", 64), p_self[:, :], start=True, stop=True).then_inc(s_turned, 1)

                def values_sample():
                    pe.wait_ge(s_p_ready, value("s_p_ready", l, 1))
                    pe.wait_ge(values_in, value("values_in", l, 16))
                    for g in range(KV_A):
                        d = slice(g * DH_A, (g + 1) * DH_A)
                        for b in range(NS):
                            m = mm(work[2][d, 2 * P + b:2 * P + 32:NS], cache_v_rows[:, b, d], p_keys[:, g * 32 + b:g * 32 + 32:NS],
                                   start=True, stop=True)
                    m.then_inc(s_pv_done, 1)

                def score_unit(u):
                    blk, g, q0, nq, k0, nk, per_bank = units_of(u)
                    d = slice(g * DH_A, (g + 1) * DH_A)
                    if u == 0:
                        pe.wait_ge(s_out, value("s_out", l, 2))
                        pe.wait_ge(row_step, value("row_step", l, 1))
                    for j in range(R_A):
                        bank, c = divmod(j, per_bank)
                        m = mm(work[bank][0:nq, c * nk:(c + 1) * nk], qa_t[d, j, q0:q0 + nq], ka_t[d, k0:k0 + nk],
                               start=True, stop=True)
                    m.then_inc(scored, 1)

                def turn_probs(u):
                    blk, g, q0, nq, k0, nk, per_bank = units_of(u)
                    pe.wait_ge(unit_p, value("unit_p", l, 3 * u + 3))
                    if u == 0:
                        pe.wait_ge(kv_ready, value("kv_ready", l, 2))
                    else:
                        pe.wait_ge(pt_ready, value("pt_ready", l, PT_THROUGH[u - 1]))
                    for i, (c, n) in enumerate(key_chunks(nk)):
                        for j in range(R_A):
                            out, p = work[2 + i][0:n, j * nq:(j + 1) * nq], scores[0:nq, u % 2, j * nk + c:j * nk + c + n]
                            if nq == P:
                                m = turn(out, p, ident)
                            else:
                                m = mm(out, p, ident[0:nq, 0:nq], start=True, stop=True)
                    m.then_inc(probs_turned, 1)

                def values_unit(u):
                    blk, g, q0, nq, k0, nk, per_bank = units_of(u)
                    d = slice(g * DH_A, (g + 1) * DH_A)
                    pe.wait_ge(pt_ready, value("pt_ready", l, PT_THROUGH[u]))
                    if u == 0:
                        pe.wait_ge(kv_ready, value("kv_ready", l, 2))
                    elif g == 0:
                        pe.wait_ge(att_lo_ready, value("att_lo_ready", l, blk))
                    chunks = key_chunks(nk)
                    for i, (c, n) in enumerate(chunks):
                        m = mm(work[4][d, 0:R_A * nq], va_rows[0:n, (k0 + c) // P, d], probs_t[0:n, u % 2, i * 512:i * 512 + R_A * nq],
                               start=(i == 0), stop=(i == len(chunks) - 1))
                    m.then_inc(pv_done, 1)

                def turn_ml(i):
                    t0, n = BLOCKS[i]
                    bk, bv = ((0, 1), (2, 3), (0, 1))[i]
                    if i == 0:
                        pe.wait_ge(took_act, value("took_act", l, ACT_NO["vm", 3] + 1))
                        pe.wait_ge(masked, value("masked", l, MASKS_THROUGH[-1]))
                    if i == 1:
                        pe.wait_ge(pt_ready, value("pt_ready", l, PT_THROUGH[-1]))
                    if i == 2:
                        pe.wait_ge(km_rows_ready, value("km_rows_ready", l, 1))
                        pe.wait_ge(ml_rows_ready, value("ml_rows_ready", l, 1))
                    for h in range(NH_M):
                        turn(work[bk][0:n, h * P:(h + 1) * P], km_t[:, h, t0:t0 + n], ident)
                    for h in range(NH_M):
                        m = turn(work[bv][0:n, h * P:(h + 1) * P], vm_t[:, h, t0:t0 + n], ident)
                    m.then_inc(ml_turned, 1)

                def turn_a_wt():
                    pe.wait_ge(dw_ready, value("dw_ready", l, 2))
                    pe.wait_ge(att_lo_ready, value("att_lo_ready", l, 3))
                    for i, (t0, n) in enumerate(BLOCKS):
                        for c, row in ((8 * i, a_row), (8 * i + 4, wt_row)):
                            mm(work[4][0:n, c:c + 4], row[:, t0:t0 + n], ident[0:4, 0:4], start=True, stop=True)

                def spread_dw():
                    for h in range(NH_M):
                        m = mm(work[4][:, 32 + 16 * h:48 + 16 * h], con("sel", 4)[:, h * P:(h + 1) * P], cdw_row[:, NP:NP + 2 * NS],
                               start=True, stop=True)
                    m.then_inc(dw_spread, 1)

                def turn_sample_ml():
                    pe.wait_ge(dk_ready, value("dk_ready", l, 2))
                    pe.wait_ge(km_rows_ready, value("km_rows_ready", l, 2))
                    pe.wait_ge(ml_rows_ready, value("ml_rows_ready", l, 2))
                    for h in range(NH_M):
                        turn(work[2][0:NS, h * P:(h + 1) * P], dk_t[:, h, :], ident)
                    for h in range(NH_M):
                        m = turn(work[3][0:NS, h * P:(h + 1) * P], vm_t[:, h, NP:T], ident)
                    m.then_inc(sk_turned, 1)

                def outer(i):
                    h, half = divmod(i, 2)
                    pe.wait_ge(vd_ready, value("vd_ready", l, h + 1))
                    if i == 0:
                        pe.wait_ge(sk_rows_ready, value("sk_rows_ready", l, 2))
                    else:
                        pe.wait_ge(c_new, value("c_new", l, i))
                    mm(work[3][:, 0:512], dk_rows[:, h * P:(h + 1) * P],
                       vd[:, 4 * half:4 * half + 4, :].rearrange("p b v -> p (b v)"), start=True, stop=True).then_inc(outer_done, 1)

                def nums_sample(h):
                    pe.wait_ge(c_new, value("c_new", l, 2 * h + 2))
                    for b in range(NS):
                        m = mm(work[4][:, T + h * NS + b:T + h * NS + b + 1], c_head[h % 2][:, b, :], qm_t[:, h, NP + b:NP + b + 1],
                               start=True, stop=True)
                    m.then_inc(nums_done, 1)

                def score_ml(h):
                    if h == 0:
                        pe.wait_ge(km_rows_ready, value("km_rows_ready", l, 3))
                        pe.wait_ge(ml_rows_ready, value("ml_rows_ready", l, 3))
                    else:
                        pe.wait_ge(ml_p_ready, value("ml_p_ready", l, 2 * h))
                    mm(work[0][:, 0:NP], con("sel", 4)[:, h * P:(h + 1) * P], cdw_row[:, 0:NP], start=True, stop=True)
                    for blk, ns, t0, nt, c in SOURCES:
                        m = mm(work[1][0:ns, c:c + nt], km_t[:, h, blk * P:blk * P + ns], qm_t[:, h, t0:t0 + nt], start=True, stop=True)
                    m.then_inc(ml_scored, 1)

                def nums_prompt(h):
                    pe.wait_ge(ml_p_ready, value("ml_p_ready", l, 2 * h + 2))
                    if h == 0:
                        pe.wait_ge(sk_rows_ready, value("sk_rows_ready", l, 1))
                        pe.wait_ge(dk_ready, value("dk_ready", l, 5))
                    else:
                        pe.wait_ge(c_prompt_ready, value("c_prompt_ready", l, h))
                        pe.wait_ge(n_kept, value("n_kept", l, h))
                    v = [vm_rows[0:ns, blk, h * P:(h + 1) * P] for blk, ns, _, _, _ in SOURCES]
                    k = [km_rows[0:ns, blk, h * P:(h + 1) * P] for blk, ns, _, _, _ in SOURCES]
                    for blk, ns, t0, nt, c in SOURCES:
                        mm(work[2][:, t0:NP], v[blk], decay_d[0:ns, c:c + nt], start=(blk == 0), stop=(blk == 2))
                    for blk, ns, t0, nt, c in SOURCES:
                        mm(work[2][:, NP:NP + P], k[blk], v[blk], start=(blk == 0), stop=(blk == 2), skip_group_check=True)
                    for blk, ns, t0, nt, c in SOURCES:
                        m = mm(work[2][:, NP + P:NP + P + 1], k[blk], ones[0:ns, 0:1], start=(blk == 0), stop=(blk == 2),
                               skip_group_check=True)
                    m.then_inc(num_done, 1)
                    rows = slice(32 * h, 32 * h + 32)
                    for blk, ns, t0, nt, c in SOURCES:
                        mm(work[4][rows, t0:NP], ones[0:ns, 0:32], decay_d[0:ns, c:c + nt], start=(blk == 0), stop=(blk == 2))
                    m = mm(work[4][rows, NP:T], ones[:, 0:32], qn_t[:, h, :], start=True, stop=True)
                    m.then_inc(dots_done, 1)

                def sum_conv():
                    pe.wait_ge(ml_p_ready, value("ml_p_ready", l, 8))
                    pe.wait_ge(conv_added, value("conv_added", l, 3))
                    mm(work[0][:, 0:T], ones[:, 0:P], conv_total[:, 0, :], start=True, stop=True).then_inc(ln_summed, 1)

                def sum_conv_squares():
                    pe.wait_ge(conv_added, value("conv_added", l, 6))
                    mm(work[1][:, 0:T], ones[:, 0:P], conv_total[:, 1, :], start=True, stop=True).then_inc(ln_summed, 1)

                def spread_m():
                    pe.wait_ge(centred, value("centred", l, 4))
                    mm(work[0][:, 0:T], con("sel32", 4), m_row[:, :], start=True, stop=True).then_inc(m_spread, 1)

                def turn_n():
                    pe.wait_ge(n_kept, value("n_kept", l, 4))
                    pe.wait_ge(c_new, value("c_new", l, 8))
                    mm(work[3][0:36, 0:P], n_all, ident, start=True, stop=True).then_inc(n_turned, 1)

                def spread_inverse():
                    pe.wait_ge(dots_inv, value("dots_inv", l, 2))
                    pe.wait_ge(ln_std, value("ln_std", l, 1))
                    pe.wait_ge(num_ready, value("num_ready", l, 4))
                    pe.wait_ge(n_ready, value("n_ready", l, 1))
                    for h in range(NH_M):
                        mm(work[h][:, 0:T], ones[32 * h:32 * h + 1, 0:P], km_t[32 * h:32 * h + 1, 2, :], start=True, stop=True)\
                            .then_inc(inv_spread, 1)

                def turn_gates():
                    pe.wait_ge(last_gate_kept, value("last_gate_kept", l, KF))
                    for half in range(2):
                        m = turn(work[1][0:110, half * P:(half + 1) * P],
                                 last_gates[:, 5 * half:5 * half + 5, :].rearrange("p t c -> p (t c)"), ident)
                    m.then_inc(gates_turned, 1)

                turn_norm()
                for n in range(N_PIECES):
                    if n in SCORES_AT[1:]:
                        pe.wait_ge(masked, value("masked", l, MASKS_THROUGH[SCORES_AT.index(n) - 1]))
                    if n in GROUPS:
                        project([n, n + 1, n + 2])
                    elif n - 1 not in GROUPS and n - 2 not in GROUPS:
                        project([n])
                    if n == N_PIECES - 1:
                        sum_norm(1)
                    if n == 3:
                        turn_vectors()
                    if n == 5:
                        turn_conv_history()
                    if n == 8:
                        turn_new_conv()
                    if n == 9:
                        turn_keys()
                    if n == 14:
                        rotate()
                    if n == 15:
                        move_f()
                    if n == 16:
                        turn_kv()
                        score_sample()
                    if n == 17:
                        turn_sample_scores()
                    if n == 19:
                        turn_sample_probs()
                    if n == 20:
                        values_sample()
                    if n in VALUES_AT:
                        values_unit(VALUES_AT.index(n))
                    if n in TURN_AT:
                        turn_probs(TURN_AT.index(n))
                    if n in SCORES_AT:
                        score_unit(SCORES_AT.index(n))
                    if n == 39:
                        turn_a_wt()
                        spread_dw()
                        turn_ml(0)
                        turn_ml(1)
                    if n == 41:
                        turn_ml(2)
                        turn_sample_ml()
                    if n in NUMS_AT:
                        nums_sample(NUMS_AT.index(n))
                    if n in OUTER_AT:
                        outer(OUTER_AT.index(n))
                    if n - 2 in ML_AT:
                        nums_prompt(ML_AT.index(n - 2))
                    if n in ML_AT:
                        score_ml(ML_AT.index(n))
                    if n == 52:
                        sum_conv()
                    if n == 54:
                        spread_m()
                        sum_conv_squares()
                    if n == 55:
                        turn_n()
                    if n == 58:
                        spread_inverse()
                    if n == STEP["down", 1]:
                        turn_gates()

            for j in range(6):
                half, i = divmod(j, 3)
                t0, n = Y_BLOCKS[i]
                if j >= 4:
                    pe.wait_ge(y_rows_half, j - 3)
                for c in range(4):
                    if i == 0:
                        pe.wait_ge(h_ready, value("h_ready", DEPTH, 4 * half + c + 1))
                    m = turn(work[1 + j % 4][0:n, c * P:(c + 1) * P], h_full[:, 4 * half + c, t0:t0 + n], ident)
                m.then_inc(y_turned, 1)

        def split_views(n, k0, k1):
            ncol = PIECES[n][3]
            s = slice(k0 * ncol, k1 * ncol)
            return w_raw[n % SLOTS][:, s], w_hi[n % SLOTS][:, s], w_lo[n % SLOTS][:, s]

        def tile_ready(eng, l, tile):
            eng.wait_ge(runs_done, value("runs_done", l, LAST_RUN[tile] + 1))

        @block.scalar
        def _(act):
            go = nc.scalar.activation

            def root_mean(w_sum, n, eps, src, dst, signal):
                act.wait_ge(*w_sum)
                go(dst, src, ACT.Sqrt, bias=eps, scale=1.0 / n).then_inc(signal, 1)

            def load_table(function, column):
                go(small[:, column:column + 1], ones[:, 0:1], function)

            act.wait_ge(const_in, 16)
            load_table(ACT.Sqrt, 118)
            for c in range(KD):
                act.wait_ge(took_dve, c + 1)
                go(x_squares[:, c, :], x[:, c, :], ACT.Square).then_inc(x_squared, 1)
            act.dma_start(const[:, 2 * P:CONST_COLS], consts[:, 2 * P:CONST_COLS]).then_inc(tables_in, 16)
            with nc.scalar.Fori(0, DEPTH) as l:
                def split_hi(n):
                    act.wait_ge(raw_in[n % SLOTS], value(f"raw_in{n % SLOTS}", l, RAW_THROUGH[n]))
                    r, h, _ = split_views(n, 0, PIECES[n][2])
                    go(h, r, ACT.Copy).then_inc(w_hi_ready, 1)

                def first_norm():
                    root_mean((squares_summed, value("squares_summed", l, 0)), D_MODEL, RMS_EPS, work[0][:, 0:T], rms[:, :], rms_ready)
                    act.wait_ge(vec_turned, value("vec_turned", l, 1))
                    go(vec[:, 0:KD], work[1][:, 0:KD], ACT.Copy).then_inc(vec_ready, 1)
                    split_hi(2)
                    for c in range(KD):
                        act.wait_ge(h_ready, value("h_ready", l, c + 1))
                        go(h_hi[:, c, :], h_full[:, c, :], ACT.Copy).then_inc(h_hi_ready, 1)

                def second_norm_hi(c):
                    act.wait_ge(h_ready, value("h_ready", l, KD + c + 1))
                    go(xg_hi[:, c, :], h_full[:, c, :], ACT.Copy).then_inc(h_hi_ready, 1)

                def take(tile):
                    kind, t = tile
                    if kind == "gate":
                        act.wait_ge(took_dve, value("took_dve", l, DVE_NO[tile] + 1))
                        if t >= 4:
                            act.wait_ge(act_lo_ready, value("act_lo_ready", l, t - 3))
                        go(last_gates[:, :, t], gate_raw[:, t % 2, T - 10:T], ACT.Copy).then_inc(last_gate_kept, 1)
                        go(gate_buf[:, t % 4, :], gate_raw[:, t % 2, :], ACT.Identity, bias=vcol("b_ffn", t),
                           scale=vcol("w_ffn", 2 * KF + t)).then_inc(gate_first, 1)
                        return
                    if tile not in ACT_NO:
                        return
                    tile_ready(act, l, tile)
                    src = ps_tile[TILE_NO[tile] % 3][:, 0:T]
                    if kind == "glub":
                        o = go(sig_b[:, t, :], src, ACT.Sigmoid)
                    elif kind == "o":
                        o = go(o_sig[:, t, :], src, ACT.Copy)
                    elif kind == "g":
                        o = go(gates[:, t, :], src, ACT.Identity, bias=vcol("b_merge", t))
                    elif kind == "km":
                        o = go(km_t[:, t, :], src, ACT.Copy, scale=DH_M ** -0.5)
                    else:
                        dst = {"ka": ka_t[:, :], "va": va_t[:, :], "qa": qa_t[:, t % R_A, :], "vm": vm_t[:, t % NH_M, :],
                               "qm": qm_t[:, t % NH_M, :]}[kind]
                        o = go(dst, src, ACT.Copy)
                    o.then_inc(took_act, 1)

                def open_gates(view, last):
                    act.wait_ge(took_act, value("took_act", l, ACT_NO[last] + 1))
                    go(view, view, ACT.Sigmoid).then_inc(gates_open, 1)

                def take_vectors():
                    act.wait_ge(vec_turned, value("vec_turned", l, 2))
                    go(vec[:, KD:VEC_COLS], work[1][:, KD:VEC_COLS], ACT.Copy).then_inc(vec_ready, 1)
                    act.wait_ge(vec_turned, value("vec_turned", l, 3))
                    go(ffn_hist[:, :], work[2][:, 0:NS * 2 * KF], ACT.Copy).then_inc(vec_ready, 1)

                def take_history():
                    for half in range(2):
                        act.wait_ge(conv_turned, value("conv_turned", l, half + 1))
                        go(u_hist[:, 4 * half:4 * half + 4, :, :].rearrange("p b t c -> p (b t c)"), work[3 + half][:, 0:480],
                           ACT.Copy).then_inc(hist_ready, 1)

                def take_conv_rows():
                    act.wait_ge(conv_turned, value("conv_turned", l, 3))
                    go(conv_rows[:, :], work[0][0:HIST, :], ACT.Copy)
                    go(conv_rows_s[:, :], work[3][0:NS, :], ACT.Copy).then_inc(hist_ready, 1)

                def take_keys():
                    for half in range(2):
                        act.wait_ge(keys_turned, value("keys_turned", l, half + 1))
                        go(key_t[:, 4 * half:4 * half + 4, :].rearrange("p b k -> p (b k)"), work[1 + half][:, :], ACT.Copy)\
                            .then_inc(keys_ready, 1)

                def take_kv():
                    act.wait_ge(kv_turned, value("kv_turned", l, 1))
                    go(kv_rows[:, 0:2 * P], work[3][:, 0:2 * P], ACT.Copy)
                    go(kv_rows[0:NS, 2 * P:4 * P], work[3][0:NS, 2 * P:4 * P], ACT.Copy).then_inc(kv_ready, 1)
                    act.wait_ge(kv_turned, value("kv_turned", l, 2))
                    go(va_rows[:, 0:2, :].rearrange("p i d -> p (i d)"), work[4][:, 0:2 * P], ACT.Copy)
                    go(va_rows[0:N_META, 2, :], work[4][0:N_META, 2 * P:3 * P], ACT.Copy).then_inc(kv_ready, 1)

                def log_forget():
                    act.wait_ge(f_moved, value("f_moved", l, 1))
                    go(lf_row[:, :], work[0][0:4, 0:T], ACT.Abs).then_inc(log_step, 1)
                    act.wait_ge(log_step, value("log_step", l, 1))
                    go(lf_row[:, :], lf_row[:, :], ACT.Exp, scale=-1.0).then_inc(log_step, 1)
                    act.wait_ge(log_step, value("log_step", l, 2))
                    go(lf_row[:, :], lf_row[:, :], ACT.Ln, bias=1.0).then_inc(log_step, 1)
                    load_table(ACT.Exp, 118)

                def weights_ml():
                    act.wait_ge(row_step, value("row_step", l, 10))
                    go(cdw_row[:, NP:NP + 2 * NS], cdw_row[:, NP:NP + 2 * NS], ACT.Exp).then_inc(dw_ready, 1)
                    go(wt_row[:, :], a_row[:, :], ACT.Exp, bias=cm_last).then_inc(dw_ready, 1)

                def take_sample_scores():
                    act.wait_ge(s_scored, value("s_scored", l, 1))
                    go(s_keys[:, 0:32], work[1][:, P:P + 32], ACT.Copy)
                    go(s_keys[:, 32:64], work[2][:, P:P + 32], ACT.Copy).then_inc(s_keys_ready, 1)

                def exp_sample():
                    act.wait_ge(s_max, value("s_max", l, 6))
                    go(s_rows[:, 0:WINDOW + 1], s_rows[:, 0:WINDOW + 1], ACT.Exp, bias=samp_small[:, 1:2],
                       accum_out=samp_small[:, 2:3]).then_inc(s_exp, 1)
                    go(samp_small[:, 3:4], sink_s, ACT.Exp, bias=samp_small[:, 1:2]).then_inc(s_exp, 1)

                def take_sample_probs():
                    act.wait_ge(s_turned, value("s_turned", l, 2))
                    go(p_keys[:, :], work[1][:, P:P + 64], ACT.Copy).then_inc(s_p_ready, 1)

                def sample_att_hi():
                    act.wait_ge(s_out, value("s_out", l, 2))
                    go(att_hi[:, :, NP:T], att_s[:, :, :], ACT.Copy).then_inc(att_hi_ready, 1)

                def exp_unit(u):
                    blk, g, q0, nq, k0, nk, _ = units_of(u)
                    sm = unit_small[u % 2]
                    act.wait_ge(unit_max, value("unit_max", l, 4 * u + 4))
                    if u >= 2:
                        act.wait_ge(unit_p, value("unit_p", l, 3 * u - 5))
                    for j in range(R_A):
                        s = scores[0:nq, u % 2, j * nk:(j + 1) * nk]
                        go(s, s, ACT.Exp, bias=sm[0:nq, 4 + j:5 + j], accum_out=sm[0:nq, 8 + j:9 + j]).then_inc(unit_exp, 1)
                    go(sm[0:nq, 12:16], sm[0:nq, 12:16], ACT.Exp).then_inc(unit_exp, 1)

                def take_probs(u):
                    blk, g, q0, nq, k0, nk, _ = units_of(u)
                    act.wait_ge(probs_turned, value("probs_turned", l, u + 1))
                    if u == 0:
                        act.wait_ge(kv_stored, value("kv_stored", l, 16 * 4))
                    if u >= 2:
                        act.wait_ge(pv_done, value("pv_done", l, u - 1))
                    for i, (c, n) in enumerate(key_chunks(nk)):
                        go(probs_t[0:n, u % 2, i * 512:i * 512 + R_A * nq], work[2 + i][0:n, 0:R_A * nq], ACT.Copy).then_inc(pt_ready, 1)

                def block_att_hi(blk):
                    q0, nq = BLOCKS[blk]
                    act.wait_ge(pv_done, value("pv_done", l, 2 * blk + 2))
                    go(att_hi[:, :, q0:q0 + nq], work[4][:, 0:R_A * nq].rearrange("p (j q) -> p j q", j=R_A), ACT.Copy)\
                        .then_inc(att_hi_ready, 1)

                def take_ml_rows(i):
                    n = BLOCKS[i][1]
                    act.wait_ge(ml_turned, value("ml_turned", l, i + 1))
                    go(vm_rows[0:n, i, :], work[(1, 3, 1)[i]][0:n, :], ACT.Copy).then_inc(ml_rows_ready, 1)

                def take_sample_ml():
                    act.wait_ge(sk_turned, value("sk_turned", l, 1))
                    go(dk_rows[:, :], work[2][0:NS, :], ACT.Copy).then_inc(sk_rows_ready, 1)
                    go(v_rows_s[:, :], work[3][0:NS, :], ACT.Copy).then_inc(sk_rows_ready, 1)

                def exp_decay(h):
                    act.wait_ge(decay_arg, value("decay_arg", l, 3 * h + 3))
                    go(decay_d[:, 0:416], decay_d[:, 0:416], ACT.Exp, scale=-1.0).then_inc(decay_ready, 1)
                    go(decay_d[0:N_META, 416:432], decay_d[0:N_META, 416:432], ACT.Exp, scale=-1.0).then_inc(decay_ready, 1)

                def take_nums(h):
                    act.wait_ge(num_done, value("num_done", l, h + 1))
                    go(num_all[:, h, 0:NP], work[2][:, 0:NP], ACT.Copy).then_inc(num_ready, 1)
                    go(c_prompt[:, h, :], work[2][:, NP:NP + P], ACT.Copy).then_inc(c_prompt_ready, 1)
                    go(n_all[:, 32 + h:33 + h], work[2][:, NP + P:NP + P + 1], ACT.Copy).then_inc(n_kept, 1)

                def square_conv():
                    act.wait_ge(centred, value("centred", l, 4))
                    go(conv_sq[:, :, :], uc[:, :, :], ACT.Square).then_inc(ln_sq, 1)

                def silu_conv():
                    for c in range(KC):
                        act.wait_ge(ln_inv, value("ln_inv", l, c + 2))
                        go(uc[:, c, :], uc[:, c, :], ACT.Silu, bias=vcol("ln_b", c)).then_inc(conv_silu, 1)
                    for c in range(KC):
                        act.wait_ge(conv_silu, value("conv_silu", l, c + 1))
                        go(conv_hi[:, c, :], uc[:, c, :], ACT.Copy).then_inc(conv_hi_ready, 1)

                def sample_nums():
                    act.wait_ge(nums_done, value("nums_done", l, 4))
                    go(num_all[:, :, NP:T], work[4][:, T:T + 32].rearrange("p (h b) -> p h b", h=NH_M), ACT.Copy).then_inc(num_ready, 1)

                def denominators():
                    act.wait_ge(m_spread, value("m_spread", l, 1))
                    go(km_t[:, 0, :], work[0][:, 0:T], ACT.Exp, scale=-1.0).then_inc(inv_m, 1)
                    act.wait_ge(dots_done, value("dots_done", l, 4))
                    go(km_t[:, 1, :], work[4][:, 0:T], ACT.Abs).then_inc(inv_m, 1)

                def take_n():
                    act.wait_ge(n_turned, value("n_turned", l, 1))
                    go(n_rows[:, :], work[3][0:36, 0:P], ACT.Copy).then_inc(n_ready, 1)

                def ml_his():
                    for h in range(NH_M):
                        act.wait_ge(hm_ready, value("hm_ready", l, h + 1))
                        go(ml_hi[:, h, :], num_all[:, h, :], ACT.Copy).then_inc(ml_hi_ready, 1)

                def merged_his(n):
                    for kind, t in PIECES[n][4]:
                        act.wait_ge(merged_ready, value("merged_ready", l, KD + t + 1))
                        go(h_hi[:, t, :], merged[:, t, :], ACT.Copy).then_inc(merged_hi_ready, 1)

                def silus(n):
                    for _, t in PIECES[n][4]:
                        act.wait_ge(gate_conv, value("gate_conv", l, 4 * t + 4))
                        go(gate_buf[:, t % 4, :], gate_buf[:, t % 4, :], ACT.Silu).then_inc(gate_silu, 1)

                def act_his(n):
                    for _, t in PIECES[n][4]:
                        act.wait_ge(took_dve, value("took_dve", l, DVE_NO["up", t] + 1))
                        go(act_hi[:, t, :], gate_buf[:, t % 4, :], ACT.Copy).then_inc(act_hi_ready, 1)

                def take_gate_rows():
                    act.wait_ge(gates_turned, value("gates_turned", l, 1))
                    go(gate_rows[:, :, :].rearrange("p i c -> p (i c)"), work[1][0:110, 0:2 * P], ACT.Copy).then_inc(gate_rows_ready, 1)

                load_table(ACT.Sqrt, 119)
                split_hi(0)
                split_hi(1)
                first_norm()
                split_hi(3)
                for n in range(N_PIECES):
                    if n == STEP["out", 1]:
                        load_table(ACT.Sqrt, 19)
                    if n == STEP["gate", 0]:
                        root_mean((squares_summed, value("squares_summed", l, 2)), D_MODEL, RMS_EPS, work[0][:, 0:T], ffn_rms[:, :],
                                  rms_ready)
                        load_table(ACT.Silu, 119)
                    for tile in PIECES[n][4]:
                        if LAST_RUN[tile] < RUNS_THROUGH[n]:
                            take(tile)
                    if n + AHEAD < N_PIECES:
                        split_hi(n + AHEAD)
                    if PIECES[n][0] == "out":
                        second_norm_hi(PIECES[n][1])
                    kind = PIECES[n][0]
                    if n == 4:
                        take_vectors()
                    if n == 6:
                        take_history()
                    if n == 9:
                        take_conv_rows()
                    if n == 10:
                        take_keys()
                    if n == 16:
                        log_forget()
                        take_sample_scores()
                        take_kv()
                    if n == 18:
                        exp_sample()
                    if n == 19:
                        take_sample_probs()
                    if n == 21:
                        weights_ml()
                        sample_att_hi()
                    if n - 1 in SCORES_AT:
                        exp_unit(SCORES_AT.index(n - 1))
                    if n in TURN_AT:
                        take_probs(TURN_AT.index(n))
                    if n - 1 in VALUES_AT[1::2]:
                        block_att_hi(VALUES_AT.index(n - 1) // 2)
                    if n == 40:
                        take_ml_rows(0)
                        take_ml_rows(1)
                    if n == 42:
                        take_ml_rows(2)
                        take_sample_ml()
                    if n - 1 in ML_AT:
                        exp_decay(ML_AT.index(n - 1))
                    if n - 3 in ML_AT:
                        take_nums(ML_AT.index(n - 3))
                    if n == 52:
                        open_gates(o_sig[:, :, :], ("o", NH_M - 1))
                        square_conv()
                    if n == 53:
                        open_gates(gates[:, 0:2 * KD, :], ("g", 2 * KD - 1))
                    if n == 54:
                        open_gates(gates[:, 2 * KD:3 * KD, :], ("g", 3 * KD - 1))
                    if n == 55:
                        root_mean((ln_summed, value("ln_summed", l, 2)), C_CONV, LN_EPS, work[1][:, 0:T], conv_std[:, 0, :], ln_std)
                    if n == 56:
                        sample_nums()
                        denominators()
                        take_n()
                    if n == 57:
                        silu_conv()
                    if n == 60:
                        ml_his()
                    if kind == "ya":
                        merged_his(n)
                    if kind == "gate":
                        silus(n)
                    if kind == "up":
                        act_his(n)
                    if n == STEP["down", 1]:
                        take_gate_rows()

            root_mean((squares_summed, value("squares_summed", DEPTH, 0)), D_MODEL, RMS_EPS, work[0][:, 0:T], rms[:, :], rms_ready)
            for j in range(6):
                half, i = divmod(j, 3)
                n = Y_BLOCKS[i][1]
                act.wait_ge(y_turned, j + 1)
                o = go(y_rows[0:n, i, half * 512:(half + 1) * 512], work[1 + j % 4][0:n, :], ACT.Copy)
                o.then_inc(y_rows_half, 1)

        @block.gpsimd
        def _(pool):
            tt = nc.gpsimd.tensor_tensor
            for i in range(SLOTS):
                pool.memset(small[:, 120 + i:121 + i], 0.0).then_inc(runs_done, 1)
            for i in range(2):
                pool.memset(small[:, 126 + i:127 + i], 0.0).then_inc(vec_turned, 1)
            with nc.gpsimd.Fori(0, DEPTH) as l:
                def split_lo(n):
                    nk, ncol = PIECES[n][2], PIECES[n][3]
                    if dve_share(n) < nk:
                        pool.wait_ge(w_hi_ready, value("w_hi_ready", l, n + 1))
                        r, h, lo = split_views(n, dve_share(n), nk)
                        tt(lo, r, h.bitcast(F32), ALU.subtract).then_inc(w_split[n % SLOTS], 1)

                def scale_gate(t):
                    if t == 0:
                        pool.wait_ge(rms_inv_ready, value("rms_inv_ready", l, 2))
                    pool.wait_ge(gate_silu, value("gate_silu", l, t + 1))
                    tt(gate_buf[:, t % 4, :], gate_buf[:, t % 4, :], ffn_rms_inv[:, :], ALU.mult).then_inc(gate_scaled, 1)

                def total(src, name, signal, k):
                    dst = conv_total[:, k, :]
                    tt(dst, src[:, 0, :], src[:, 1, :], ALU.add).then_inc(signal, 1)
                    for c in (2, 3):
                        pool.wait_ge(signal, value(name, l, 3 * k + c - 1))
                        tt(dst, dst, src[:, c, :], ALU.add).then_inc(signal, 1)

                def total_conv():
                    pool.wait_ge(tap_done, value("tap_done", l, KC * CONV_W))
                    pool.wait_ge(hist_sum, value("hist_sum", l, 5))
                    total(uc, "conv_added", conv_added, 0)

                def total_conv_squares():
                    pool.wait_ge(ln_sq, value("ln_sq", l, 1))
                    total(conv_sq, "conv_added", conv_added, 1)

                def rope_cosine():
                    pool.wait_ge(tables_in, 16)
                    for i in range(5):
                        q = qa_t[:, i, :] if i < R_A else ka_t[:, :]
                        pool.wait_ge(rotated, value("rotated", l, i + 1))
                        tt(q, q, con("cos"), ALU.mult).then_inc(rope_cos, 1)

                def scale_c(h):
                    pool.wait_ge(c_in[h % 2], value(f"c_in{h % 2}", l, 16 * (h // 2 + 1)))
                    pool.wait_ge(dk_ready, value("dk_ready", l, 1))
                    c = c_head[h % 2][:, :, :]
                    tt(c, c, dw_b[:, h, NS:2 * NS].unsqueeze(2).to_broadcast([P, NS, P]), ALU.mult).then_inc(c_scaled, 1)

                def spread_v(h):
                    if h == 0:
                        pool.wait_ge(sk_rows_ready, value("sk_rows_ready", l, 2))
                    else:
                        pool.wait_ge(outer_done, value("outer_done", l, 2 * h))
                    tt(vd[:, :, :], v_rows_s[:, h * P:(h + 1) * P].unsqueeze(1).to_broadcast([NS, NS, P]),
                       ident[0:NS, 0:NS].unsqueeze(2).to_broadcast([NS, NS, P]), ALU.mult).then_inc(vd_ready, 1)

                def gate_nums():
                    pool.wait_ge(num_ready, value("num_ready", l, 5))
                    pool.wait_ge(gates_open, value("gates_open", l, 1))
                    for h in range(NH_M):
                        tt(num_all[:, h, :], num_all[:, h, :], o_sig[:, h, :], ALU.mult).then_inc(num_gated, 1)

                for n in range(AHEAD):
                    split_lo(n)
                for n in range(N_PIECES):
                    if PIECES[n][0] == "up":
                        scale_gate(PIECES[n][1])
                    if n + AHEAD < N_PIECES:
                        split_lo(n + AHEAD)
                    if n == 14:
                        rope_cosine()
                    if n == 51:
                        total_conv()
                    if n == 53:
                        total_conv_squares()
                    if n + 2 in OUTER_AT[0::2]:
                        scale_c(OUTER_AT.index(n + 2) // 2)
                        spread_v(OUTER_AT.index(n + 2) // 2)
                    if n == 57:
                        gate_nums()

        @block.vector
        def _(dve):
            tt, ts, stt = nc.vector.tensor_tensor, nc.vector.tensor_scalar, nc.vector.scalar_tensor_tensor
            dve.wait_ge(const_in, 16)
            for c in range(KD):
                dve.wait_ge(x_turned, c + 1)
                dve.tensor_copy(x[:, c, :], work[c % 4][:, 0:T]).then_inc(took_dve, 1)

            def square(c, l, k):
                done = SQ_STEPS * (k - 1)
                dst = squares[:, 1 if c == 0 else 0, :]
                if c == 0:
                    dve.wait_ge(squares_summed, value("squares_summed", l, 2 * k - 2))
                elif c >= 2:
                    dve.wait_ge(squared, value("squared", l, done + 2 * c - 1))
                tt(dst, x[:, c, :], x[:, c, :], ALU.mult).then_inc(squared, 1)
                if 0 < c < KD - 1:
                    dve.wait_ge(squared, value("squared", l, done + 2 * c))
                    tt(squares[:, 1, :], squares[:, 1, :], squares[:, 0, :], ALU.add).then_inc(squared, 1)

            def inverse_root(w, root, inverse):
                dve.wait_ge(rms_ready, w)
                dve.reciprocal(inverse[:, :], root[:, :]).then_inc(rms_inv_ready, 1)

            with nc.vector.Fori(0, DEPTH) as l:
                def split_lo(n):
                    nk, ncol = PIECES[n][2], PIECES[n][3]
                    dve.wait_ge(w_hi_ready, value("w_hi_ready", l, n + 1))
                    r, h, lo = split_views(n, 0, dve_share(n))
                    tt(lo, r, h.bitcast(F32), ALU.subtract).then_inc(w_split[n % SLOTS], 1)

                def first_norm():
                    inverse_root(value("rms_ready", l, 1), rms, rms_inv)
                    split_lo(2)
                    dve.wait_ge(rms_inv_ready, value("rms_inv_ready", l, 1))
                    dve.wait_ge(vec_ready, value("vec_ready", l, 1))

                    def lo(c):
                        dve.wait_ge(h_hi_ready, value("h_hi_ready", l, c + 1))
                        tt(h_lo[:, c, :], h_full[:, c, :], h_hi[:, c, :].bitcast(F32), ALU.subtract).then_inc(h_lo_ready, 1)

                    for c in range(KD):
                        stt(h_full[:, c, :], x[:, c, :], vcol("norm1", c), rms_inv[:, :], ALU.mult, ALU.mult).then_inc(h_ready, 1)
                        if c >= 1:
                            lo(c - 1)
                    lo(KD - 1)

                def second_norm_lo(c):
                    if c == 0:
                        dve.wait_ge(c_stored[0], value("c_stored0", l, 32))
                        dve.wait_ge(c_stored[1], value("c_stored1", l, 32))
                    dve.wait_ge(h_hi_ready, value("h_hi_ready", l, KD + c + 1))
                    tt(xg_lo[:, c, :], h_full[:, c, :], xg_hi[:, c, :].bitcast(F32), ALU.subtract).then_inc(h_lo_ready, 1)

                def take(tile):
                    kind, t = tile
                    if tile not in DVE_NO:
                        return
                    bank = ps_tile[TILE_NO[tile] % 3]
                    src = bank[:, 0:T]
                    tile_ready(dve, l, tile)
                    if kind == "glua":
                        dve.wait_ge(took_act, value("took_act", l, ACT_NO["glub", t] + 1))
                        tt(u_pad[:, t, HIST:HIST + NP], src[:, 0:NP], sig_b[:, t, 0:NP], ALU.mult)
                        o = tt(u_new[:, t, :], src[:, NP:T], sig_b[:, t, NP:T], ALU.mult)
                    elif kind == "if":
                        dve.wait_ge(tiny_in, value("tiny_in", l, 16 * 5))
                        o = ts(if_rows[:, :], bank[0:8, 0:T], bias_if, None, ALU.add)
                    elif kind == "yc":
                        if t == 0:
                            dve.wait_ge(gates_open, value("gates_open", l, 3))
                        o = tt(merged[:, t, :], src, gates[:, 2 * KD + t, :], ALU.mult)
                    elif kind in ("yb", "ya"):
                        u = t if kind == "yb" else KD + t
                        if u >= 2:
                            dve.wait_ge(merged_ready, value("merged_ready", l, u - 1))
                        else:
                            dve.wait_ge(took_dve, value("took_dve", l, DVE_NO["yc", KD - 1] + 1))
                        o = tt(prod[:, t % 2, :], src, gates[:, (KD if kind == "yb" else 0) + t, :], ALU.mult)
                    elif kind in ("out", "down"):
                        tt(x[:, t, :], x[:, t, :], src, ALU.add).then_inc(took_dve, 1)
                        dve.wait_ge(took_dve, value("took_dve", l, DVE_NO[tile] + 1))
                        if kind == "out":
                            ts(h_full[:, t, :], x[:, t, :], vcol("norm2", t), None, ALU.mult).then_inc(h_ready, 1)
                            if t >= 1:
                                second_norm_lo(t - 1)
                        square(t, l, 1 if kind == "out" else 2)
                        return
                    elif kind == "gate":
                        buf = gate_buf[:, t % 4, :]
                        hist = ffn_hist[:, :].rearrange("p (b w c) -> p b w c", b=NS, w=2)
                        raw_gate = gate_raw[:, t % 2, :]
                        if t >= 2:
                            dve.wait_ge(gate_conv, value("gate_conv", l, 4 * t - 4))
                        tt(raw_gate, src, ffn_rms_inv[:, :], ALU.mult).then_inc(took_dve, 1)
                        dve.wait_ge(gate_first, value("gate_first", l, t + 1))
                        stt(buf[:, NP:T], hist[:, :, 0, t], vcol("w_ffn", t), buf[:, NP:T], ALU.mult, ALU.add).then_inc(gate_conv, 1)
                        stt(buf[:, 1:NP], raw_gate[:, 0:NP - 1], vcol("w_ffn", KF + t), buf[:, 1:NP], ALU.mult, ALU.add).then_inc(gate_conv, 1)
                        dve.wait_ge(gate_conv, value("gate_conv", l, 4 * t + 1))
                        stt(buf[:, NP:T], hist[:, :, 1, t], vcol("w_ffn", KF + t), buf[:, NP:T], ALU.mult, ALU.add).then_inc(gate_conv, 1)
                        dve.wait_ge(gate_conv, value("gate_conv", l, 4 * t + 2))
                        stt(buf[:, 2:NP], raw_gate[:, 0:NP - 2], vcol("w_ffn", t), buf[:, 2:NP], ALU.mult, ALU.add).then_inc(gate_conv, 1)
                        return
                    elif kind == "up":
                        dve.wait_ge(gate_scaled, value("gate_scaled", l, t + 1))
                        o = tt(gate_buf[:, t % 4, :], gate_buf[:, t % 4, :], src, ALU.mult)
                    o.then_inc(took_dve, 1)
                    if kind in ("yb", "ya"):
                        dve.wait_ge(took_dve, value("took_dve", l, DVE_NO[tile] + 1))
                        tt(merged[:, t, :], merged[:, t, :], prod[:, t % 2, :], ALU.add).then_inc(merged_ready, 1)

                def taps(first, count):
                    for i in range(first, min(first + count, KC * CONV_W)):
                        tap, c = divmod(i, KC)
                        w, dst, src = vcol("w_dconv", i), uc[:, c, 0:NP], u_pad[:, c, tap:tap + NP]
                        if tap == 0:
                            if c == 0:
                                dve.wait_ge(took_dve, value("took_dve", l, DVE_NO["glua", KC - 1] + 1))
                                dve.wait_ge(pad_zero, value("pad_zero", l, 1))
                                dve.wait_ge(vec_ready, value("vec_ready", l, 2))
                            ts(dst, src, w, vcol("b_dconv", c), ALU.mult, ALU.add).then_inc(tap_done, 1)
                        else:
                            dve.wait_ge(tap_done, value("tap_done", l, i - KC + 1))
                            stt(dst, src, w, dst, ALU.mult, ALU.add).then_inc(tap_done, 1)

                def conv_sample():
                    flat = u_hist[:, :, :, :].rearrange("p b t c -> p b (t c)")
                    dst = uc[:, :, NP:T]
                    dve.wait_ge(hist_ready, value("hist_ready", l, 3))
                    tt(flat, flat, vcol("w_dconv", 0, 120).unsqueeze(1).to_broadcast([P, NS, 120]), ALU.mult).then_inc(hist_sum, 1)
                    tt(u_new[:, :, :], u_new[:, :, :], vcol("w_dconv", 120, 4).unsqueeze(2).to_broadcast([P, KC, NS]), ALU.mult)\
                        .then_inc(hist_sum, 1)
                    for c in range(KC):
                        if c == 0:
                            dve.wait_ge(hist_sum, value("hist_sum", l, 1))
                        o = nc.vector.tensor_reduce(uc[:, c, NP:T], u_hist[:, :, :, c], AX.X, ALU.add)
                    o.then_inc(hist_sum, 1)
                    dve.wait_ge(hist_sum, value("hist_sum", l, 3))
                    tt(dst, dst, u_new[:, :, :], ALU.add).then_inc(hist_sum, 1)
                    dve.wait_ge(hist_sum, value("hist_sum", l, 4))
                    tt(dst, dst, vcol("b_dconv", 0, 4).unsqueeze(2).to_broadcast([P, KC, NS]), ALU.add).then_inc(hist_sum, 1)

                def rope():
                    dve.wait_ge(tables_in, 16)
                    for i, bank in enumerate((0, 3, 4, 1, 2)):
                        q = qa_t[:, i, :] if i < R_A else ka_t[:, :]
                        tmp = probs_t[:, 1, (i % 2) * T:(i % 2 + 1) * T]
                        dve.wait_ge(rotated, value("rotated", l, i + 1))
                        if i >= 2:
                            dve.wait_ge(roped, value("roped", l, i - 1))
                        tt(tmp, work[bank][:, 0:T], con("sin"), ALU.mult).then_inc(rope_sin, 1)
                        dve.wait_ge(rope_sin, value("rope_sin", l, i + 1))
                        dve.wait_ge(rope_cos, value("rope_cos", l, i + 1))
                        tt(q, q, tmp, ALU.add).then_inc(roped, 1)

                def self_products():
                    dve.wait_ge(roped, value("roped", l, 5))
                    tt(qk_self[:, :, :], qa_t[:, :, NP:T], ka_t[:, NP:T].unsqueeze(1).to_broadcast([P, R_A, NS]), ALU.mult)\
                        .then_inc(qk_ready, 1)

                def row_stage():
                    steps = [0]

                    def step(ins, wait=True):
                        steps[0] += 1
                        ins.then_inc(row_step, 1)
                        if wait:
                            dve.wait_ge(row_step, value("row_step", l, steps[0]))

                    one = con("ones", 4)
                    cm, d, w = cdw_row[:, 0:NP], cdw_row[:, NP:NP + NS], cdw_row[:, NP + NS:NP + 2 * NS]
                    ig = if_rows[0:4, :]
                    dve.wait_ge(log_step, value("log_step", l, 3))
                    step(stt(lf_row[:, :], work[0][0:4, 0:T], 0.0, lf_row[:, :], ALU.min, ALU.subtract))
                    step(nc.vector.tensor_tensor_scan(b_row[:, :], one, lf_row[:, 0:NP], 0.0, ALU.mult, ALU.add))
                    step(tt(a_row[:, :], ig[:, 0:NP], b_row[:, :], ALU.subtract))
                    step(nc.vector.tensor_tensor_scan(cm, one, a_row[:, :], 0.0, ALU.mult, ALU.max))
                    step(tt(m_row[:, 0:NP], b_row[:, :], cm, ALU.add), wait=False)
                    step(ts(cm_last, cm[:, NP - 1:NP], -1.0, None, ALU.mult), wait=False)
                    step(tt(w, lf_row[:, NP:T], m_old, ALU.add))
                    step(tt(m_row[:, NP:T], w, ig[:, NP:T], ALU.max))
                    step(tt(d, ig[:, NP:T], m_row[:, NP:T], ALU.subtract), wait=False)
                    step(tt(w, w, m_row[:, NP:T], ALU.subtract))

                def softmax_sample_1():
                    sm = samp_small
                    dve.wait_ge(s_turned, value("s_turned", l, 1))
                    ts(s_rows[:, 0:P], work[2][0:64, 0:P], DH_A ** -0.5, None, ALU.mult).then_inc(s_max, 1)
                    for g in range(KV_A):
                        r = slice(32 * g, 32 * g + 32)
                        ts(s_rows[r, P:P + 1], work[1 + g][r, P + 32:P + 33], DH_A ** -0.5, None, ALU.mult).then_inc(s_max, 1)
                    dve.wait_ge(s_max, value("s_max", l, 3))
                    nc.vector.tensor_reduce(sm[:, 0:1], s_rows[:, 0:P + 1], AX.X, ALU.max).then_inc(s_max, 1)
                    dve.wait_ge(s_max, value("s_max", l, 4))
                    tt(sm[:, 0:1], sm[:, 0:1], sink_s, ALU.max).then_inc(s_max, 1)
                    dve.wait_ge(s_max, value("s_max", l, 5))
                    ts(sm[:, 1:2], sm[:, 0:1], -1.0, None, ALU.mult).then_inc(s_max, 1)

                def softmax_sample_2():
                    sm = samp_small
                    dve.wait_ge(s_exp, value("s_exp", l, 2))
                    tt(sm[:, 4:5], sm[:, 2:3], sm[:, 3:4], ALU.add).then_inc(s_max, 1)
                    dve.wait_ge(s_max, value("s_max", l, 7))
                    dve.reciprocal(sm[:, 5:6], sm[:, 4:5]).then_inc(s_max, 1)
                    dve.wait_ge(s_max, value("s_max", l, 8))
                    ts(s_rows[:, 0:P + 1], s_rows[:, 0:P + 1], sm[:, 5:6], None, ALU.mult).then_inc(s_max, 1)
                    dve.wait_ge(s_max, value("s_max", l, 9))
                    ts(p_self[:, :], con("eye32", 64), s_rows[:, P:P + 1], None, ALU.mult).then_inc(s_self, 1)

                def output_sample():
                    dve.wait_ge(s_pv_done, value("s_pv_done", l, 1))
                    tt(att_s[:, :, :], work[1][:, P + 64:P + 96].rearrange("p (j b) -> p j b", j=R_A),
                       va_t[:, NP:T].unsqueeze(1).to_broadcast([P, R_A, NS]), ALU.mult).then_inc(s_out, 1)
                    dve.wait_ge(s_out, value("s_out", l, 1))
                    tt(att_s[:, :, :], att_s[:, :, :], work[2][:, 2 * P:2 * P + 32].rearrange("p (j b) -> p j b", j=R_A), ALU.add)\
                        .then_inc(s_out, 1)

                def sample_att_lo():
                    dve.wait_ge(att_hi_ready, value("att_hi_ready", l, 1))
                    tt(att_lo[:, :, NP:T], att_s[:, :, :], att_hi[:, :, NP:T].bitcast(F32), ALU.subtract).then_inc(s_lo, 1)

                def softmax_unit_1(u):
                    blk, g, q0, nq, k0, nk, per_bank = units_of(u)
                    sm = unit_small[u % 2]
                    dve.wait_ge(scored, value("scored", l, u + 1))
                    if u == 0:
                        dve.wait_ge(conv_stored, value("conv_stored", l, 32))
                        dve.wait_ge(tiny_in, value("tiny_in", l, 16 * 5))
                    if u >= 2:
                        dve.wait_ge(probs_turned, value("probs_turned", l, u - 1))
                    mask = con("amask", nq)[:, P:2 * P] if blk == 0 else con("amask", nq)[:, 0:nk]
                    for bank in range(R_A // per_bank):
                        c = bank * per_bank * nk
                        stt(scores[0:nq, u % 2, c:c + per_bank * nk].rearrange("p (j k) -> p j k", j=per_bank),
                            work[bank][0:nq, 0:per_bank * nk].rearrange("p (j k) -> p j k", j=per_bank), DH_A ** -0.5,
                            mask.unsqueeze(1).to_broadcast([nq, per_bank, nk]), ALU.mult, ALU.add).then_inc(masked, 1)
                    dve.wait_ge(masked, value("masked", l, MASKS_THROUGH[u]))
                    nc.vector.tensor_reduce(sm[0:nq, 0:4], scores[0:nq, u % 2, 0:R_A * nk].rearrange("p (j k) -> p j k", j=R_A),
                                            AX.X, ALU.max).then_inc(unit_max, 1)
                    sink = sink_b[0:nq, g * R_A:(g + 1) * R_A]
                    dve.wait_ge(unit_max, value("unit_max", l, 4 * u + 1))
                    tt(sm[0:nq, 0:4], sm[0:nq, 0:4], sink, ALU.max).then_inc(unit_max, 1)
                    dve.wait_ge(unit_max, value("unit_max", l, 4 * u + 2))
                    ts(sm[0:nq, 4:8], sm[0:nq, 0:4], -1.0, None, ALU.mult).then_inc(unit_max, 1)
                    tt(sm[0:nq, 12:16], sink, sm[0:nq, 0:4], ALU.subtract).then_inc(unit_max, 1)

                def softmax_unit_2(u):
                    blk, g, q0, nq, k0, nk, per_bank = units_of(u)
                    sm = unit_small[u % 2]
                    dve.wait_ge(unit_exp, value("unit_exp", l, 5 * u + 5))
                    tt(sm[0:nq, 8:12], sm[0:nq, 8:12], sm[0:nq, 12:16], ALU.add).then_inc(unit_p, 1)
                    dve.wait_ge(unit_p, value("unit_p", l, 3 * u + 1))
                    dve.reciprocal(sm[0:nq, 8:12], sm[0:nq, 8:12]).then_inc(unit_p, 1)
                    dve.wait_ge(unit_p, value("unit_p", l, 3 * u + 2))
                    s = scores[0:nq, u % 2, 0:R_A * nk].rearrange("p (j k) -> p j k", j=R_A)
                    tt(s, s, sm[0:nq, 8:12].unsqueeze(2).to_broadcast([nq, R_A, nk]), ALU.mult).then_inc(unit_p, 1)

                def block_att_lo(blk):
                    q0, nq = BLOCKS[blk]
                    dve.wait_ge(att_hi_ready, value("att_hi_ready", l, blk + 2))
                    tt(att_lo[:, :, q0:q0 + nq], work[4][:, 0:R_A * nq].rearrange("p (j q) -> p j q", j=R_A),
                       att_hi[:, :, q0:q0 + nq].bitcast(F32), ALU.subtract).then_inc(att_lo_ready, 1)

                def take_a_wt():
                    dve.wait_ge(dw_spread, value("dw_spread", l, 1))
                    dve.tensor_copy(small[:, 56:72], work[4][:, 0:16]).then_inc(a_wt_ready, 1)
                    dve.tensor_copy(small[0:N_META, 72:80], work[4][0:N_META, 16:24]).then_inc(a_wt_ready, 1)

                def km_weighted(i):
                    n = BLOCKS[i][1]
                    dve.wait_ge(ml_turned, value("ml_turned", l, i + 1))
                    dve.wait_ge(a_wt_ready, value("a_wt_ready", l, 2))
                    tt(km_rows[0:n, i, :].rearrange("p (h d) -> p h d", h=NH_M),
                       work[(0, 2, 0)[i]][0:n, :].rearrange("p (h d) -> p h d", h=NH_M),
                       a_wt[0:n, i, 4:8].unsqueeze(2).to_broadcast([n, NH_M, P]), ALU.mult).then_inc(km_rows_ready, 1)

                def sample_dk():
                    dve.tensor_copy(dw_b[:, :, :].rearrange("p h c -> p (h c)"), work[4][:, 32:96]).then_inc(dk_ready, 1)
                    dve.wait_ge(dk_ready, value("dk_ready", l, 1))
                    tt(dk_t[:, :, :], km_t[:, :, NP:T], dw_b[:, :, 0:NS], ALU.mult).then_inc(dk_ready, 1)
                    n_new = n_all[:, 0:32].rearrange("p (b h) -> p h b", h=NH_M)
                    n_old = vcol("state_n", 0, 32).rearrange("p (b h) -> p h b", h=NH_M)
                    tt(n_new, n_old, dw_b[:, :, NS:2 * NS], ALU.mult).then_inc(dk_ready, 1)
                    dve.wait_ge(dk_ready, value("dk_ready", l, 3))
                    tt(n_new, n_new, dk_t[:, :, :], ALU.add).then_inc(dk_ready, 1)
                    dve.wait_ge(dk_ready, value("dk_ready", l, 4))
                    tt(qn_t[:, :, :], qm_t[:, :, NP:T], n_new, ALU.mult).then_inc(dk_ready, 1)

                def decay_args(h):
                    dve.wait_ge(ml_scored, value("ml_scored", l, h + 1))
                    if h >= 1:
                        dve.wait_ge(dots_done, value("dots_done", l, h))
                    for blk, ns, t0, nt, c in SOURCES:
                        stt(decay_d[0:ns, c:c + nt], work[0][0:ns, t0:t0 + nt], a_wt[0:ns, blk, h:h + 1], con("pmask", ns)[:, 0:nt],
                            ALU.subtract, ALU.add).then_inc(decay_arg, 1)

                def decayed_scores(h):
                    dve.wait_ge(decay_ready, value("decay_ready", l, 2 * h + 2))
                    tt(decay_d[:, 0:416], decay_d[:, 0:416], work[1][:, 0:416], ALU.mult).then_inc(ml_p_ready, 1)
                    tt(decay_d[0:N_META, 416:432], decay_d[0:N_META, 416:432], work[1][0:N_META, 416:432], ALU.mult)\
                        .then_inc(ml_p_ready, 1)

                def add_outer(i):
                    h, half = divmod(i, 2)
                    dve.wait_ge(outer_done, value("outer_done", l, i + 1))
                    dve.wait_ge(c_scaled, value("c_scaled", l, h + 1))
                    c = c_head[h % 2][:, 4 * half:4 * half + 4, :].rearrange("p b v -> p (b v)")
                    tt(c, c, work[3][:, :], ALU.add).then_inc(c_new, 1)

                def centre():
                    dve.wait_ge(ln_summed, value("ln_summed", l, 1))
                    for c in range(KC):
                        stt(uc[:, c, :], work[0][:, 0:T], -1.0 / C_CONV, uc[:, c, :], ALU.mult, ALU.add).then_inc(centred, 1)

                def norm_conv():
                    inv = conv_std[:, 1, :]
                    dve.wait_ge(ln_std, value("ln_std", l, 1))
                    dve.reciprocal(inv, conv_std[:, 0, :]).then_inc(ln_inv, 1)
                    dve.wait_ge(ln_inv, value("ln_inv", l, 1))
                    for c in range(KC):
                        stt(uc[:, c, :], uc[:, c, :], vcol("ln_g", c), inv, ALU.mult, ALU.mult).then_inc(ln_inv, 1)

                def conv_los():
                    for c in range(KC):
                        dve.wait_ge(conv_hi_ready, value("conv_hi_ready", l, c + 1))
                        tt(conv_lo[:, c, :], uc[:, c, :], conv_hi[:, c, :].bitcast(F32), ALU.subtract).then_inc(conv_lo_ready, 1)

                def invert_dots():
                    dve.wait_ge(inv_m, value("inv_m", l, 2))
                    tt(km_t[:, 2, :], km_t[:, 0, :], km_t[:, 1, :], ALU.max).then_inc(dots_inv, 1)
                    dve.wait_ge(dots_inv, value("dots_inv", l, 1))
                    dve.reciprocal(km_t[:, 2, :], km_t[:, 2, :]).then_inc(dots_inv, 1)

                def divide_nums():
                    for h in range(NH_M):
                        dve.wait_ge(inv_spread, value("inv_spread", l, h + 1))
                        dve.wait_ge(num_gated, value("num_gated", l, h + 1))
                        tt(num_all[:, h, :], num_all[:, h, :], work[h][:, 0:T], ALU.mult).then_inc(hm_ready, 1)
                    for h in range(NH_M):
                        dve.wait_ge(ml_hi_ready, value("ml_hi_ready", l, h + 1))
                        tt(ml_lo[:, h, :], num_all[:, h, :], ml_hi[:, h, :].bitcast(F32), ALU.subtract).then_inc(ml_lo_ready, 1)

                def merged_los(n):
                    for kind, t in PIECES[n][4]:
                        dve.wait_ge(merged_hi_ready, value("merged_hi_ready", l, t + 1))
                        tt(h_lo[:, t, :], merged[:, t, :], h_hi[:, t, :].bitcast(F32), ALU.subtract).then_inc(merged_lo_ready, 1)

                def act_los(n):
                    for _, t in PIECES[n][4]:
                        dve.wait_ge(act_hi_ready, value("act_hi_ready", l, t + 1))
                        tt(act_lo[:, t, :], gate_buf[:, t % 4, :], act_hi[:, t, :].bitcast(F32), ALU.subtract).then_inc(act_lo_ready, 1)

                split_lo(0)
                split_lo(1)
                first_norm()
                split_lo(3)
                nc.vector.memset(u_pad[:, :, 0:HIST], 0.0).then_inc(pad_zero, 1)
                for n in range(N_PIECES):
                    kind = PIECES[n][0]
                    if n == STEP["gate", 0]:
                        second_norm_lo(KD - 1)
                        inverse_root(value("rms_ready", l, 2), ffn_rms, ffn_rms_inv)
                        dve.wait_ge(rms_inv_ready, value("rms_inv_ready", l, 2))
                    for tile in PIECES[n][4]:
                        if LAST_RUN[tile] < RUNS_THROUGH[n]:
                            take(tile)
                    if n == 17:
                        softmax_sample_1()
                    if n == 18:
                        softmax_sample_2()
                    if n + AHEAD < N_PIECES:
                        split_lo(n + AHEAD)
                    if n == 10:
                        conv_sample()
                    if n == 14:
                        rope()
                        self_products()
                    if n == 19:
                        row_stage()
                    if n == 20:
                        output_sample()
                    if n - 2 in SCORES_AT:
                        softmax_unit_2(SCORES_AT.index(n - 2))
                    if n == 22:
                        sample_att_lo()
                    if n - 1 in VALUES_AT[1::2]:
                        block_att_lo(VALUES_AT.index(n - 1) // 2)
                    if n in SCORES_AT:
                        softmax_unit_1(SCORES_AT.index(n))
                    if n == 39:
                        take_a_wt()
                        sample_dk()
                        km_weighted(0)
                        km_weighted(1)
                    if n == 41:
                        km_weighted(2)
                    if n in ML_AT:
                        decay_args(ML_AT.index(n))
                    if n in OUTER_AT:
                        add_outer(OUTER_AT.index(n))
                    if n - 1 in ML_AT:
                        decayed_scores(ML_AT.index(n - 1))
                    if n == 52:
                        centre()
                    if n == 56:
                        norm_conv()
                    if n == 57:
                        invert_dots()
                    if n == 58:
                        conv_los()
                    if n == 59:
                        divide_nums()
                    if kind == "ya":
                        merged_los(n)
                    if kind == "up":
                        act_los(n)
                    taps(sum(TAPS_AT[:n]), TAPS_AT[n])

            inverse_root(value("rms_ready", DEPTH, 1), rms, rms_inv)
            dve.wait_ge(rms_inv_ready, value("rms_inv_ready", DEPTH, 1))
            for c in range(KD):
                stt(h_full[:, c, :], x[:, c, :], vcol("final", c), rms_inv[:, :], ALU.mult, ALU.mult).then_inc(h_ready, 1)


INPUTS = ["x_prompt", "x_sample", "state_mlstm_c", "state_mlstm_n", "state_mlstm_m", "state_conv", "cache_swa_k",
          "cache_swa_v", "state_ffn_conv", "meta_tokens", "norm1_g", "w_in", "b_igate", "b_fgate", "w_mlstm_out",
          "w_dconv", "b_dconv", "ln_conv_g", "ln_conv_b", "w_conv_out", "attn_sinks", "w_attn_out", "b_merge",
          "w_out", "norm2_g", "w_ffn_gate", "w_ffn_up", "w_ffn_conv", "b_ffn_conv", "w_ffn_down", "final_norm_g"]
OUTPUTS = [(1, SEQ, D_MODEL), (NS, 1, D_MODEL)] + [
    shape for b, prompt in ((1, True), (NS, False)) for shape in (
        (DEPTH, b, NH_M, DH_M, DH_M), (DEPTH, b, NH_M, DH_M), (DEPTH, b, NH_M), (DEPTH, b, HIST, C_CONV),
        (DEPTH, b, WINDOW, KV_A, DH_A), (DEPTH, b, WINDOW, KV_A, DH_A), (DEPTH, b, FFN_CONV_W - 1, D_FF))]


def kernel(**inputs):
    import concourse.bacc as bacc
    from concourse.bass_utils import run_bass_kernel_spmd

    nc = bacc.Bacc("TRN2", target_bir_lowering=False, num_devices=1)
    arrays, ins, outs = {}, [], []
    for name in INPUTS:
        arrays[f"in_{name}"] = np.ascontiguousarray(inputs[name])
    arrays["in_constants"] = constants()
    for name, a in arrays.items():
        ins.append(nc.dram_tensor(name, a.shape, F32, kind="ExternalInput").ap())
    for i, shape in enumerate(OUTPUTS):
        outs.append(nc.dram_tensor(f"out_{i}", shape, F32, kind="ExternalOutput").ap())
    program(nc, ins, outs)
    r = run_bass_kernel_spmd(nc, [arrays], core_ids=[0])
    return tuple(r.results[0][f"out_{i}"] for i in range(len(OUTPUTS)))
```
